# Optimizing a Trainium2 kernel written in Bass

```python
import math
import jax
import jax.numpy as jnp
from jax import lax
import numpy as np
import jax, jax.numpy as jnp

D_MODEL = 1024
BATCH = 1
SEQ = 512
DEPTH = 2

HEAD_DIM = 64
N_EVEN = (DEPTH + 1) // 2
N_ODD = DEPTH // 2
NORM_EPS = 1e-6
D_FF = ((8 * D_MODEL // 3 + 255) // 256) * 256

POOL_WINDOWS = (2, 4, 8, 16)
POOL_GROUPS = len(POOL_WINDOWS)
POOL_WIDTH = D_MODEL // 4
POOL_GC = POOL_WIDTH // POOL_GROUPS

ATTN_Q_HEADS = (3 * D_MODEL // 4) // HEAD_DIM
ATTN_KV_HEADS = ATTN_Q_HEADS // 3
GQA_GROUP = ATTN_Q_HEADS // ATTN_KV_HEADS
WINDOW = 128
ATTN_BLOCK = 128
ROPE_THETA = 10000.0
EVEN_IN = POOL_WIDTH + (ATTN_Q_HEADS + 2 * ATTN_KV_HEADS) * HEAD_DIM
EVEN_MIX = POOL_WIDTH + ATTN_Q_HEADS * HEAD_DIM

CONV_CH = D_MODEL // 2
CONV_K = 31

SSM_INNER = D_MODEL
SSM_HEAD_DIM = 64
SSM_HEADS = SSM_INNER // SSM_HEAD_DIM
SSM_GROUPS = 4
SSM_STATE = 128
SSM_CONV = 4
SSM_CHUNK = 128
SSM_XBC = SSM_INNER + 2 * SSM_GROUPS * SSM_STATE
ODD_IN = 2 * CONV_CH + SSM_INNER + SSM_XBC + 2 * SSM_HEADS
ODD_MIX = CONV_CH + SSM_INNER


def rms_norm(x, w):
    xf = x.astype(jnp.float32)
    y = xf * lax.rsqrt(jnp.mean(xf * xf, axis=-1, keepdims=True) + NORM_EPS)
    return (y * w.astype(jnp.float32)).astype(x.dtype)

def layer_norm(x, g, b):
    xf = x.astype(jnp.float32)
    mu = jnp.mean(xf, axis=-1, keepdims=True)
    xc = xf - mu
    y = xc * lax.rsqrt(jnp.mean(xc * xc, axis=-1, keepdims=True) + NORM_EPS)
    return (y * g.astype(jnp.float32) + b.astype(jnp.float32)).astype(x.dtype)

def swiglu(h, w_gate, w_up, w_down):
    return (jax.nn.silu(h @ w_gate) * (h @ w_up)) @ w_down

def depthwise_conv(x, w, b, pad_left, pad_right):
    y = lax.conv_general_dilated(
        x, w[:, None, :].astype(x.dtype), window_strides=(1,),
        padding=[(pad_left, pad_right)],
        dimension_numbers=('NWC', 'WIO', 'NWC'),
        feature_group_count=x.shape[-1])
    return y + b.astype(x.dtype)

def rope_tables(seq_len):
    inv = 1.0 / (ROPE_THETA ** (jnp.arange(0, HEAD_DIM, 2, dtype=jnp.float32) / HEAD_DIM))
    ang = jnp.arange(seq_len, dtype=jnp.float32)[:, None] * inv[None, :]
    return jnp.cos(ang), jnp.sin(ang)

def apply_rope(t, cos, sin):
    tf = t.astype(jnp.float32)
    t1, t2 = tf[..., :HEAD_DIM // 2], tf[..., HEAD_DIM // 2:]
    c, s = cos[None, :, None, :], sin[None, :, None, :]
    return jnp.concatenate([t1 * c - t2 * s, t2 * c + t1 * s], axis=-1).astype(t.dtype)

def multiscale_pool(u, w_grp, scale):
    b, S, C = u.shape
    uf = u.astype(jnp.float32)
    cs = jnp.concatenate([jnp.zeros((b, 1, C), jnp.float32), jnp.cumsum(uf, axis=1)], axis=1)
    t = jnp.arange(S)
    outs = []
    for g, w in enumerate(POOL_WINDOWS):
        lo = jnp.clip(t - w // 2, 0, S)
        hi = jnp.clip(t + w - w // 2, 0, S)
        csg = cs[..., g * POOL_GC:(g + 1) * POOL_GC]
        cnt = (hi - lo).astype(jnp.float32)[None, :, None]
        mean = (jnp.take(csg, hi, axis=1) - jnp.take(csg, lo, axis=1)) / cnt
        outs.append(mean - uf[..., g * POOL_GC:(g + 1) * POOL_GC])
    p = jnp.stack(outs, axis=2).astype(u.dtype)
    y = jnp.einsum('bsgc,gcd->bsgd', p, w_grp).reshape(b, S, C)
    return y * scale

def windowed_gqa(q, k, v, sink):
    b, S = q.shape[0], q.shape[1]
    nb = S // ATTN_BLOCK
    qb = q.reshape(b, nb, ATTN_BLOCK, ATTN_KV_HEADS, GQA_GROUP, HEAD_DIM)

    def band(t):
        tp = jnp.pad(t, ((0, 0), (ATTN_BLOCK, ATTN_BLOCK), (0, 0), (0, 0)))
        tp = tp.reshape(b, nb + 2, ATTN_BLOCK, ATTN_KV_HEADS, HEAD_DIM)
        return jnp.concatenate([tp[:, :-2], tp[:, 1:-1], tp[:, 2:]], axis=2)

    kw, vw = band(k), band(v)
    s = jnp.einsum('bnqhgd,bnkhd->bnhgqk', qb, kw).astype(jnp.float32) * (HEAD_DIM ** -0.5)
    blk = jnp.arange(nb)[:, None, None] * ATTN_BLOCK
    qpos = blk + jnp.arange(ATTN_BLOCK)[None, :, None]
    kpos = blk - ATTN_BLOCK + jnp.arange(3 * ATTN_BLOCK)[None, None, :]
    valid = (jnp.abs(qpos - kpos) <= WINDOW) & (kpos >= 0) & (kpos < S)
    s = jnp.where(valid[None, :, None, None], s, -jnp.inf)
    sk = sink.astype(jnp.float32).reshape(ATTN_KV_HEADS, GQA_GROUP)[None, None, :, :, None, None]
    m = jnp.maximum(jnp.max(s, axis=-1, keepdims=True), sk)
    p = jnp.exp(s - m)
    denom = jnp.sum(p, axis=-1, keepdims=True) + jnp.exp(sk - m)
    o = jnp.einsum('bnhgqk,bnkhd->bnqhgd', (p / denom).astype(v.dtype), vw)
    return o.reshape(b, S, ATTN_Q_HEADS * HEAD_DIM)

def ssd_scan(x, dt, A, Bm, Cm):
    b, L, H, P = x.shape
    G, N = Bm.shape[2], Bm.shape[3]
    Hg = H // G
    c = L // SSM_CHUNK
    X = (x * dt[..., None]).reshape(b, c, SSM_CHUNK, G, Hg, P)
    a = jnp.moveaxis((dt * A).reshape(b, c, SSM_CHUNK, G, Hg), 2, -1)
    a_cs = jnp.cumsum(a, axis=-1)
    Bc = Bm.reshape(b, c, SSM_CHUNK, G, N)
    Cc = Cm.reshape(b, c, SSM_CHUNK, G, N)
    lower = jnp.tril(jnp.ones((SSM_CHUNK, SSM_CHUNK), bool))
    seg = a_cs[..., :, None] - a_cs[..., None, :]
    Lmat = jnp.exp(jnp.where(lower, seg, -jnp.inf))
    CB = jnp.einsum('bclgn,bcsgn->bcgls', Cc, Bc)
    y_diag = jnp.einsum('bcghls,bcsghp->bclghp', CB[:, :, :, None] * Lmat, X)
    decay_s = jnp.exp(a_cs[..., -1:] - a_cs)
    states = jnp.einsum('bclgn,bcghl,bclghp->bcghpn', Bc, decay_s, X)
    chunk_decay = jnp.exp(a_cs[..., -1])

    def step(h, inp):
        st, d = inp
        return h * d[..., None, None] + st, h

    h0 = jnp.zeros((b, G, Hg, P, N), jnp.float32)
    _, prev = lax.scan(step, h0, (jnp.moveaxis(states, 1, 0), jnp.moveaxis(chunk_decay, 1, 0)))
    prev = jnp.moveaxis(prev, 0, 1)
    y_off = jnp.einsum('bclgn,bcghpn,bcghl->bclghp', Cc, prev, jnp.exp(a_cs))
    return (y_diag + y_off).reshape(b, L, H, P)

def even_mixer(h, w_in, pool_w, pool_scale, sink, w_out, cos, sin):
    b, S, _ = h.shape
    proj = h @ w_in
    qw, kw = ATTN_Q_HEADS * HEAD_DIM, ATTN_KV_HEADS * HEAD_DIM
    o = POOL_WIDTH
    u = proj[..., :o]
    q = proj[..., o:o + qw].reshape(b, S, ATTN_Q_HEADS, HEAD_DIM)
    k = proj[..., o + qw:o + qw + kw].reshape(b, S, ATTN_KV_HEADS, HEAD_DIM)
    v = proj[..., o + qw + kw:o + qw + 2 * kw].reshape(b, S, ATTN_KV_HEADS, HEAD_DIM)
    q = apply_rope(q, cos, sin)
    k = apply_rope(k, cos, sin)
    pool_out = multiscale_pool(u, pool_w, pool_scale)
    attn_out = windowed_gqa(q, k, v, sink)
    return jnp.concatenate([pool_out, attn_out], axis=-1) @ w_out

def odd_mixer(h, w_in, dw_w, dw_b, ln_g, ln_b, conv_w, conv_b, A_log, dt_bias, D_skip, norm_w, w_out):
    b, S, _ = h.shape
    proj = h @ w_in
    glu_a = proj[..., :CONV_CH]
    glu_b = proj[..., CONV_CH:2 * CONV_CH]
    o = 2 * CONV_CH
    z = proj[..., o:o + SSM_INNER]
    o += SSM_INNER
    xbc = proj[..., o:o + SSM_XBC]
    o += SSM_XBC
    dt_raw = proj[..., o:o + 2 * SSM_HEADS].reshape(b, S, 2, SSM_HEADS)
    g = glu_a * jax.nn.sigmoid(glu_b)
    g = depthwise_conv(g, dw_w, dw_b, CONV_K // 2, CONV_K // 2)
    g = jax.nn.silu(layer_norm(g, ln_g, ln_b))
    xbc = jax.nn.silu(depthwise_conv(xbc, conv_w, conv_b, SSM_CONV // 2, SSM_CONV - 1 - SSM_CONV // 2))
    gn = SSM_GROUPS * SSM_STATE
    xs = xbc[..., :SSM_INNER].reshape(b, S, SSM_HEADS, SSM_HEAD_DIM).astype(jnp.float32)
    Bm = xbc[..., SSM_INNER:SSM_INNER + gn].reshape(b, S, SSM_GROUPS, SSM_STATE).astype(jnp.float32)
    Cm = xbc[..., SSM_INNER + gn:].reshape(b, S, SSM_GROUPS, SSM_STATE).astype(jnp.float32)
    dt = jax.nn.softplus(dt_raw.astype(jnp.float32) + dt_bias.astype(jnp.float32))
    A = -jnp.exp(A_log.astype(jnp.float32))
    flip = lambda t: jnp.flip(t, axis=1)
    y_f = ssd_scan(xs, dt[:, :, 0], A[0], Bm, Cm)
    y_b = flip(ssd_scan(flip(xs), flip(dt[:, :, 1]), A[1], flip(Bm), flip(Cm)))
    y = (y_f + y_b + xs * D_skip.astype(jnp.float32)[:, None]).reshape(b, S, SSM_INNER)
    y = rms_norm(y * jax.nn.silu(z.astype(jnp.float32)), norm_w).astype(h.dtype)
    return jnp.concatenate([g, y], axis=-1) @ w_out

def first_inputs(seed: int = 0) -> dict:
    key = jax.random.key(seed)
    ks = jax.random.split(key, 24)
    f32 = jnp.float32

    def nrm(k, shape, fan_in):
        return jax.random.normal(k, shape, f32) * (fan_in ** -0.5)

    def near_one(k, shape, s):
        return 1.0 + s * jax.random.normal(k, shape, f32)

    dt0 = jnp.exp(jax.random.uniform(ks[20], (N_ODD, 2, SSM_HEADS), f32,
                                     minval=math.log(1e-3), maxval=math.log(1e-1)))
    return {
        'x': jax.random.normal(ks[0], (BATCH, SEQ, D_MODEL), f32),
        'norm_w': near_one(ks[1], (DEPTH, 6, D_MODEL), 0.05),
        'ffn_w_gate': nrm(ks[2], (DEPTH, 2, D_MODEL, D_FF), D_MODEL),
        'ffn_w_up': nrm(ks[3], (DEPTH, 2, D_MODEL, D_FF), D_MODEL),
        'ffn_w_down': nrm(ks[4], (DEPTH, 2, D_FF, D_MODEL), D_FF),
        'ev_w_in': nrm(ks[5], (N_EVEN, D_MODEL, EVEN_IN), D_MODEL),
        'ev_pool_w': nrm(ks[6], (N_EVEN, POOL_GROUPS, POOL_GC, POOL_GC), POOL_GC),
        'ev_pool_scale': near_one(ks[7], (N_EVEN, POOL_WIDTH), 0.1),
        'ev_sink': 0.5 * jax.random.normal(ks[8], (N_EVEN, ATTN_Q_HEADS), f32),
        'ev_w_out': nrm(ks[9], (N_EVEN, EVEN_MIX, D_MODEL), EVEN_MIX),
        'od_w_in': nrm(ks[10], (N_ODD, D_MODEL, ODD_IN), D_MODEL),
        'cv_dw_w': nrm(ks[11], (N_ODD, CONV_K, CONV_CH), CONV_K),
        'cv_dw_b': 0.02 * jax.random.normal(ks[12], (N_ODD, CONV_CH), f32),
        'cv_ln_g': near_one(ks[13], (N_ODD, CONV_CH), 0.05),
        'cv_ln_b': 0.02 * jax.random.normal(ks[14], (N_ODD, CONV_CH), f32),
        'ssm_conv_w': nrm(ks[15], (N_ODD, SSM_CONV, SSM_XBC), SSM_CONV),
        'ssm_conv_b': 0.02 * jax.random.normal(ks[16], (N_ODD, SSM_XBC), f32),
        'ssm_A_log': jnp.log(jax.random.uniform(ks[17], (N_ODD, 2, SSM_HEADS), f32, minval=1.0, maxval=16.0)),
        'ssm_dt_bias': dt0 + jnp.log(-jnp.expm1(-dt0)),
        'ssm_D': near_one(ks[18], (N_ODD, SSM_HEADS), 0.1),
        'ssm_norm_w': near_one(ks[19], (N_ODD, SSM_INNER), 0.05),
        'od_w_out': nrm(ks[21], (N_ODD, ODD_MIX, D_MODEL), ODD_MIX),
    }

def first_block(x, norm_w, ffn_w_gate, ffn_w_up, ffn_w_down,
              ev_w_in, ev_pool_w, ev_pool_scale, ev_sink, ev_w_out,
              od_w_in, cv_dw_w, cv_dw_b, cv_ln_g, cv_ln_b,
              ssm_conv_w, ssm_conv_b, ssm_A_log, ssm_dt_bias, ssm_D, ssm_norm_w, od_w_out):
    cos, sin = rope_tables(x.shape[1])
    for l in range(DEPTH):
        nw = norm_w[l]
        x = x + 0.5 * rms_norm(swiglu(rms_norm(x, nw[0]), ffn_w_gate[l, 0], ffn_w_up[l, 0], ffn_w_down[l, 0]), nw[1])
        hn = rms_norm(x, nw[2])
        i = l // 2
        if l % 2 == 0:
            m = even_mixer(hn, ev_w_in[i], ev_pool_w[i], ev_pool_scale[i], ev_sink[i], ev_w_out[i], cos, sin)
        else:
            m = odd_mixer(hn, od_w_in[i], cv_dw_w[i], cv_dw_b[i], cv_ln_g[i], cv_ln_b[i],
                          ssm_conv_w[i], ssm_conv_b[i], ssm_A_log[i], ssm_dt_bias[i], ssm_D[i],
                          ssm_norm_w[i], od_w_out[i])
        x = x + rms_norm(m, nw[3])
        x = x + 0.5 * rms_norm(swiglu(rms_norm(x, nw[4]), ffn_w_gate[l, 1], ffn_w_up[l, 1], ffn_w_down[l, 1]), nw[5])
    return x


GRID_W = 64
Q_BLOCK = 128
EPS = 1e-6

GQA_HEADS = 8
GQA_KV_HEADS = 2
GQA_GROUP_2 = GQA_HEADS // GQA_KV_HEADS
GQA_HEAD_DIM = D_MODEL // 16
GQA_Q_W = GQA_HEADS * GQA_HEAD_DIM
GQA_KV_W = GQA_KV_HEADS * GQA_HEAD_DIM

MLA_HEADS = 8
MLA_NOPE_DIM = D_MODEL // 16
MLA_ROPE_DIM = D_MODEL // 32
MLA_V_DIM = D_MODEL // 16
MLA_QK_DIM = MLA_NOPE_DIM + MLA_ROPE_DIM
MLA_Q_RANK = (3 * D_MODEL) // 8
MLA_KV_RANK = D_MODEL // 4
MLA_OUT_W = MLA_HEADS * MLA_V_DIM

D_FF_2 = 4 * D_MODEL

SPLIT_SIZES = (GQA_Q_W, GQA_KV_W, GQA_KV_W, MLA_Q_RANK, MLA_KV_RANK, MLA_ROPE_DIM, 2 * D_MODEL)
IN_W = sum(SPLIT_SIZES)
SPLIT_POINTS = [int(v) for v in np.cumsum(SPLIT_SIZES)[:-1]]


def rmsnorm(x, g):
    xf = x.astype(jnp.float32)
    y = xf * lax.rsqrt(jnp.mean(xf * xf, axis=-1, keepdims=True) + EPS)
    return (y * g.astype(jnp.float32)).astype(x.dtype)

def axial_rope_tables(seq, rot_dim):
    rows = seq // GRID_W
    row = jnp.repeat(jnp.arange(rows, dtype=jnp.float32), GRID_W)
    col = jnp.tile(jnp.arange(GRID_W, dtype=jnp.float32), rows)
    half = rot_dim // 2
    inv = ROPE_THETA ** (-jnp.arange(0, half, 2, dtype=jnp.float32) / half)
    ar = row[:, None] * inv[None, :]
    ac = col[:, None] * inv[None, :]
    ang = jnp.concatenate([ar, ar, ac, ac], axis=-1)
    return jnp.cos(ang), jnp.sin(ang)

def apply_axial_rope(x, cos, sin):
    d = x.shape[-1]
    h = d // 2
    q = h // 2
    shape = (cos.shape[0],) + (1,) * (x.ndim - 3) + (d,)
    c = cos.reshape(shape).astype(x.dtype)
    s = sin.reshape(shape).astype(x.dtype)
    xr, xc = x[..., :h], x[..., h:]
    rot = lambda z: jnp.concatenate([-z[..., q:], z[..., :q]], axis=-1)
    x_rot = jnp.concatenate([rot(xr), rot(xc)], axis=-1)
    return x * c + x_rot * s

def blocked_attention(q, k, v, scale):
    b, s, hk, g, dk = q.shape
    dv = v.shape[-1]
    nb = s // Q_BLOCK
    qb = q.reshape(b, nb, Q_BLOCK, hk, g, dk).swapaxes(0, 1)

    def one_block(qblk):
        sc = jnp.einsum('bqhgd,bkhd->bhgqk', qblk, k).astype(jnp.float32) * scale
        p = jax.nn.softmax(sc, axis=-1).astype(v.dtype)
        return jnp.einsum('bhgqk,bkhd->bqhgd', p, v)

    out = lax.map(one_block, qb)
    return out.swapaxes(0, 1).reshape(b, s, hk * g * dv)

def token_mixer(u, w_in, b_gate, q_norm_g, k_norm_g, q_a_norm_g, kv_a_norm_g,
                w_q_up, w_kv_up, w_branch_a, w_branch_b, w_o,
                cos_a, sin_a, cos_b, sin_b):
    b, s, _ = u.shape
    z = u @ w_in
    qa, ka, va, cq, ckv, kr, gl = jnp.split(z, SPLIT_POINTS, axis=-1)

    qa = qa.reshape(b, s, GQA_HEADS, GQA_HEAD_DIM)
    ka = ka.reshape(b, s, GQA_KV_HEADS, GQA_HEAD_DIM)
    va = va.reshape(b, s, GQA_KV_HEADS, GQA_HEAD_DIM)
    qa = apply_axial_rope(rmsnorm(qa, q_norm_g), cos_a, sin_a)
    ka = apply_axial_rope(rmsnorm(ka, k_norm_g), cos_a, sin_a)
    qa = qa.reshape(b, s, GQA_KV_HEADS, GQA_GROUP_2, GQA_HEAD_DIM)
    ya = blocked_attention(qa, ka, va, 1.0 / math.sqrt(GQA_HEAD_DIM))

    qb = (rmsnorm(cq, q_a_norm_g) @ w_q_up).reshape(b, s, MLA_HEADS, MLA_QK_DIM)
    q_nope, q_rope = qb[..., :MLA_NOPE_DIM], qb[..., MLA_NOPE_DIM:]
    q_rope = apply_axial_rope(q_rope, cos_b, sin_b)
    kvb = (rmsnorm(ckv, kv_a_norm_g) @ w_kv_up).reshape(b, s, MLA_HEADS, MLA_NOPE_DIM + MLA_V_DIM)
    k_nope, vb = kvb[..., :MLA_NOPE_DIM], kvb[..., MLA_NOPE_DIM:]
    k_rope = apply_axial_rope(kr, cos_b, sin_b)
    k_rope = jnp.broadcast_to(k_rope[:, :, None, :], (b, s, MLA_HEADS, MLA_ROPE_DIM))
    qb = jnp.concatenate([q_nope, q_rope], axis=-1)[:, :, :, None, :]
    kb = jnp.concatenate([k_nope, k_rope], axis=-1)
    yb = blocked_attention(qb, kb, vb, 1.0 / math.sqrt(MLA_QK_DIM))

    gates = jax.nn.sigmoid((gl + b_gate).astype(jnp.float32)).astype(u.dtype)
    g_a, g_b = gates[..., :D_MODEL], gates[..., D_MODEL:]
    merged = g_a * (ya @ w_branch_a) + g_b * (yb @ w_branch_b)
    return merged @ w_o

def second_inputs(seed: int = 0) -> dict:
    key = jax.random.key(seed)
    ks = jax.random.split(key, 20)
    f32 = jnp.float32

    def w(k, fan_in, fan_out):
        return jax.random.normal(k, (DEPTH, fan_in, fan_out), f32) * fan_in ** -0.5

    def gain(k, n):
        return 1.0 + 0.05 * jax.random.normal(k, (DEPTH, n), f32)

    return {
        "x": jax.random.normal(ks[0], (BATCH, SEQ, D_MODEL), f32),
        "w_in": w(ks[1], D_MODEL, IN_W),
        "b_gate": 0.1 * jax.random.normal(ks[2], (DEPTH, 2 * D_MODEL), f32),
        "q_norm_g": gain(ks[3], GQA_HEAD_DIM),
        "k_norm_g": gain(ks[4], GQA_HEAD_DIM),
        "q_a_norm_g": gain(ks[5], MLA_Q_RANK),
        "kv_a_norm_g": gain(ks[6], MLA_KV_RANK),
        "w_q_up": w(ks[7], MLA_Q_RANK, MLA_HEADS * MLA_QK_DIM),
        "w_kv_up": w(ks[8], MLA_KV_RANK, MLA_HEADS * (MLA_NOPE_DIM + MLA_V_DIM)),
        "w_branch_a": w(ks[9], GQA_Q_W, D_MODEL),
        "w_branch_b": w(ks[10], MLA_OUT_W, D_MODEL),
        "w_o": w(ks[11], D_MODEL, D_MODEL),
        "w_ffn_up": w(ks[12], D_MODEL, D_FF_2),
        "w_ffn_down": w(ks[13], D_FF_2, D_MODEL),
        "pre_mix_g": gain(ks[14], D_MODEL),
        "post_mix_g": gain(ks[15], D_MODEL),
        "pre_ffn_g": gain(ks[16], D_MODEL),
        "post_ffn_g": gain(ks[17], D_MODEL),
    }

def second_block(x, w_in, b_gate, q_norm_g, k_norm_g, q_a_norm_g, kv_a_norm_g,
              w_q_up, w_kv_up, w_branch_a, w_branch_b, w_o, w_ffn_up, w_ffn_down,
              pre_mix_g, post_mix_g, pre_ffn_g, post_ffn_g):
    seq = x.shape[1]
    cos_a, sin_a = axial_rope_tables(seq, GQA_HEAD_DIM)
    cos_b, sin_b = axial_rope_tables(seq, MLA_ROPE_DIM)
    for l in range(DEPTH):
        u = rmsnorm(x, pre_mix_g[l])
        m = token_mixer(u, w_in[l], b_gate[l], q_norm_g[l], k_norm_g[l],
                        q_a_norm_g[l], kv_a_norm_g[l], w_q_up[l], w_kv_up[l],
                        w_branch_a[l], w_branch_b[l], w_o[l],
                        cos_a, sin_a, cos_b, sin_b)
        x = x + rmsnorm(m, post_mix_g[l])
        h = rmsnorm(x, pre_ffn_g[l]) @ w_ffn_up[l]
        f = jnp.square(jax.nn.relu(h)) @ w_ffn_down[l]
        x = x + rmsnorm(f, post_ffn_g[l])
    return x


def setup_inputs(seed=0):
    out = dict(first_inputs(seed))
    for name, value in second_inputs(seed + 1).items():
        if name != "x":
            out[name + "_2"] = value
    return out


def reference(
    x, norm_w, ffn_w_gate, ffn_w_up, ffn_w_down, ev_w_in, ev_pool_w, ev_pool_scale, ev_sink,
    ev_w_out, od_w_in, cv_dw_w, cv_dw_b, cv_ln_g, cv_ln_b, ssm_conv_w, ssm_conv_b, ssm_A_log,
    ssm_dt_bias, ssm_D, ssm_norm_w, od_w_out, w_in_2, b_gate_2, q_norm_g_2, k_norm_g_2,
    q_a_norm_g_2, kv_a_norm_g_2, w_q_up_2, w_kv_up_2, w_branch_a_2, w_branch_b_2, w_o_2,
    w_ffn_up_2, w_ffn_down_2, pre_mix_g_2, post_mix_g_2, pre_ffn_g_2, post_ffn_g_2,
):
    x = first_block(
        x, norm_w, ffn_w_gate, ffn_w_up, ffn_w_down, ev_w_in, ev_pool_w, ev_pool_scale, ev_sink,
        ev_w_out, od_w_in, cv_dw_w, cv_dw_b, cv_ln_g, cv_ln_b, ssm_conv_w, ssm_conv_b,
        ssm_A_log, ssm_dt_bias, ssm_D, ssm_norm_w, od_w_out,
    )
    return second_block(
        x, w_in_2, b_gate_2, q_norm_g_2, k_norm_g_2, q_a_norm_g_2, kv_a_norm_g_2, w_q_up_2,
        w_kv_up_2, w_branch_a_2, w_branch_b_2, w_o_2, w_ffn_up_2, w_ffn_down_2, pre_mix_g_2,
        post_mix_g_2, pre_ffn_g_2, post_ffn_g_2,
    )


_drawn_inputs = setup_inputs


def setup_inputs(seed=0):
    import zlib

    import numpy as np

    out = dict(_drawn_inputs(seed))
    spreads = {}
    factors = {'ev_sink': 8.0,
     'cv_ln_b': 4.383,
     'ssm_conv_b': 2.782,
     'q_norm_g_2': 7.412,
     'k_norm_g_2': 7.501,
     'q_a_norm_g_2': 5.779}
    for name, (base, spread) in spreads.items():
        noise = np.random.default_rng([zlib.crc32(name.encode()), seed]).standard_normal(out[name].shape)
        drawn = base * np.exp(spread * noise) if base else spread * noise
        out[name] = jnp.asarray(drawn.astype(out[name].dtype))
    for name, factor in factors.items():
        out[name] = (out[name] * factor).astype(out[name].dtype)
    return out
```

```python
from contextlib import ExitStack

import concourse.bass as bass
import numpy as np
from concourse import mybir

P = 128
S = 512
D = 1024
KD = D // P
F = 2816
NF = F // P
EPS = 1e-6
RING = 4
AHEAD = 2
DOWN = (8, 8, 6)
ACCS = 4
STAT, SPREAD = 4, 5
SCORES, TURNED, HEADS = 4, 6, 7
F2 = 4096
NH = F2 // 2 // P
HD = 64
NEG = -1e30

POOL_W, Q_HEADS, KV_HEADS = 256, 12, 4
EVEN_PAIRS = [(0, 3), (1, 4), (2, 5), (6, 9), (7, 10), (8, 11)]
EVEN_ORDER = [("lin", 0), ("lin", 1), ("lin", 2), ("grp", 0), ("grp", 1), ("lin", 3), ("rot", 2)]
for _i in range(4, 10):
    EVEN_ORDER += [("lin", _i), ("rot", _i - 1)]
EVEN_ORDER += [("val", 0), ("rot", 9), ("val", 1)]

CONV_K, CONV_T = 31, 4
SSM_K = 4
SH, SG, SN = 16, 4, 128
ODD_LINS = 2 * CONV_T + 16 + 1 + 8
LOG_TERMS = 7

QR, KR = 3, 2
RAWS = 5
QK = 96

ALU = mybir.AluOpType
ACT = mybir.ActivationFunctionType
F32 = mybir.dt.float32
F32R = mybir.dt.float32r


class Counts:

    def __init__(self):
        self.blocks = 0
        self.tiles = 0
        self.hidden = 0
        self.sums = 0
        self.squares = 0
        self.norms = 0
        self.xr = 0
        self.xn = 0
        self.units = 0
        self.heads = 0
        self.marks = {}

    def at(self, name):
        return self.marks.get(name, 0)

    def copy(self):
        k = Counts()
        k.blocks, k.tiles, k.hidden, k.sums, k.squares = self.blocks, self.tiles, self.hidden, self.sums, self.squares
        k.norms, k.xr, k.xn, k.units, k.heads = self.norms, self.xr, self.xn, self.units, self.heads
        k.marks = dict(self.marks)
        return k

    def add(self, name, n):
        self.marks[name] = self.at(name) + n


class Chain:

    def __init__(self, eng, sem):
        self.eng, self.sem, self.n = eng, sem, 0

    def step(self, ins):
        self.n += 1
        ins.then_inc(self.sem, 1)
        return self.n

    def link(self, ins):
        self.eng.wait_ge(self.sem, self.step(ins))


def build(nc, t, stop=99):
    with ExitStack() as ctx:
        def sb(name, shape, dt=F32):
            return ctx.enter_context(nc.sbuf_tensor(name, shape, dt))

        def sem(name):
            return ctx.enter_context(nc.semaphore(name))

        def over(under, *tensors):
            with ExitStack() as same:
                return [same.enter_context(nc.sbuf_tensor(name, shape, dt)) for name, shape, dt in tensors]

        x = sb("x", [P, KD, S])
        y, = over("xh", ("y", [P, KD, S], F32))
        o_xf, o_xb = over("xh, xl", ("o_xf", [P, 4, D], F32), ("o_xb", [P, 4, D], F32))
        xh = sb("xh", [P, KD, S], F32R)
        xl = sb("xl", [P, KD, S], F32R)
        w_raw = sb("w_raw", [P, RING, 1024])
        w_hi = sb("w_hi", [P, RING, 1024], F32R)
        w_lo = sb("w_lo", [P, RING, 1024], F32R)
        ident = sb("ident", [P, P])
        meancol = sb("meancol", [P, 6])
        gains = sb("gains", [P, 20, KD])
        stat = sb("stat", [P, 2, 48])
        red = sb("red", [P, 3, 8])
        sq = sb("sq", [P, 2, S])
        sqsum = sb("sqsum", [P, S])
        tmp = sb("tmp", [P, 2, S])
        work = sb("work", [P, 6, S])
        sig, h = work[:, 0:2, :], work[:, 2:4, :]
        pbuf, ptb, raw = work[:, 0:3, :], work[:, 3:5, :], work[:, 4:6, :]
        o_e = work[:].rearrange("p a b -> p (a b)")[:, 0:1920].rearrange("p (a b) -> p a b", a=3)

        BF16 = mybir.dt.bfloat16
        e_tab, e_wg, e_small, e_nsink, e_pw, e_u, e_a, e_qk, e_v, m_hi, m_lo = over(
            "hh", ("e_tab", [P, 2560], F32), ("e_wg", [P, 2, P], F32), ("e_small", [P, 14], F32),
            ("e_nsink", [P, 12], F32), ("e_pw", [P, 2, S], F32), ("e_u", [P, 2, S + 16], F32),
            ("e_a", [P, 2, S + 16], F32), ("e_qk", [P, 8, S], F32), ("e_v", [P, 2, S], F32),
            ("m_hi", [P, KD, S], F32R), ("m_lo", [P, KD, S], F32R))
        odd_fixed = [("o_tab", [P, 2 + 2 * P], F32), ("o_small", [P, 234], F32), ("o_a", [32, 2], F32),
                     ("o_r", [32, S], F32), ("o_dt", [P, 4, 32], F32), ("o_nr", [P, 4, 32], F32),
                     ("o_mask", [P, 2, P], BF16), ("identb", [P, P], BF16), ("o_x", [P, KD, S], F32),
                     ("o_b", [P, SG, S], F32), ("o_c", [P, SG, S], F32), ("g_hi", [P, CONV_T, S], F32R),
                     ("g_lo", [P, CONV_T, S], F32R)]
        o_tab, o_small, o_a, o_r, o_dt, o_nr, o_mask, identb, o_x, o_b, o_c, g_hi, g_lo, o_z, o_g, o_cv = over(
            "hh", *odd_fixed, ("o_z", [P, KD, S], F32), ("o_g", [P, CONV_T, S], F32), ("o_cv", [P, CONV_T, S], F32))
        o_y, o_cb = over("hh", *[(n + "_", s, d) for n, s, d in odd_fixed], ("o_y", [P, KD, S], F32),
                         ("o_cb", [P, 2, 4, S], F32))[-2:]
        tab2 = [("b_tab", [P, 4 * S + 2 * P], F32), ("b_small", [P, 24], F32)]
        head2 = [("c_hi", [P, QR + KR, S], F32R), ("c_lo", [P, QR + KR, S], F32R)]
        mid2 = [("b_qk", [P, RAWS, S], F32), ("b_va", [P, S], F32), ("krot", [P, S], F32), ("gap2", [P, S], F32)]
        b_tab, b_small, c_hi, c_lo, b_qk, b_va, krot, _, b_q, b_k, b_vb = over(
            "hh", *tab2, *head2, *mid2, ("b_q", [P, 8, S], F32), ("b_k", [P, 8, S], F32), ("b_vb", [P, 4, S], F32))
        (ya_hi, ya_lo, _, yb_hi, yb_lo, mm_hi, mm_lo) = over(
            "hh", *[(n + "_", s, d) for n, s, d in tab2], ("ya_hi", [P, 4, S], F32R), ("ya_lo", [P, 4, S], F32R),
            ("gap3", [P, 2, S], F32), ("yb_hi", [P, 4, S], F32R), ("yb_lo", [P, 4, S], F32R),
            ("mm_hi", [P, KD, S], F32R), ("mm_lo", [P, KD, S], F32R))[2:]
        c_raw = over("hh", *[(n + "__", s, d) for n, s, d in tab2 + head2 + mid2], ("c_raw", [P, QR + KR, S], F32))[-1]
        hh2, hl2, y_b = over("hh", ("hh2", [P, NH, S], F32R), ("hl2", [P, NH, S], F32R), ("y_b", [P, KD, S], F32))
        hh = sb("hh", [P, NF, S], F32R)
        hl = sb("hl", [P, NF, S], F32R)
        bank = [ctx.enter_context(nc.psum_tensor(f"bank{i}", [P, S], F32)) for i in range(8)]

        gains_loaded, x_loaded = sem("gains_loaded"), sem("x_loaded")
        pool_made, dve_made = sem("pool_made"), sem("dve_made")
        w_loaded = [sem(f"w_loaded{i}") for i in range(RING)]
        w_rounded, w_rest = sem("w_rounded"), sem("w_rest")
        blocks_done, acc_drained = sem("blocks_done"), sem("acc_drained")
        silu_done, hh_done, hl_done = sem("silu_done"), sem("hh_done"), sem("hl_done")
        y_squared, sum_used = sem("y_squared"), sem("sum_used")
        dve_step, act_step = sem("dve_step"), sem("act_step")
        x_ready, x_squared = sem("x_ready"), sem("x_squared")
        squares_summed, std_ready = sem("squares_summed"), sem("std_ready")
        rstd_ready, spread_ready = sem("rstd_ready"), sem("spread_ready")
        xn_ready, xh_ready, xl_ready = sem("xn_ready"), sem("xh_ready"), sem("xl_ready")
        stored = sem("stored")
        side_done, raw_copied, rotated = sem("side_done"), sem("raw_copied"), sem("rotated")
        tables_loaded, odd_loaded = sem("tables_loaded"), sem("odd_loaded")
        pooled, pool_rounded, pool_split = sem("pooled"), sem("pool_rounded"), sem("pool_split")
        scores_ready, rowmax_ready, probs_ready = sem("scores_ready"), sem("rowmax_ready"), sem("probs_ready")
        probs_scaled, probs_turned, turned_copied = sem("probs_scaled"), sem("probs_turned"), sem("turned_copied")
        attended, head_rounded, head_split = sem("attended"), sem("head_rounded"), sem("head_split")
        a_ready, glu_done, xbc_done, z_done = sem("a_ready"), sem("glu_done"), sem("xbc_done"), sem("z_done")
        dt_arg, dt_exp, steps_ready = sem("dt_arg"), sem("dt_exp"), sem("steps_ready")
        centered, normed, g_silu, g_rounded, g_split = (sem(n) for n in ("centered", "normed", "g_silu", "g_rounded", "g_split"))
        scaled_in, cb_summed, cb_copied = sem("scaled_in"), sem("cb_summed"), sem("cb_copied")
        decays_spread, exps_ready, weighted = sem("decays_spread"), sem("exps_ready"), sem("weighted")
        scanned, pair_read, gated = sem("scanned"), sem("pair_read"), sem("gated")
        up_done, kr_copied, rstd2_ready, cn_ready = sem("up_done"), sem("kr_copied"), sem("rstd2_ready"), sem("cn_ready")
        gate_ready, merged, merged_rounded, merged_split = (sem(n) for n in ("gate_ready", "merged", "merged_rounded", "merged_split"))
        block = ctx.enter_context(nc.Block())

        def raw_free(g):
            return g + 1

        def rest_done(g):
            return RING + g + 1

        def slot_free(g):
            return g + 1

        def block_done(g):
            return RING + g + 1

        def acc_free(n):
            return n + 1

        def drained(n):
            return ACCS + n + 1

        widths = []

        def load(sp, g, slot, src):
            sp.wait_ge(w_rest, raw_free(g))
            sp.dma_start(w_raw[:, slot, 0:src.shape[1]], src).then_inc(w_loaded[slot], 16)

        def round_block(act, g, slot, turn, width):
            act.wait_ge(w_loaded[slot], (turn + 1) * 16)
            act.wait_ge(blocks_done, slot_free(g))
            act.activation(w_hi[:, slot, 0:width], w_raw[:, slot, 0:width], ACT.Copy).then_inc(w_rounded, 1)

        def round_ahead(act, g):
            g += AHEAD
            if g < len(widths):
                round_block(act, g, g % RING, g // RING, widths[g])

        def rest_block(pool, g, slot, width):
            pool.wait_ge(w_rounded, g + 1)
            pool.tensor_tensor(w_lo[:, slot, 0:width], w_raw[:, slot, 0:width],
                               w_hi[:, slot, 0:width].bitcast(F32), ALU.subtract).then_inc(w_rest, 1)

        def products(pe, out, slot, hi, lo, first, last):
            for k in range(len(hi)):
                wh, wl = w_hi[:, slot, k * P:(k + 1) * P], w_lo[:, slot, k * P:(k + 1) * P]
                pe.matmul(out, wh, hi[k], start=first and k == 0, stop=False)
                pe.matmul(out, wh, lo[k], start=False, stop=False)
                mm = pe.matmul(out, wl, hi[k], start=False, stop=last and k == len(hi) - 1)
            mm.then_inc(blocks_done, 1)

        def sum_squares(pe, src, first, mean=0):
            for n in range(4):
                mm = pe.matmul(bank[STAT][:, n:n + 1], src[:, n * P:(n + 1) * P], meancol[:, mean:mean + 1],
                               start=first and n == 0, stop=True, skip_group_check=True)
            mm.then_inc(squares_summed, 1)

        def spread(pe, c):
            pe.wait_ge(rstd_ready, c.norms + 1)
            for n in range(4):
                mm = pe.matmul(bank[SPREAD][:, n * P:(n + 1) * P], stat[:, 1, n:n + 1].to_broadcast([P, P]),
                               ident[:], start=True, stop=True)
            mm.then_inc(spread_ready, 1)

        def std(act, c, n):
            act.wait_ge(squares_summed, c.squares + n)
            act.activation(stat[:, 0, 0:4], bank[STAT][:, 0:4], ACT.Sqrt, bias=EPS).then_inc(std_ready, 1)

        def rstd(dve, c):
            dve.wait_ge(std_ready, c.at("std") + 1)
            dve.reciprocal(stat[:, 1, 0:4], stat[:, 0, 0:4]).then_inc(rstd_ready, 1)
            dve.wait_ge(spread_ready, c.norms + 1)

        def post_pe(pe, c):
            pe.wait_ge(sum_used, 2 + c.sums)
            sum_squares(pe, sqsum, True)
            spread(pe, c)

        def post_act(act, c):
            std(act, c, 1)

        def post_dve(dve, ch, c, gain, y):
            rstd(dve, c)
            at = {}

            def scaled(k):
                if k >= 2:
                    dve.wait_ge(x_ready, c.xr + k - 1)
                at[k] = ch.step(dve.scalar_tensor_tensor(
                    out=tmp[:, k % 2, :], in0=y[:, k, :], scalar=gains[:, gain, k:k + 1],
                    in1=bank[SPREAD][:], op0=ALU.mult, op1=ALU.mult))
            scaled(0)
            for k in range(KD):
                if k + 1 < KD:
                    scaled(k + 1)
                dve.wait_ge(dve_step, at[k])
                dve.tensor_tensor(x[:, k, :], x[:, k, :], tmp[:, k % 2, :], ALU.add).then_inc(x_ready, 1)
            dve.wait_ge(x_ready, c.xr + KD)

        def post_end(c):
            c.norms += 1
            c.add("std", 1)
            c.squares += 1
            c.xr += KD

        def norm_pe(pe, c):
            for k in range(KD):
                pe.wait_ge(x_squared, c.at("sq") + k + 1)
                sum_squares(pe, sq[:, k % 2, :], k == 0)
            spread(pe, c)

        def norm_act(act, c, src, ready):
            for k in range(KD):
                ready(k)
                if k >= 2:
                    act.wait_ge(squares_summed, c.squares + k - 1)
                act.activation(sq[:, k % 2, :], src[:, k, :], ACT.Square).then_inc(x_squared, 1)
            std(act, c, KD)
            for k in range(KD):
                act.wait_ge(xn_ready, c.at("xnr") + k + 1)
                act.activation(xh[:, k, :], tmp[:, k % 2, :], ACT.Copy).then_inc(xh_ready, 1)

        def norm_dve(dve, c, src, gain):
            rstd(dve, c)

            def scaled(k):
                if k >= 2:
                    dve.wait_ge(xl_ready, c.xn + k - 1)
                dve.scalar_tensor_tensor(
                    out=tmp[:, k % 2, :], in0=src[:, k, :], scalar=gain(k),
                    in1=bank[SPREAD][:], op0=ALU.mult, op1=ALU.mult).then_inc(xn_ready, 1)
            scaled(0)
            for k in range(KD):
                if k + 1 < KD:
                    scaled(k + 1)
                dve.wait_ge(xh_ready, c.xn + k + 1)
                dve.tensor_tensor(xl[:, k, :], tmp[:, k % 2, :], xh[:, k, :].bitcast(F32), ALU.subtract)\
                   .then_inc(xl_ready, 1)
            dve.wait_ge(xl_ready, c.xn + KD)

        def norm_end(c):
            c.norms += 1
            c.add("std", 1)
            c.add("sq", KD)
            c.add("xnr", KD)
            c.squares += KD
            c.xn += KD

        def pre_pe(pe, c):
            norm_pe(pe, c)

        def pre_act(act, c):
            if c.xr == 0:
                act.wait_ge(x_loaded, 16)
            else:
                act.wait_ge(sum_used, 2 + c.sums)
            norm_act(act, c, x, lambda k: act.wait_ge(x_ready, c.xr - KD + k + 1) if c.xr else None)

        def pre_dve(dve, ch, c, gain):
            norm_dve(dve, c, x, lambda k: gains[:, gain, k:k + 1])

        def pre_end(c):
            norm_end(c)

        def y_act(act, c, m, y):
            act.wait_ge(acc_drained, drained(c.tiles + m))
            act.wait_ge(sum_used, c.sums + m + 1)
            act.activation(sq[:, m % 2, :], y[:, m, :], ACT.Square).then_inc(y_squared, 1)

        def y_dve(dve, c, m, blk):
            dve.wait_ge(blocks_done, block_done(blk))
            dve.tensor_copy(y[:, m, :], bank[(c.tiles + m) % ACCS][:]).then_inc(acc_drained, 1)

        def y_sum(dve, c, m):
            dve.wait_ge(y_squared, c.sums + m + 1)
            dve.wait_ge(sum_used, 2 + c.sums + m)
            dve.tensor_tensor(sqsum[:], sqsum[:], sq[:, m % 2, :], ALU.add).then_inc(sum_used, 1)

        def ffn_sp(sp, c, i):
            B = c.blocks
            with sp.Fori(0, NF // 2) as it:
                for j in range(4):
                    load(sp, it * 4 + (B + j), (B + j) % RING, t["ffn_up"][i, it * 4 + j])
            B += 2 * NF
            with sp.Fori(0, 2) as it:
                for m in range(4):
                    for b, nk in enumerate(DOWN):
                        j = 3 * m + b
                        load(sp, it * 12 + (B + j), (B + j) % RING,
                             t["ffn_down"][i, it * 4 + m][:, b * 1024:b * 1024 + nk * P])

        def ffn_pool(pool, c, i):
            B = c.blocks
            with pool.Fori(0, NF // 2) as it:
                for j in range(4):
                    rest_block(pool, it * 4 + (B + j), (B + j) % RING, 1024)
            B += 2 * NF
            with pool.Fori(0, 2) as it:
                for j in range(12):
                    rest_block(pool, it * 12 + (B + j), (B + j) % RING, DOWN[j % 3] * P)

        def ffn_pe(pe, c, i):
            B, T = c.blocks, c.tiles
            pe.wait_ge(xl_ready, c.xn)
            with pe.Fori(0, NF // 2) as it:
                for j in range(4):
                    pe.wait_ge(acc_drained, it * 4 + acc_free(T + j))
                    pe.wait_ge(w_rest, it * 4 + rest_done(B + j))
                    products(pe, bank[(T + j) % ACCS][:], (B + j) % RING,
                             [xh[:, k, :] for k in range(KD)], [xl[:, k, :] for k in range(KD)], True, True)
            B += 2 * NF
            T += 2 * NF
            pe.wait_ge(hl_done, 2 + c.hidden + NF)
            with pe.Fori(0, 2) as it:
                for m in range(4):
                    pe.wait_ge(acc_drained, it * 4 + acc_free(T + m))
                    for b, nk in enumerate(DOWN):
                        j = 3 * m + b
                        pe.wait_ge(w_rest, it * 12 + rest_done(B + j))
                        products(pe, bank[(T + m) % ACCS][:], (B + j) % RING,
                                 [hh[:, 8 * b + k, :] for k in range(nk)], [hl[:, 8 * b + k, :] for k in range(nk)],
                                 b == 0, b == 2)

        def ffn_act(act, c, i):
            B, T, H = c.blocks, c.tiles, c.hidden
            with act.Fori(0, NF // 2) as it:
                for n in range(2):
                    for j in (2 * n, 2 * n + 1):
                        g = B + j + AHEAD
                        round_block(act, it * 4 + g, g % RING, it + g // RING, 1024)
                    act.wait_ge(blocks_done, it * 4 + block_done(B + 2 * n))
                    act.wait_ge(acc_drained, it * 4 + drained(T + 2 * n - 3))
                    act.activation(sig[:, n, :], bank[(T + 2 * n) % ACCS][:], ACT.Silu).then_inc(silu_done, 1)
                    act.wait_ge(acc_drained, it * 4 + drained(T + 2 * n + 1))
                    act.activation(hh[:, it * 2 + n, :], h[:, n, :], ACT.Copy).then_inc(hh_done, 1)
            c.tiles += 2 * NF
            for m in range(KD):
                for b in range(3):
                    round_ahead(act, B + 2 * NF + 3 * m + b)
                y_act(act, c, m, y)
            c.tiles -= 2 * NF

        def ffn_dve(dve, ch, c, i):
            B, T, H = c.blocks, c.tiles, c.hidden
            ch.link(dve.memset(sqsum[:], 0.0))
            with dve.Fori(0, NF // 2) as it:
                for n in range(2):
                    dve.wait_ge(silu_done, it * 2 + (H + n + 1))
                    dve.wait_ge(blocks_done, it * 4 + block_done(B + 2 * n + 1))
                    dve.wait_ge(hl_done, it * 2 + (H + n + 1))
                    dve.tensor_tensor(h[:, n, :], sig[:, n, :], bank[(T + 2 * n + 1) % ACCS][:], ALU.mult)\
                       .then_inc(acc_drained, 2)
                    dve.wait_ge(hh_done, it * 2 + (H + n + 1))
                    dve.tensor_tensor(hl[:, it * 2 + n, :], h[:, n, :], hh[:, it * 2 + n, :].bitcast(F32),
                                      ALU.subtract).then_inc(hl_done, 1)
            c.tiles += 2 * NF
            for m in range(KD):
                y_dve(dve, c, m, B + 2 * NF + 3 * m + 2)
                y_sum(dve, c, m)
            c.tiles -= 2 * NF

        def ffn_end(c):
            c.blocks += 2 * NF + 3 * KD
            c.tiles += 2 * NF + KD
            c.hidden += NF
            c.sums += KD

        def stream_sp(sp, g, arr, n):
            if n >= RING:
                with sp.Fori(0, n // RING) as it:
                    for j in range(RING):
                        load(sp, it * RING + (g + j), (g + j) % RING, arr[it * RING + j])
            for j in range(n // RING * RING, n):
                load(sp, g + j, (g + j) % RING, arr[j])

        def stream_pool(pool, g, n):
            if n >= RING:
                with pool.Fori(0, n // RING) as it:
                    for j in range(RING):
                        rest_block(pool, it * RING + (g + j), (g + j) % RING, 1024)
            for j in range(n // RING * RING, n):
                rest_block(pool, g + j, (g + j) % RING, 1024)

        def xs_of(hi, lo, n, first=0):
            return [hi[:, first + k, :] for k in range(n)], [lo[:, first + k, :] for k in range(n)]

        def take_block(pe, c):
            g = c.blocks
            pe.wait_ge(w_rest, rest_done(g))
            c.blocks += 1
            return g % RING

        def project(pe, c, tile, parts):
            pe.wait_ge(acc_drained, acc_free(tile))
            for b, (hi, lo) in enumerate(parts):
                products(pe, bank[tile % ACCS][:], take_block(pe, c), hi, lo, b == 0, b == len(parts) - 1)

        def project_values(pe, c, tile):
            pe.wait_ge(acc_drained, acc_free(tile))
            slot = take_block(pe, c)
            for n in range(4):
                out, tok = bank[tile % ACCS][:, n * P:(n + 1) * P], slice(n * P, (n + 1) * P)
                for k in range(KD):
                    wh, wl = w_hi[:, slot, k * P:(k + 1) * P], w_lo[:, slot, k * P:(k + 1) * P]
                    pe.matmul(out, xh[:, k, tok], wh, start=k == 0, stop=False)
                    pe.matmul(out, xh[:, k, tok], wl, start=False, stop=False)
                    mm = pe.matmul(out, xl[:, k, tok], wh, start=False, stop=k == KD - 1)
            mm.then_inc(blocks_done, 1)

        def y_begin(dve, ch):
            ch.link(dve.memset(sqsum[:], 0.0))

        def out_pe(pe, c, parts):
            for m in range(KD):
                project(pe, c, c.tiles + m, parts)

        def out_act(act, c, nblk, g0, y):
            for m in range(KD):
                for b in range(nblk):
                    round_ahead(act, g0 + nblk * m + b)
                y_act(act, c, m, y)

        def out_dve(dve, c, nblk, g0, y):
            for m in range(KD):
                dve.wait_ge(blocks_done, block_done(g0 + nblk * m + nblk - 1))
                dve.tensor_copy(y[:, m, :], bank[(c.tiles + m) % ACCS][:]).then_inc(acc_drained, 1)
                y_sum(dve, c, m)

        def out_end(c):
            c.tiles += KD
            c.sums += KD

        def attend_pe(pe, c, units):
            n = len(units)
            for s in range(n + 3):
                if s < n:
                    u, g = units[s], c.units + s
                    if g >= 2:
                        pe.wait_ge(probs_ready, g - 1)
                    pe.matmul(bank[SCORES + g % 2][:, 0:u["keys"]], u["q"], u["k"], start=True, stop=True)\
                      .then_inc(scores_ready, 1)
                if 0 <= s - 2 < n:
                    u, g = units[s - 2], c.units + s - 2
                    pe.wait_ge(probs_scaled, g + 1)
                    if g:
                        pe.wait_ge(turned_copied, g)
                    for j in range(len(u["v"])):
                        mm = pe.transpose(bank[TURNED][:, j * P:(j + 1) * P], pbuf[:, g % 3, j * P:(j + 1) * P],
                                          ident[:])
                    mm.then_inc(probs_turned, 1)
                if 0 <= s - 3 < n:
                    u, g = units[s - 3], c.units + s - 3
                    pe.wait_ge(turned_copied, g + 1)
                    hd = c.heads + (s - 3) // 4
                    if (s - 3) % 4 == 0 and hd >= 2:
                        pe.wait_ge(head_split, hd - 1)
                    for j, v in enumerate(u["v"]):
                        mm = pe.matmul(bank[HEADS][u["half"], u["n"] * P:(u["n"] + 1) * P], v,
                                       ptb[:, g % 2, j * P:(j + 1) * P], start=j == 0, stop=j == len(u["v"]) - 1)
                    mm.then_inc(attended, 1)

        def attend_dve(dve, ch, c, units, scale):
            n = len(units)
            at = {}
            for s in range(n + 5):
                if s < n:
                    u, g = units[s], c.units + s
                    r = red[:, g % 3, :]
                    dve.wait_ge(scores_ready, g + 1)
                    if g >= 3:
                        dve.wait_ge(probs_turned, g - 2)
                    if u["mask"] is not None:
                        ch.link(dve.tensor_tensor_reduce(pbuf[:, g % 3, 0:u["keys"]], bank[SCORES + g % 2][:, 0:u["keys"]],
                                                         u["mask"], 1.0, NEG, ALU.add, ALU.max, r[:, 0:1]))
                        dve.tensor_scalar(r[:, 1:2], r[:, 0:1], -scale, u["nsink"], ALU.mult, ALU.min)\
                           .then_inc(rowmax_ready, 1)
                    else:
                        ch.link(dve.reduce_max(r[:, 0:1], bank[SCORES + g % 2][:, 0:u["keys"]], mybir.AxisListType.X))
                        dve.tensor_scalar(r[:, 1:2], r[:, 0:1], -scale, None, ALU.mult).then_inc(rowmax_ready, 1)
                if 0 <= s - 1 < n:
                    u, g = units[s - 1], c.units + s - 1
                    r = red[:, g % 3, :]
                    dve.wait_ge(probs_ready, g + 1)
                    if u["mask"] is not None:
                        ch.link(dve.tensor_tensor(r[:, 4:5], r[:, 2:3], r[:, 3:4], ALU.add))
                        ch.link(dve.reciprocal(r[:, 5:6], r[:, 4:5]))
                    else:
                        ch.link(dve.reciprocal(r[:, 5:6], r[:, 2:3]))
                    dve.tensor_scalar(pbuf[:, g % 3, 0:u["keys"]], pbuf[:, g % 3, 0:u["keys"]], r[:, 5:6], None,
                                      ALU.mult).then_inc(probs_scaled, 1)
                if s - 4 >= 0 and (s - 4) % 4 == 3 and s - 4 < n:
                    u, hd = units[s - 4], (s - 4) // 4
                    dve.wait_ge(head_rounded, c.heads + hd + 1)
                    dve.tensor_tensor(u["lo"], bank[HEADS][u["half"], :], u["hi"].bitcast(F32), ALU.subtract)\
                       .then_inc(head_split, 1)

        def attend_act(act, c, units, scale):
            n = len(units)
            for s in range(n + 5):
                if s < n:
                    u, g = units[s], c.units + s
                    r = red[:, g % 3, :]
                    act.wait_ge(rowmax_ready, g + 1)
                    if u["mask"] is not None:
                        act.activation(pbuf[:, g % 3, 0:u["keys"]], pbuf[:, g % 3, 0:u["keys"]], ACT.Exp,
                                       bias=r[:, 1:2], scale=scale, accum_out=r[:, 2:3])
                        act.activation(r[:, 3:4], u["sink"], ACT.Exp, bias=r[:, 1:2]).then_inc(probs_ready, 1)
                    else:
                        act.activation(pbuf[:, g % 3, 0:u["keys"]], bank[SCORES + g % 2][:, 0:u["keys"]], ACT.Exp,
                                       bias=r[:, 1:2], scale=scale, accum_out=r[:, 2:3]).then_inc(probs_ready, 1)
                if 0 <= s - 2 < n:
                    u, g = units[s - 2], c.units + s - 2
                    act.wait_ge(probs_turned, g + 1)
                    if g >= 2:
                        act.wait_ge(attended, g - 1)
                    act.activation(ptb[:, g % 2, 0:u["keys"]], bank[TURNED][:, 0:u["keys"]], ACT.Copy)\
                       .then_inc(turned_copied, 1)
                if s - 4 >= 0 and (s - 4) % 4 == 3 and s - 4 < n:
                    u, g = units[s - 4], c.units + s - 4
                    act.wait_ge(attended, g + 1)
                    act.activation(u["hi"], bank[HEADS][u["half"], :], ACT.Copy).then_inc(head_rounded, 1)

        def attend_end(c, units):
            c.units += len(units)
            c.heads += len(units) // 4

        NB = S // P

        def even_units():
            units = []
            for j, pair in enumerate(EVEN_PAIRS):
                for side, head in enumerate(pair):
                    half = slice(side * HD, (side + 1) * HD)
                    keys = head // 3 // 2
                    for n in range(NB):
                        lo, hi = max(n - 1, 0), min(n + 1, NB - 1)
                        width = (hi - lo + 1) * P
                        off = 0 if n else P
                        units.append(dict(
                            q=e_qk[half, 2 + j, n * P:(n + 1) * P], k=e_qk[half, keys, lo * P:(hi + 1) * P],
                            keys=width, mask=e_tab[:, 1024 + off:1024 + off + width], n=n, half=half,
                            sink=e_small[:, 2 + head:3 + head], nsink=e_nsink[:, head:head + 1],
                            v=[e_v[:, keys, m * P + half.start:m * P + half.stop] for m in range(lo, hi + 1)],
                            hi=m_hi[half, 2 + j, :], lo=m_lo[half, 2 + j, :]))
            return units

        def even_sp(sp, c):
            stream_sp(sp, c.blocks, t["ev_in"], 12)
            stream_sp(sp, c.blocks + 12, t["ev_out"], 8)

        def even_pool(pool, c):
            stream_pool(pool, c.blocks, 12)
            stream_pool(pool, c.blocks + 12, 8)

        def even_end(c):
            c.blocks += 20
            c.tiles += len(EVEN_ORDER)
            c.add("side", 10)
            c.add("raw", 8)
            c.add("rotated", 8)
            attend_end(c, even_units())
            out_end(c)

        def even_pe(pe, c):
            pe.wait_ge(xl_ready, c.xn)
            k = Counts()
            k.blocks = c.blocks
            for n, (kind, i) in enumerate(EVEN_ORDER):
                tile = c.tiles + n
                out = bank[tile % ACCS][:]
                if kind == "lin":
                    project(pe, k, tile, [xs_of(xh, xl, KD)])
                elif kind == "val":
                    project_values(pe, k, tile)
                elif kind == "rot":
                    pe.wait_ge(acc_drained, acc_free(tile))
                    pe.wait_ge(raw_copied, c.at("raw") + i - 2 + 1)
                    pe.wait_ge(tables_loaded, 48)
                    pe.matmul(out, e_tab[:, 2432:2560], raw[:, i % 2, :], start=True, stop=True).then_inc(side_done, 1)
                else:
                    pe.wait_ge(acc_drained, acc_free(tile))
                    pe.wait_ge(pooled, i + 1)
                    pe.wait_ge(tables_loaded, 48)
                    pe.matmul(out, e_wg[:, i, :], e_pw[:, i, :], start=True, stop=True).then_inc(side_done, 1)
            pe.wait_ge(acc_drained, drained(c.tiles + len(EVEN_ORDER) - 1))
            pe.wait_ge(rotated, 8)
            units = even_units()
            attend_pe(pe, c, units)
            pe.wait_ge(head_split, c.heads + 12)
            pe.wait_ge(pool_split, 2)
            k.tiles = c.tiles + len(EVEN_ORDER)
            out_pe(pe, k, [xs_of(m_hi, m_lo, KD)])

        def even_act(act, c):
            act.wait_ge(blocks_done, block_done(c.blocks - 1))
            act.dma_start(e_tab[:], t["tab_even"]).then_inc(tables_loaded, 16)
            act.dma_start(e_wg[:], t["ev_wg"]).then_inc(tables_loaded, 16)
            act.dma_start(e_small[:], t["ev_small"]).then_inc(tables_loaded, 16)
            g = c.blocks
            for n, (kind, i) in enumerate(EVEN_ORDER):
                if kind in ("lin", "val"):
                    round_ahead(act, g)
                    g += 1
                if kind == "lin" and i >= 2:
                    act.wait_ge(blocks_done, block_done(g - 1))
                    act.activation(raw[:, i % 2, :], bank[(c.tiles + n) % ACCS][:], ACT.Copy).then_inc(raw_copied, 1)
                if kind == "grp":
                    act.wait_ge(acc_drained, drained(c.tiles + n))
                    act.activation(m_hi[:, i, :], tmp[:, i, :], ACT.Copy).then_inc(pool_rounded, 1)
            attend_act(act, c, even_units(), HD ** -0.5)
            k = Counts()
            k.tiles, k.sums = c.tiles + len(EVEN_ORDER), c.sums
            out_act(act, k, 1, c.blocks + 12, y)

        def even_dve(dve, ch, c):
            y_begin(dve, ch)
            dve.wait_ge(tables_loaded, 48)
            ch.link(dve.memset(e_u[:], 0.0))
            ch.link(dve.tensor_scalar(e_nsink[:], e_small[:, 2:14], -1.0, None, ALU.mult))
            side = c.at("side")
            for n, (kind, i) in enumerate(EVEN_ORDER):
                src = bank[(c.tiles + n) % ACCS][:]
                if kind == "lin" and i < 2:
                    dve.wait_ge(blocks_done, block_done(c.blocks + i))
                    dve.tensor_copy(e_u[:, i, 8:8 + S], src).then_inc(acc_drained, 1)
                    dve.wait_ge(acc_drained, drained(c.tiles + n))
                    u, a, b = e_u[:, i, :], e_a[:, 0, :], e_a[:, 1, :]
                    W = S + 16
                    ch.link(dve.tensor_tensor(a[:, 1:W], u[:, 0:W - 1], u[:, 1:W], ALU.add))
                    rows = slice(HD, P) if i == 0 else slice(0, P)
                    ch.link(dve.tensor_tensor(b[rows, 2:W - 1], a[rows, 1:W - 2], a[rows, 3:W], ALU.add))
                    if i == 1:
                        ch.link(dve.tensor_tensor(a[:, 4:W - 3], b[:, 2:W - 5], b[:, 6:W - 1], ALU.add))
                        ch.link(dve.tensor_tensor(b[HD:P, 8:W - 8], a[HD:P, 4:W - 12], a[HD:P, 12:W - 4], ALU.add))
                    ch.link(dve.tensor_tensor(e_pw[0:HD, i, :], a[0:HD, 8:8 + S], e_tab[0:HD, 1408 + i * S:1408 + (i + 1) * S], ALU.mult))
                    ch.link(dve.tensor_tensor(e_pw[HD:P, i, :], b[HD:P, 8:8 + S], e_tab[HD:P, 1408 + i * S:1408 + (i + 1) * S], ALU.mult))
                    dve.tensor_tensor(e_pw[:, i, :], e_pw[:, i, :], u[:, 8:8 + S], ALU.subtract).then_inc(pooled, 1)
                elif kind == "lin":
                    dve.wait_ge(raw_copied, c.at("raw") + i - 1)
                    dve.tensor_tensor(e_qk[:, i - 2, :], src, e_tab[:, 0:S], ALU.mult).then_inc(acc_drained, 1)
                elif kind == "rot":
                    side += 1
                    dve.wait_ge(side_done, side)
                    if i >= 4:
                        dve.wait_ge(rotated, i - 3)
                    dve.tensor_tensor(tmp[:, i % 2, :], src, e_tab[:, S:2 * S], ALU.mult).then_inc(acc_drained, 1)
                    dve.wait_ge(acc_drained, drained(c.tiles + n))
                    dve.tensor_tensor(e_qk[:, i - 2, :], e_qk[:, i - 2, :], tmp[:, i % 2, :], ALU.add)\
                       .then_inc(rotated, 1)
                elif kind == "grp":
                    side += 1
                    dve.wait_ge(side_done, side)
                    dve.tensor_scalar(tmp[:, i, :], src, e_small[:, i:i + 1], None, ALU.mult).then_inc(acc_drained, 1)
                    dve.wait_ge(pool_rounded, i + 1)
                    dve.tensor_tensor(m_lo[:, i, :], tmp[:, i, :], m_hi[:, i, :].bitcast(F32), ALU.subtract)\
                       .then_inc(pool_split, 1)
                    dve.wait_ge(pool_split, i + 1)
                else:
                    dve.wait_ge(blocks_done, block_done(c.blocks + 10 + i))
                    dve.tensor_copy(e_v[:, i, :], src).then_inc(acc_drained, 1)
            dve.wait_ge(acc_drained, drained(c.tiles + len(EVEN_ORDER) - 1))
            dve.wait_ge(rotated, 8)
            attend_dve(dve, ch, c, even_units(), HD ** -0.5)
            k = Counts()
            k.tiles, k.sums = c.tiles + len(EVEN_ORDER), c.sums
            out_dve(dve, k, 1, c.blocks + 12, y)

        SIGN, BACK, MASK_F, MASK_B = 0, 1, 2, 2 + P
        CW, CB_, LG, LB, SW, SB, DS, NG, DTB, ALOG = 0, 124, 128, 132, 136, 200, 216, 224, 232, 233
        LAST = 2 * CONV_T + 25

        def odd_sp(sp, c):
            stream_sp(sp, c.blocks, t["od_in"], ODD_LINS)
            g = c.blocks + ODD_LINS
            for m in range(KD):
                for b, nk in enumerate((8, 4)):
                    n = 2 * m + b
                    load(sp, g + n, (g + n) % RING, t["od_out"][m][:, b * 1024:b * 1024 + nk * P])

        def odd_pool(pool, c):
            stream_pool(pool, c.blocks, ODD_LINS)
            g = c.blocks + ODD_LINS
            for n in range(2 * KD):
                rest_block(pool, g + n, (g + n) % RING, (1024, 512)[n % 2])

        def odd_end(c):
            c.blocks += ODD_LINS + 2 * KD
            c.tiles += LAST + 1 + 8
            c.add("side", 1 + 8)
            c.norms += 2
            c.add("std", 1)
            c.squares += 4 + 4
            c.add("sq", 4)
            norm_end(c)
            out_end(c)

        def ssm_units():
            return [(head, st) for head in range(SH) for st in range(4)]

        def odd_pe(pe, c):
            pe.wait_ge(xl_ready, c.xn)
            k = c.copy()
            for n in range(LAST):
                project(pe, k, c.tiles + n, [xs_of(xh, xl, KD)])
            T = c.tiles + LAST
            pe.wait_ge(acc_drained, acc_free(T))
            pe.wait_ge(steps_ready, 1)
            for n in range(4):
                tok = slice(n * P, (n + 1) * P)
                pe.transpose(bank[T % ACCS][:, n * 32:(n + 1) * 32], work[0:32, 2, tok], ident[0:32, 0:32])
                mm = pe.transpose(bank[T % ACCS][:, P + n * 32:P + (n + 1) * 32], o_r[:, tok], ident[0:32, 0:32])
            mm.then_inc(side_done, 1)
            pe.wait_ge(acc_drained, drained(T))
            for i in range(CONV_T):
                sum_squares(pe, o_cv[:, i, :], i == 0, 1)

            def turn(j):
                pe.wait_ge(acc_drained, acc_free(T + 1 + j))
                pe.wait_ge(xbc_done, 16)
                n, half = j // 2, j % 2
                for q in range(4):
                    mm = pe.transpose(bank[(T + 1 + j) % ACCS][:, q * P:(q + 1) * P],
                                      o_x[:, 4 * half + q, n * P:(n + 1) * P], ident[:])
                mm.then_inc(side_done, 1)
            for j in range(4):
                turn(j)
            spread(pe, k)
            k.norms += 1
            for j in range(4, 8):
                turn(j)
            for i in range(CONV_T):
                pe.wait_ge(x_squared, c.at("sq") + i + 1)
                sum_squares(pe, sq[:, i % 2, :], i == 0, 1)
            spread(pe, k)
            k.norms += 1
            pe.wait_ge(scaled_in, 8)
            pe.wait_ge(g_split, CONV_T)
            units = ssm_units()
            n = len(units)
            for s in range(n + 2):
                if s == 0 or (s % 16 == 12 and s < 60):
                    grp = 0 if s == 0 else s // 16 + 1
                    if grp < SG:
                        for st in range(4):
                            q = grp * 4 + st
                            if q >= 2:
                                pe.wait_ge(cb_copied, q - 1)
                            pe.matmul(bank[q % 2][:], o_b[:, grp, st * P:(st + 1) * P], o_c[:, grp, :],
                                      start=True, stop=True).then_inc(cb_summed, 1)
                if s < n:
                    head, st = units[s]
                    if s >= 2:
                        pe.wait_ge(exps_ready, s - 1)
                    for d, (lo, hi, mask) in enumerate(((st * P, S, o_mask[:, 0, :]), (0, (st + 1) * P, o_mask[:, 1, :]))):
                        row = d * SH + head
                        out = bank[4 + 2 * (s % 2) + d]
                        pe.matmul(out[:, lo:hi], ident[0:32, row:row + 1].to_broadcast([32, P]), o_r[:, lo:hi],
                                  start=True, stop=True)
                        mm = pe.matmul(out[:, st * P:(st + 1) * P], identb[:], mask, start=False, stop=True,
                                       skip_group_check=True)
                    mm.then_inc(decays_spread, 1)
                if 0 <= s - 2 < n:
                    head, st = units[s - 2]
                    half, pair = slice(head % 2 * HD, (head % 2 + 1) * HD), head // 2
                    pe.wait_ge(weighted, s - 1)
                    if head % 2 == 0 and st == 0 and pair >= 2:
                        pe.wait_ge(pair_read, pair - 1)
                    out, cols = bank[2 + pair % 2], slice(head * HD, (head + 1) * HD)
                    wide = S - st * P
                    e = o_e[:, (s - 2) % 3, :]
                    pe.matmul(out[half, st * P:S], o_xf[:, st, cols], e[:, 0:wide], start=st == 0, stop=False,
                              skip_group_check=True)
                    pe.matmul(out[half, 0:(st + 1) * P], o_xb[:, st, cols], e[:, wide:640], start=False, stop=st == 3,
                              skip_group_check=True).then_inc(scanned, 1)
            k.add("sq", 4)
            norm_pe(pe, k)
            k.norms += 1
            pe.wait_ge(xl_ready, c.xn + KD)
            k.tiles = T + 9
            out_pe(pe, k, [(xs_of(g_hi, g_lo, 4)[0] + xs_of(xh, xl, 4)[0], xs_of(g_hi, g_lo, 4)[1] + xs_of(xh, xl, 4)[1]),
                           xs_of(xh, xl, 4, 4)])

        def odd_act(act, c):
            act.wait_ge(blocks_done, block_done(c.blocks - 1))
            act.dma_start(o_tab[:], t["tab_odd"]).then_inc(odd_loaded, 16)
            act.dma_start(o_small[:], t["od_small"]).then_inc(odd_loaded, 16)
            act.wait_ge(odd_loaded, 32)
            act.activation(o_a[:, 0:1], o_small[0:32, ALOG:ALOG + 1], ACT.Exp).then_inc(a_ready, 1)
            B, T = c.blocks, c.tiles
            for n in range(LAST):
                round_ahead(act, B + n)
                tile = bank[(T + n) % ACCS][:]
                if n < 2 * CONV_T and n % 2 == 1:
                    i = n // 2
                    act.wait_ge(blocks_done, block_done(B + n))
                    act.wait_ge(acc_drained, drained(T + n - 4))
                    act.activation(work[:, i % 2, :], tile, ACT.Sigmoid).then_inc(glu_done, 1)
                elif 2 * CONV_T <= n < 2 * CONV_T + 16:
                    i = n - 2 * CONV_T
                    dst = (o_x[:, i, :] if i < 8 else o_b[:, i - 8, :] if i < 12 else o_c[:, i - 12, :])
                    act.wait_ge(acc_drained, drained(T + n))
                    act.activation(dst, tmp[:, i % 2, :], ACT.Silu).then_inc(xbc_done, 1)
                elif n == 2 * CONV_T + 16:
                    act.wait_ge(dt_arg, 1)
                    act.activation(work[0:32, 3, :], work[0:32, 3, :], ACT.Exp).then_inc(dt_exp, 1)
                elif n > 2 * CONV_T + 16:
                    i = n - 2 * CONV_T - 17
                    act.wait_ge(acc_drained, drained(T + n))
                    act.activation(o_z[:, i, :], o_z[:, i, :], ACT.Silu).then_inc(z_done, 1)
            k = c.copy()
            k.squares += 4
            for i in range(CONV_T):
                act.wait_ge(centered, i + 1)
                if i >= 2:
                    act.wait_ge(squares_summed, k.squares + i - 1)
                act.activation(sq[:, i % 2, :], o_cv[:, i, :], ACT.Square).then_inc(x_squared, 1)
            std(act, k, 4)
            for i in range(CONV_T):
                act.wait_ge(normed, i + 1)
                if i >= 2:
                    act.wait_ge(g_split, i - 1)
                act.activation(tmp[:, i % 2, :], o_cv[:, i, :], ACT.Silu, bias=o_small[:, LB + i:LB + i + 1],
                               scale=o_small[:, LG + i:LG + i + 1]).then_inc(g_silu, 1)
                act.wait_ge(g_silu, i + 1)
                act.activation(g_hi[:, i, :], tmp[:, i % 2, :], ACT.Copy).then_inc(g_rounded, 1)
            for s, (head, st) in enumerate(ssm_units()):
                act.wait_ge(decays_spread, s + 1)
                if s >= 3:
                    act.wait_ge(scanned, s - 2)
                wide = S - st * P
                act.activation(o_e[:, s % 3, 0:wide], bank[4 + 2 * (s % 2)][:, st * P:S], ACT.Exp,
                               bias=o_nr[:, st, head:head + 1])
                act.activation(o_e[:, s % 3, wide:640], bank[5 + 2 * (s % 2)][:, 0:(st + 1) * P], ACT.Exp,
                               bias=o_nr[:, st, SH + head:SH + head + 1]).then_inc(exps_ready, 1)
            k = c.copy()
            k.squares += 8
            act.wait_ge(squares_summed, k.squares)
            norm_act(act, k, o_x, lambda j: act.wait_ge(gated, j + 1))
            k.tiles = T + LAST + 9
            out_act(act, k, 2, B + LAST, o_y)

        def odd_dve(dve, ch, c):
            B, T = c.blocks, c.tiles
            y_begin(dve, ch)
            dve.wait_ge(odd_loaded, 32)
            ch.link(dve.tensor_copy(o_mask[:, 0, :], o_tab[:, MASK_F:MASK_F + P]))
            ch.link(dve.tensor_copy(o_mask[:, 1, :], o_tab[:, MASK_B:MASK_B + P]))
            ch.link(dve.tensor_copy(identb[:], ident[:]))
            dve.wait_ge(a_ready, 1)
            ch.link(dve.tensor_scalar(o_a[:, 1:2], o_a[:, 0:1], -1.0, None, ALU.mult))

            taps = [(i, j) for p in (0, 2) for j in [15] + [j for j in range(CONV_K) if j != 15] for i in (p, p + 1)]
            last = {}

            def tap():
                if not taps:
                    return
                i, j = taps.pop(0)
                d = j - CONV_K // 2
                w = o_small[:, CW + i * CONV_K + j:CW + i * CONV_K + j + 1]
                if d == 0:
                    last[i] = ch.step(dve.tensor_scalar(o_cv[:, i, :], o_g[:, i, :], w, o_small[:, CB_ + i:CB_ + i + 1],
                                                        ALU.mult, ALU.add))
                    return
                a, b = max(0, -d), min(S, S - d)
                dve.wait_ge(dve_step, last[i])
                last[i] = ch.step(dve.scalar_tensor_tensor(out=o_cv[:, i, a:b], in0=o_g[:, i, a + d:b + d], scalar=w,
                                                           in1=o_cv[:, i, a:b], op0=ALU.mult, op1=ALU.add))

            for n in range(LAST):
                src = bank[(T + n) % ACCS]
                if n < 2 * CONV_T:
                    if n % 2:
                        i = n // 2
                        dve.wait_ge(glu_done, i + 1)
                        dve.tensor_tensor(o_g[:, i, :], work[:, i % 2, :], bank[(T + n - 1) % ACCS][:], ALU.mult)\
                           .then_inc(acc_drained, 2)
                        dve.wait_ge(acc_drained, drained(T + n))
                    continue
                dve.wait_ge(blocks_done, block_done(B + n))
                if n < 2 * CONV_T + 16:
                    i = n - 2 * CONV_T
                    if i >= 2:
                        dve.wait_ge(xbc_done, i - 1)
                    o = tmp[:, i % 2, :]

                    def w(j):
                        return o_small[:, SW + i * SSM_K + j:SW + i * SSM_K + j + 1]
                    at = ch.step(dve.tensor_scalar(o, src[:], w(2), o_small[:, SB + i:SB + i + 1], ALU.mult, ALU.add))
                    for j, (a, b, d) in ((0, (2, S, -2)), (1, (1, S, -1)), (3, (0, S - 1, 1))):
                        tap()
                        dve.wait_ge(dve_step, at)
                        ins = dve.scalar_tensor_tensor(out=o[:, a:b], in0=src[:, a + d:b + d], scalar=w(j), in1=o[:, a:b],
                                                       op0=ALU.mult, op1=ALU.add)
                        if j < 3:
                            at = ch.step(ins)
                        else:
                            ins.then_inc(acc_drained, 1)
                    tap()
                elif n == 2 * CONV_T + 16:
                    A, Bq, C, Dq = (work[0:32, q, :] for q in (2, 3, 4, 5))
                    dve.tensor_scalar(A, src[0:32, :], o_small[0:32, DTB:DTB + 1], None, ALU.add).then_inc(acc_drained, 1)
                    dve.wait_ge(acc_drained, drained(T + n))
                    dve.scalar_tensor_tensor(out=Bq, in0=A, scalar=-1.0, in1=A, op0=ALU.mult, op1=ALU.min)\
                       .then_inc(dt_arg, 1)
                    dve.wait_ge(dt_exp, 1)
                    ch.link(dve.tensor_scalar(C, Bq, 2.0, None, ALU.add))
                    ch.link(dve.reciprocal(C, C))
                    ch.link(dve.tensor_tensor(Bq, Bq, C, ALU.mult))
                    ch.link(dve.tensor_tensor(C, Bq, Bq, ALU.mult))
                    ch.link(dve.tensor_scalar(Dq, C, 1.0 / (2 * LOG_TERMS + 1), None, ALU.mult))
                    for q in range(LOG_TERMS - 1, 0, -1):
                        ch.link(dve.scalar_tensor_tensor(out=Dq, in0=Dq, scalar=1.0 / (2 * q + 1), in1=C, op0=ALU.add, op1=ALU.mult))
                    ch.link(dve.scalar_tensor_tensor(out=Dq, in0=Dq, scalar=1.0, in1=Bq, op0=ALU.add, op1=ALU.mult))
                    ch.link(dve.tensor_scalar(A, A, 0.0, None, ALU.max))
                    ch.link(dve.scalar_tensor_tensor(out=A, in0=Dq, scalar=2.0, in1=A, op0=ALU.mult, op1=ALU.add))
                    ch.link(dve.tensor_scalar(Bq, A, o_a[:, 1:2], None, ALU.mult))
                    ch.link(dve.memset(Dq, 1.0))
                    ch.link(dve.tensor_tensor_scan(C, Dq, Bq, 0.0, ALU.mult, ALU.add))
                    ch.link(dve.tensor_scalar(Bq, Bq, o_tab[0:32, BACK:BACK + 1], None, ALU.mult))
                    dve.scalar_tensor_tensor(out=o_r[:], in0=C, scalar=o_tab[0:32, SIGN:SIGN + 1], in1=Bq,
                                             op0=ALU.mult, op1=ALU.add).then_inc(steps_ready, 1)
                else:
                    i = n - 2 * CONV_T - 17
                    dve.tensor_copy(o_z[:, i, :], src[:]).then_inc(acc_drained, 1)
                    for _ in range(8):
                        tap()
            while taps:
                tap()
            dve.wait_ge(dve_step, ch.n)
            k = c.copy()
            T2, side = T + LAST, c.at("side")
            dve.wait_ge(side_done, side + 1)
            ch.link(dve.tensor_copy(o_dt[:], bank[T2 % ACCS][:, 0:P]))
            dve.tensor_scalar(o_nr[:], bank[T2 % ACCS][:, P:2 * P], -1.0, None, ALU.mult).then_inc(acc_drained, 1)
            dve.wait_ge(squares_summed, c.squares + 4)
            dve.tensor_copy(stat[:, 1, 0:4], bank[STAT][:, 0:4]).then_inc(rstd_ready, 1)
            dve.wait_ge(acc_drained, drained(T2))

            def scale_in(j):
                n, half = j // 2, j % 2
                src = bank[(T2 + 1 + j) % ACCS][:].rearrange("p (h d) -> p h d", d=HD)
                dve.wait_ge(side_done, side + 2 + j)
                for d, dst in enumerate((o_xf, o_xb)):
                    step = o_dt[:, n, d * SH + 8 * half:d * SH + 8 * half + 8].unsqueeze(2).broadcast_to([P, 8, HD])
                    ins = dve.tensor_tensor(dst[:, n, half * S:(half + 1) * S].rearrange("p (h d) -> p h d", d=HD),
                                            src, step, ALU.mult)
                    ins.then_inc(scaled_in if d == 0 else acc_drained, 1)
            for j in range(4):
                scale_in(j)
            dve.wait_ge(spread_ready, k.norms + 1)
            k.norms += 1
            for i in range(CONV_T):
                dve.tensor_tensor(o_cv[:, i, :], o_cv[:, i, :], bank[SPREAD][:], ALU.subtract).then_inc(centered, 1)
            for j in range(4, 8):
                scale_in(j)
            rstd(dve, k)
            k.norms += 1
            k.add("std", 1)
            dve.wait_ge(centered, CONV_T)
            for i in range(CONV_T):
                dve.tensor_tensor(o_cv[:, i, :], o_cv[:, i, :], bank[SPREAD][:], ALU.mult).then_inc(normed, 1)
            for i in range(CONV_T):
                dve.wait_ge(g_rounded, i + 1)
                dve.tensor_tensor(g_lo[:, i, :], tmp[:, i % 2, :], g_hi[:, i, :].bitcast(F32), ALU.subtract)\
                   .then_inc(g_split, 1)
            dve.wait_ge(z_done, KD)
            units = ssm_units()
            n = len(units)
            for s in range(n + 3):
                if s == 0 or (s % 16 == 12 and s < 60):
                    grp = 0 if s == 0 else s // 16 + 1
                    if grp < SG:
                        for st in range(4):
                            dve.wait_ge(cb_summed, grp * 4 + st + 1)
                            dve.tensor_copy(o_cb[:, grp % 2, st, :], bank[st % 2][:]).then_inc(cb_copied, 1)
                if s < n:
                    head, st = units[s]
                    grp, wide = head // 4, S - st * P
                    if head % 4 == 0 and st == 0:
                        dve.wait_ge(cb_copied, 4 * grp + 4)
                    dve.wait_ge(exps_ready, s + 1)
                    e, cb = o_e[:, s % 3, :], o_cb[:, grp % 2, st, :]
                    dve.tensor_tensor(e[:, 0:wide], e[:, 0:wide], cb[:, st * P:S], ALU.mult)
                    dve.tensor_tensor(e[:, wide:640], e[:, wide:640], cb[:, 0:(st + 1) * P], ALU.mult)\
                       .then_inc(weighted, 1)
                if s - 3 >= 0 and (s - 3) % 8 == 7:
                    j = (s - 3) // 8
                    dve.wait_ge(scanned, s - 2)
                    dve.scalar_tensor_tensor(out=o_x[:, j, :], in0=o_x[:, j, :], scalar=o_small[:, DS + j:DS + j + 1],
                                             in1=bank[2 + j % 2][:], op0=ALU.mult, op1=ALU.add).then_inc(pair_read, 1)
                    dve.wait_ge(pair_read, j + 1)
                    dve.tensor_tensor(o_x[:, j, :], o_x[:, j, :], o_z[:, j, :], ALU.mult).then_inc(gated, 1)
            dve.wait_ge(gated, KD)
            norm_dve(dve, k, o_x, lambda j: o_small[:, NG + j:NG + j + 1])
            k.tiles = T2 + 9
            out_dve(dve, k, 2, B + LAST, o_y)

        COS_A, SIN_A, COS_B, SIN_B, ROT_A, ROT_B = 0, S, 2 * S, 3 * S, 4 * S, 4 * S + P
        NORMS2 = [("qk", i) for i in range(RAWS)] + [("cq", i) for i in range(QR)] + [("kv", i) for i in range(KR)]
        LINS2 = NORMS2 + [("kr", 0), ("va", 0)]
        SIDES2 = ([("spread", i) for i in range(RAWS)] + [("spread", RAWS), ("spread", RAWS + 1), ("rotkr", 0)]
                  + [("rot", i) for i in range(RAWS)])
        UPS2 = []
        for _h in range(8):
            UPS2 += [("up", _h)] + ([("rotup", _h - 1)] if _h else [])
        UPS2 += [("kn", 0), ("rotup", 7), ("kn", 1), ("kn", 2), ("kn", 3)] + [("vb", i) for i in range(4)]
        ORDER2 = LINS2 + SIDES2 + UPS2
        UP_HEADS = (3, 3, 2)

        def mix2_blocks():
            return [1024] * len(LINS2) + [n * QR * QK for n in UP_HEADS] + [1024, 1024] + [1024] * (3 * KD) + [1024] * KD

        def grouped_units():
            return [dict(q=b_qk[half, j, n * P:(n + 1) * P], k=b_qk[half, 4, :], keys=S, mask=None, n=n, half=half,
                         v=[b_va[:, m * P + half.start:m * P + half.stop] for m in range(4)], hi=ya_hi[half, j, :], lo=ya_lo[half, j, :])
                    for j in range(4) for half in (slice(0, HD), slice(HD, P)) for n in range(4)]

        def latent_units():
            return [dict(q=b_q[0:QK, head, n * P:(n + 1) * P], k=b_k[0:QK, head, :], keys=S, mask=None, n=n, half=half,
                         v=[b_vb[:, head // 2, m * P + half.start:m * P + half.stop] for m in range(4)], hi=yb_hi[half, head // 2, :],
                         lo=yb_lo[half, head // 2, :])
                    for head in range(8) for half in (slice(head % 2 * HD, head % 2 * HD + HD),) for n in range(4)]

        def mix2_sp(sp, c, i):
            g = c.blocks
            stream_sp(sp, g, t["b_in"][i], len(LINS2))
            g += len(LINS2)
            for b, n in enumerate(UP_HEADS):
                w = QR * QK
                load(sp, g + b, (g + b) % RING, t["b_up"][i][:, 3 * b * w:(3 * b + n) * w])
            g += 3
            stream_sp(sp, g, t["b_kv"][i], 2)
            stream_sp(sp, g + 2, t["b_gates"][i], 3 * KD)
            stream_sp(sp, g + 2 + 3 * KD, t["b_out"][i], KD)

        def mix2_pool(pool, c):
            g = c.blocks
            stream_pool(pool, g, len(LINS2))
            g += len(LINS2)
            for b, n in enumerate(UP_HEADS):
                rest_block(pool, g + b, (g + b) % RING, n * QR * QK)
            stream_pool(pool, g + 3, 2 + 4 * KD)

        def mix2_end(c):
            c.blocks += len(mix2_blocks())
            c.tiles += len(ORDER2)
            c.add("side", len(SIDES2) + 8)
            c.add("raw", 1 + 8)
            c.add("rotated", RAWS + 1 + 8)
            c.add("sq", len(NORMS2))
            c.squares += len(NORMS2)
            c.add("std", 1)
            c.add("rstd2", 1)
            c.xn += QR + KR
            attend_end(c, grouped_units())
            attend_end(c, latent_units())
            c.tiles += 4 * KD
            c.add("gates", KD)
            c.add("tables", 1)
            out_end(c)

        def stat_cols(i):
            return slice(8 * i, 8 * i + 8) if i < RAWS else slice(8 * RAWS + 4 * (i - RAWS), 8 * RAWS + 4 * (i - RAWS) + 4)

        def norm_group(i):
            return i if i < RAWS else RAWS if i < RAWS + QR else RAWS + 1

        def mix2_pe(pe, c):
            pe.wait_ge(xl_ready, c.xn)
            k = c.copy()
            side = 0
            kn_slot = vb_slot = None

            def sums(i):
                pe.wait_ge(x_squared, c.at("sq") + i + 1)
                col = stat_cols(norm_group(i))
                for n in range(4):
                    src = sq[:, i % 2, n * P:(n + 1) * P]
                    if i < RAWS:
                        mm = pe.matmul(bank[STAT][:, col.start + 2 * n:col.start + 2 * n + 2], src, meancol[:, 4:6],
                                       start=i == 0 and n == 0, stop=True, skip_group_check=True)
                    else:
                        m = 2 if i < RAWS + QR else 3
                        mm = pe.matmul(bank[STAT][:, col.start + n:col.start + n + 1], src, meancol[:, m:m + 1],
                                       start=False, stop=True, skip_group_check=True)
                mm.then_inc(squares_summed, 1)

            for n, (kind, i) in enumerate(ORDER2):
                tile = c.tiles + n
                out = bank[tile % ACCS][:]
                if kind in ("qk", "cq", "kv", "kr"):
                    project(pe, k, tile, [xs_of(xh, xl, KD)])
                elif kind == "va":
                    project_values(pe, k, tile)
                elif kind == "spread":
                    pe.wait_ge(acc_drained, acc_free(tile))
                    pe.wait_ge(rstd2_ready, c.at("rstd2") + 1)
                    col = stat_cols(i).start
                    for m in range(4):
                        many = 2 if i < RAWS else 1
                        for half in range(many):
                            r = stat[:, 1, col + many * m + half:col + many * m + half + 1].to_broadcast([P, P // many])
                            rows = slice(half * HD, (half + 1) * HD) if many == 2 else slice(0, P)
                            mm = pe.matmul(out[rows, m * P:(m + 1) * P], r, ident[:], start=True, stop=True)
                    mm.then_inc(side_done, 1)
                elif kind == "rotkr":
                    pe.wait_ge(acc_drained, acc_free(tile))
                    pe.wait_ge(raw_copied, c.at("raw") + 1)
                    pe.wait_ge(tables_loaded, 48 + 32 * (c.at("tables") + 1))
                    pe.matmul(out[0:QK, :], b_tab[0:QK, ROT_B:ROT_B + QK], raw[0:QK, 0, :], start=True, stop=True)\
                      .then_inc(side_done, 1)
                elif kind == "rot":
                    pe.wait_ge(acc_drained, acc_free(tile))
                    pe.wait_ge(acc_drained, drained(c.tiles + len(LINS2) + i))
                    pe.matmul(out, b_tab[:, ROT_A:ROT_A + P], b_qk[:, i, :], start=True, stop=True)\
                      .then_inc(side_done, 1)
                elif kind == "rotup":
                    pe.wait_ge(acc_drained, acc_free(tile))
                    pe.wait_ge(raw_copied, c.at("raw") + 1 + i + 1)
                    pe.matmul(out[0:QK, :], b_tab[0:QK, ROT_B:ROT_B + QK], raw[0:QK, (1 + i) % 2, :], start=True, stop=True)\
                      .then_inc(side_done, 1)
                elif kind == "up":
                    pe.wait_ge(acc_drained, acc_free(tile))
                    if i == 0:
                        pe.wait_ge(xl_ready, c.xn + QR + KR)
                    if i % 3 == 0:
                        up_slot = take_block(pe, k)
                    for q in range(QR):
                        at = (i % 3 * QR + q) * QK
                        wh, wl = w_hi[:, up_slot, at:at + QK], w_lo[:, up_slot, at:at + QK]
                        pe.matmul(out[0:QK, :], wh, c_hi[:, q, :], start=q == 0, stop=False)
                        pe.matmul(out[0:QK, :], wh, c_lo[:, q, :], start=False, stop=False)
                        mm = pe.matmul(out[0:QK, :], wl, c_hi[:, q, :], start=False, stop=q == QR - 1)
                    mm.then_inc(blocks_done if i % 3 == 2 or i == 7 else up_done, 1)
                elif kind == "kn":
                    pe.wait_ge(acc_drained, acc_free(tile))
                    if i == 0:
                        kn_slot = take_block(pe, k)
                    for q in range(KR):
                        at = (i * KR + q) * P
                        wh, wl = w_hi[:, kn_slot, at:at + P], w_lo[:, kn_slot, at:at + P]
                        pe.matmul(out, wh, c_hi[:, QR + q, :], start=q == 0, stop=False)
                        pe.matmul(out, wh, c_lo[:, QR + q, :], start=False, stop=False)
                        mm = pe.matmul(out, wl, c_hi[:, QR + q, :], start=False, stop=q == KR - 1)
                    mm.then_inc(blocks_done if i == 3 else up_done, 1)
                else:
                    pe.wait_ge(acc_drained, acc_free(tile))
                    if i == 0:
                        vb_slot = take_block(pe, k)
                    for m in range(4):
                        tok = slice(m * P, (m + 1) * P)
                        for q in range(KR):
                            at = (i * KR + q) * P
                            wh, wl = w_hi[:, vb_slot, at:at + P], w_lo[:, vb_slot, at:at + P]
                            pe.matmul(out[:, tok], c_hi[:, QR + q, tok], wh, start=q == 0, stop=False)
                            pe.matmul(out[:, tok], c_hi[:, QR + q, tok], wl, start=False, stop=False)
                            mm = pe.matmul(out[:, tok], c_lo[:, QR + q, tok], wh, start=False, stop=q == KR - 1)
                    mm.then_inc(blocks_done if i == 3 else up_done, 1)
                if 1 <= n <= len(NORMS2):
                    sums(n - 1)
            pe.wait_ge(acc_drained, drained(c.tiles + len(ORDER2) - 1))
            pe.wait_ge(rotated, c.at("rotated") + RAWS + 1 + 8)
            pe.wait_ge(kr_copied, c.at("tables") + 1)
            units = grouped_units()
            attend_pe(pe, k, units)
            attend_end(k, units)
            units = latent_units()
            attend_pe(pe, k, units)
            attend_end(k, units)
            pe.wait_ge(head_split, k.heads)
            k.tiles = c.tiles + len(ORDER2)
            for m in range(KD):
                for q in range(2):
                    project(pe, k, k.tiles, [xs_of(xh, xl, KD)])
                    k.tiles += 1
                slot = take_block(pe, k)
                for q, (hi, lo) in enumerate(((ya_hi, ya_lo), (yb_hi, yb_lo))):
                    pe.wait_ge(acc_drained, acc_free(k.tiles))
                    out = bank[k.tiles % ACCS][:]
                    for j in range(4):
                        at = (4 * q + j) * P
                        wh, wl = w_hi[:, slot, at:at + P], w_lo[:, slot, at:at + P]
                        pe.matmul(out, wh, hi[:, j, :], start=j == 0, stop=False)
                        pe.matmul(out, wh, lo[:, j, :], start=False, stop=False)
                        mm = pe.matmul(out, wl, hi[:, j, :], start=False, stop=j == 3)
                    if q:
                        mm.then_inc(blocks_done, 1)
                    k.tiles += 1
            pe.wait_ge(merged_split, KD * (c.at("tables") + 1))
            out_pe(pe, k, [xs_of(mm_hi, mm_lo, KD)])

        def mix2_act(act, c, layer):
            act.wait_ge(blocks_done, block_done(c.blocks - 1))
            act.dma_start(b_tab[:], t["tab_b"]).then_inc(tables_loaded, 16)
            act.dma_start(b_small[:], t["b_small"][layer]).then_inc(tables_loaded, 16)
            g = c.blocks
            T = c.tiles
            raws = c.at("raw")
            for n, (kind, i) in enumerate(ORDER2):
                src = bank[(T + n) % ACCS]
                if kind in ("qk", "cq", "kv", "kr", "va") or (kind == "up" and i % 3 == 0) or (kind in ("kn", "vb") and i == 0):
                    round_ahead(act, g)
                    g += 1
                if kind in ("qk", "cq", "kv"):
                    act.wait_ge(acc_drained, drained(T + n))
                    if n >= 2:
                        act.wait_ge(squares_summed, c.squares + n - 1)
                    dst = b_qk[:, i, :] if kind == "qk" else c_raw[:, i if kind == "cq" else QR + i, :]
                    act.activation(sq[:, n % 2, :], dst, ACT.Square).then_inc(x_squared, 1)
                elif kind == "kr":
                    act.wait_ge(blocks_done, block_done(g - 1))
                    act.activation(raw[0:QK, 0, :], src[0:QK, :], ACT.Copy).then_inc(raw_copied, 1)
                elif kind == "va":
                    act.wait_ge(squares_summed, c.squares + len(NORMS2))
                    act.activation(stat[:, 0, :], bank[STAT][:, 0:48], ACT.Sqrt, bias=EPS).then_inc(std_ready, 1)
                elif kind == "spread" and i >= RAWS:
                    for q in range(QR if i == RAWS else KR):
                        j = q if i == RAWS else QR + q
                        if q == (QR if i == RAWS else KR) - 1:
                            act.wait_ge(acc_drained, drained(T + n))
                        else:
                            act.wait_ge(cn_ready, (QR + KR - 2) * c.at("tables") + (q if i == RAWS else QR - 1 + q) + 1)
                        act.activation(c_hi[:, j, :], tmp[:, j % 2, :], ACT.Copy).then_inc(xh_ready, 1)
                elif kind == "up":
                    act.wait_ge(blocks_done if i % 3 == 2 or i == 7 else up_done, block_done(g - 1) if i % 3 == 2 or i == 7
                                else ups(c, i))
                    act.activation(raw[0:QK, (1 + i) % 2, :], src[0:QK, :], ACT.Copy).then_inc(raw_copied, 1)
                elif kind == "rotkr":
                    act.wait_ge(rotated, c.at("rotated") + 1)
                    act.activation(b_k[HD:QK, :, :], krot[HD:QK, :].unsqueeze(1).broadcast_to([QK - HD, 8, S]), ACT.Copy)\
                       .then_inc(kr_copied, 1)
            k = c.copy()
            for units, scale in ((grouped_units(), HD ** -0.5), (latent_units(), QK ** -0.5)):
                attend_act(act, k, units, scale)
                attend_end(k, units)
            T += len(ORDER2)
            G = KD * c.at("tables")
            for m in range(KD):
                for q in range(2):
                    round_ahead(act, g)
                    act.wait_ge(blocks_done, block_done(g))
                    g += 1
                    if q == 0:
                        act.wait_ge(acc_drained, drained(T + 4 * m - 1))
                    act.activation(work[:, q, :], bank[(T + 4 * m + q) % ACCS][:], ACT.Sigmoid,
                                   bias=b_small[:, 8 + KD * q + m:9 + KD * q + m]).then_inc(gate_ready, 1)
                round_ahead(act, g)
                g += 1
                act.wait_ge(merged, G + m + 1)
                act.activation(mm_hi[:, m, :], work[:, 2, :], ACT.Copy).then_inc(merged_rounded, 1)
            k.tiles = T + 4 * KD
            out_act(act, k, 1, g, y)

        def ups(c, i):
            return 11 * c.at("tables") + i + 1 - i // 3

        def mix2_dve(dve, ch, c):
            y_begin(dve, ch)
            T, B, L = c.tiles, c.blocks, c.at("tables")
            side, rots = c.at("side"), c.at("rotated")
            dve.wait_ge(tables_loaded, 48 + 32 * (L + 1))
            xn = c.xn
            for n, (kind, i) in enumerate(ORDER2):
                src = bank[(T + n) % ACCS]
                if n < len(LINS2):
                    dve.wait_ge(blocks_done, block_done(B + n))
                if kind == "qk":
                    dve.tensor_copy(b_qk[:, i, :], src[:]).then_inc(acc_drained, 1)
                elif kind in ("cq", "kv"):
                    dve.tensor_copy(c_raw[:, i if kind == "cq" else QR + i, :], src[:]).then_inc(acc_drained, 1)
                elif kind == "kr":
                    dve.wait_ge(raw_copied, c.at("raw") + 1)
                    dve.tensor_tensor(krot[0:QK, :], src[0:QK, :], b_tab[0:QK, COS_B:COS_B + S], ALU.mult).then_inc(acc_drained, 1)
                elif kind == "va":
                    dve.tensor_copy(b_va[:], src[:]).then_inc(acc_drained, 1)
                    dve.wait_ge(std_ready, c.at("std") + 1)
                    dve.reciprocal(stat[:, 1, :], stat[:, 0, :]).then_inc(rstd2_ready, 1)
                elif kind == "spread" and i < RAWS:
                    side += 1
                    dve.wait_ge(side_done, side)
                    gain = b_small[:, 0:1] if i < 4 else b_small[:, 1:2]
                    dve.scalar_tensor_tensor(out=b_qk[:, i, :], in0=b_qk[:, i, :], scalar=gain, in1=src[:],
                                             op0=ALU.mult, op1=ALU.mult).then_inc(acc_drained, 1)
                elif kind == "spread":
                    side += 1
                    dve.wait_ge(side_done, side)
                    many = QR if i == RAWS else KR
                    for q in range(many):
                        j = q if i == RAWS else QR + q
                        if j >= 2:
                            dve.wait_ge(xl_ready, xn + j - 1)
                        dve.scalar_tensor_tensor(out=tmp[:, j % 2, :], in0=c_raw[:, j, :], scalar=b_small[:, 2 + j:3 + j],
                                                 in1=src[:], op0=ALU.mult, op1=ALU.mult)\
                           .then_inc(acc_drained if q == many - 1 else cn_ready, 1)
                        dve.wait_ge(xh_ready, xn + j + 1)
                        dve.tensor_tensor(c_lo[:, j, :], tmp[:, j % 2, :], c_hi[:, j, :].bitcast(F32), ALU.subtract)\
                           .then_inc(xl_ready, 1)
                    dve.wait_ge(xl_ready, xn + j + 1)
                elif kind == "rotkr":
                    side, rots = side + 1, rots + 1
                    dve.wait_ge(side_done, side)
                    dve.tensor_tensor(work[0:QK, 0, :], src[0:QK, :], b_tab[0:QK, SIN_B:SIN_B + S], ALU.mult).then_inc(acc_drained, 1)
                    dve.wait_ge(acc_drained, drained(T + n))
                    dve.tensor_tensor(krot[0:QK, :], krot[0:QK, :], work[0:QK, 0, :], ALU.add).then_inc(rotated, 1)
                elif kind == "rot":
                    side, rots = side + 1, rots + 1
                    dve.wait_ge(side_done, side)
                    dve.wait_ge(rotated, rots - 1)
                    dve.tensor_tensor(work[:, 0, :], src[:], b_tab[:, SIN_A:SIN_A + S], ALU.mult).then_inc(acc_drained, 1)
                    ch.link(dve.tensor_tensor(b_qk[:, i, :], b_qk[:, i, :], b_tab[:, COS_A:COS_A + S], ALU.mult))
                    dve.tensor_tensor(b_qk[:, i, :], b_qk[:, i, :], work[:, 0, :], ALU.add).then_inc(rotated, 1)
                elif kind == "up":
                    dve.wait_ge(raw_copied, c.at("raw") + 1 + i + 1)
                    dve.tensor_tensor(b_q[0:QK, i, :], src[0:QK, :], b_tab[0:QK, COS_B:COS_B + S], ALU.mult).then_inc(acc_drained, 1)
                elif kind == "rotup":
                    side, rots = side + 1, rots + 1
                    dve.wait_ge(side_done, side)
                    dve.wait_ge(rotated, rots - 1)
                    dve.tensor_tensor(work[0:QK, 0, :], src[0:QK, :], b_tab[0:QK, SIN_B:SIN_B + S], ALU.mult).then_inc(acc_drained, 1)
                    dve.wait_ge(acc_drained, drained(T + n))
                    dve.tensor_tensor(b_q[0:QK, i, :], b_q[0:QK, i, :], work[0:QK, 0, :], ALU.add).then_inc(rotated, 1)
                elif kind == "kn":
                    if i == 3:
                        dve.wait_ge(blocks_done, block_done(B + len(LINS2) + 3))
                    else:
                        dve.wait_ge(up_done, 11 * L + 5 + i + 1)
                    ch.link(dve.tensor_copy(b_k[0:HD, 2 * i, :], src[0:HD, :]))
                    dve.tensor_copy(b_k[0:HD, 2 * i + 1, :], src[HD:P, :]).then_inc(acc_drained, 1)
                elif kind == "vb":
                    if i == 3:
                        dve.wait_ge(blocks_done, block_done(B + len(LINS2) + 4))
                    else:
                        dve.wait_ge(up_done, 11 * L + 8 + i + 1)
                    dve.tensor_copy(b_vb[:, i, :], src[:]).then_inc(acc_drained, 1)
            k = c.copy()
            for units, scale in ((grouped_units(), HD ** -0.5), (latent_units(), QK ** -0.5)):
                attend_dve(dve, ch, k, units, scale)
                attend_end(k, units)
            T += len(ORDER2)
            G, g = KD * L, B + len(LINS2) + 5
            for m in range(KD):
                dve.wait_ge(gate_ready, 2 * (G + m) + 2)
                dve.wait_ge(blocks_done, block_done(g + 3 * m + 2))
                dve.wait_ge(merged_split, G + m) if G + m else None
                dve.tensor_tensor(work[:, 2, :], work[:, 0, :], bank[(T + 4 * m + 2) % ACCS][:], ALU.mult).then_inc(acc_drained, 3)
                dve.tensor_tensor(work[:, 3, :], work[:, 1, :], bank[(T + 4 * m + 3) % ACCS][:], ALU.mult).then_inc(acc_drained, 1)
                dve.wait_ge(acc_drained, drained(T + 4 * m + 3))
                dve.tensor_tensor(work[:, 2, :], work[:, 2, :], work[:, 3, :], ALU.add).then_inc(merged, 1)
                dve.wait_ge(merged_rounded, G + m + 1)
                dve.tensor_tensor(mm_lo[:, m, :], work[:, 2, :], mm_hi[:, m, :].bitcast(F32), ALU.subtract)\
                   .then_inc(merged_split, 1)
            k.tiles = T + 4 * KD
            out_dve(dve, k, 1, g + 3 * KD, y)

        def ffn2_end(c):
            c.blocks += 2 * (NH + 2 * KD)
            c.tiles += 2 * (NH + KD)
            c.hidden += 2 * NH
            c.sums += KD

        def ffn2_sp(sp, c, i):
            g = c.blocks
            for part in range(2):
                stream_sp(sp, g, t["b_ffn_up"][i, part], NH)
                stream_sp(sp, g + NH, t["b_ffn_down"][i, part], 2 * KD)
                g += NH + 2 * KD

        def ffn2_pool(pool, c):
            stream_pool(pool, c.blocks, 2 * (NH + 2 * KD))

        def ffn2_pe(pe, c):
            B, T = c.blocks, c.tiles
            pe.wait_ge(xl_ready, c.xn)
            for part in range(2):
                with pe.Fori(0, NH // 4) as it:
                    for j in range(4):
                        pe.wait_ge(acc_drained, it * 4 + acc_free(T + j))
                        pe.wait_ge(w_rest, it * 4 + rest_done(B + j))
                        products(pe, bank[(T + j) % ACCS][:], (B + j) % RING, *xs_of(xh, xl, KD), True, True)
                B += NH
                T += NH
                pe.wait_ge(hl_done, 2 + c.hidden + NH * (part + 1))
                with pe.Fori(0, 2) as it:
                    for m in range(4):
                        pe.wait_ge(acc_drained, it * 4 + acc_free(T + m))
                        for b in range(2):
                            pe.wait_ge(w_rest, it * 8 + rest_done(B + 2 * m + b))
                            products(pe, bank[(T + m) % ACCS][:], (B + 2 * m + b) % RING,
                                     *xs_of(hh2, hl2, 8, 8 * b), b == 0, b == 1)
                B += 2 * KD
                T += KD

        def ffn2_act(act, c):
            B, T, H = c.blocks, c.tiles, c.hidden
            for part in range(2):
                with act.Fori(0, NH // 4) as it:
                    for j in range(4):
                        g = B + j + AHEAD
                        round_block(act, it * 4 + g, g % RING, it + g // RING, 1024)
                        act.wait_ge(blocks_done, it * 4 + block_done(B + j))
                        act.wait_ge(acc_drained, it * 4 + drained(T + j - 2))
                        act.activation(sig[:, j % 2, :], bank[(T + j) % ACCS][:], ACT.Relu).then_inc(silu_done, 1)
                        act.wait_ge(acc_drained, it * 4 + drained(T + j))
                        act.activation(hh2[:, it * 4 + j, :], h[:, j % 2, :], ACT.Copy).then_inc(hh_done, 1)
                B += NH
                T += NH
                k = c.copy()
                k.tiles = T
                for m in range(KD):
                    for b in range(2):
                        round_ahead(act, B + 2 * m + b)
                    if part:
                        act.wait_ge(acc_drained, drained(T + m))
                        act.wait_ge(sum_used, c.sums + m + 1)
                        act.activation(sq[:, m % 2, :], y_b[:, m, :], ACT.Square).then_inc(y_squared, 1)
                B += 2 * KD
                T += KD

        def ffn2_dve(dve, ch, c):
            B, T, H = c.blocks, c.tiles, c.hidden
            y_begin(dve, ch)
            for part in range(2):
                with dve.Fori(0, NH // 4) as it:
                    for j in range(4):
                        dve.wait_ge(silu_done, it * 4 + (H + j + 1))
                        dve.wait_ge(hl_done, it * 4 + (H + j + 1))
                        dve.scalar_tensor_tensor(out=h[:, j % 2, :], in0=bank[(T + j) % ACCS][:], scalar=0.0,
                                                 in1=sig[:, j % 2, :], op0=ALU.max, op1=ALU.mult).then_inc(acc_drained, 1)
                        dve.wait_ge(hh_done, it * 4 + (H + j + 1))
                        dve.tensor_tensor(hl2[:, it * 4 + j, :], h[:, j % 2, :], hh2[:, it * 4 + j, :].bitcast(F32),
                                          ALU.subtract).then_inc(hl_done, 1)
                B += NH
                T += NH
                H += NH
                for m in range(KD):
                    dve.wait_ge(blocks_done, block_done(B + 2 * m + 1))
                    if part == 0:
                        dve.tensor_copy(y_b[:, m, :], bank[(T + m) % ACCS][:]).then_inc(acc_drained, 1)
                    else:
                        dve.wait_ge(acc_drained, drained(T + m - 1))
                        dve.tensor_tensor(y_b[:, m, :], y_b[:, m, :], bank[(T + m) % ACCS][:], ALU.add)\
                           .then_inc(acc_drained, 1)
                        y_sum(dve, c, m)
                B += 2 * KD
                T += KD

        PHASES = [("ffn", 0), ("even", 0), ("ffn", 1), ("ffn", 2), ("odd", 0), ("ffn", 3),
                  ("mix2", 0), ("ffn2", 0), ("mix2", 1), ("ffn2", 1)][:stop]
        for kind, _ in PHASES:
            widths.extend({"ffn": [1024] * (2 * NF) + [n * P for n in DOWN] * KD,
                           "even": [1024] * 20,
                           "odd": [1024] * ODD_LINS + [1024, 512] * KD,
                           "mix2": mix2_blocks(),
                           "ffn2": [1024] * (2 * (NH + 2 * KD))}[kind])
        END = {"ffn": ffn_end, "even": even_end, "odd": odd_end, "mix2": mix2_end, "ffn2": ffn2_end}

        def end(kind, c):
            END[kind](c)

        @block.sync
        def _(sp):
            c = Counts()
            sp.dma_start(gains[:], t["gains"]).then_inc(gains_loaded, 16)
            sp.dma_start(x[:], t["x"]).then_inc(x_loaded, 16)
            for kind, i in PHASES:
                pre_end(c)
                if kind == "ffn":
                    ffn_sp(sp, c, i)
                elif kind == "even":
                    even_sp(sp, c)
                elif kind == "odd":
                    odd_sp(sp, c)
                elif kind == "mix2":
                    mix2_sp(sp, c, i)
                else:
                    ffn2_sp(sp, c, i)
                end(kind, c)
                post_end(c)
            sp.wait_ge(x_ready, c.xr)
            sp.dma_start(t["out"], x[:]).then_inc(stored, 16)
            sp.wait_ge(stored, 16)

        @block.gpsimd
        def _(pool):
            c = Counts()
            pool.sem_inc(w_rest, RING)
            pool.memset(ident[:], 0.0).then_inc(pool_made, 1)
            pool.wait_ge(pool_made, 1)
            pool.affine_select(out=ident[:], in_=ident[:], compare_op=ALU.not_equal, fill=1.0, base=0,
                               pattern=[[-1, P]], channel_multiplier=1).then_inc(pool_made, 1)
            for kind, i in PHASES:
                if kind == "ffn":
                    ffn_pool(pool, c, i)
                elif kind == "even":
                    even_pool(pool, c)
                elif kind == "odd":
                    odd_pool(pool, c)
                elif kind == "mix2":
                    mix2_pool(pool, c)
                else:
                    ffn2_pool(pool, c)
                end(kind, c)

        @block.tensor
        def _(pe):
            c = Counts()
            pe.sem_inc(blocks_done, RING)
            pe.wait_ge(pool_made, 2)
            pe.wait_ge(dve_made, 6)
            for kind, i in PHASES:
                pre_pe(pe, c)
                pre_end(c)
                if kind == "ffn":
                    ffn_pe(pe, c, i)
                elif kind == "even":
                    even_pe(pe, c)
                elif kind == "odd":
                    odd_pe(pe, c)
                elif kind == "mix2":
                    mix2_pe(pe, c)
                else:
                    ffn2_pe(pe, c)
                end(kind, c)
                post_pe(pe, c)
                post_end(c)

        @block.scalar
        def _(act):
            c = Counts()
            for g in range(AHEAD):
                round_block(act, g, g, 0, widths[g])
            for kind, i in PHASES:
                pre_act(act, c)
                pre_end(c)
                if kind == "ffn":
                    ffn_act(act, c, i)
                elif kind == "even":
                    even_act(act, c)
                elif kind == "odd":
                    odd_act(act, c)
                elif kind == "mix2":
                    mix2_act(act, c, i)
                else:
                    ffn2_act(act, c)
                end(kind, c)
                post_act(act, c)
                post_end(c)

        @block.vector
        def _(dve):
            c = Counts()
            ch = Chain(dve, dve_step)
            dve.sem_inc(acc_drained, ACCS)
            dve.sem_inc(hl_done, 2)
            dve.sem_inc(sum_used, 2)
            for n, width in enumerate((D, CONV_T * P, QR * P, KR * P)):
                dve.memset(meancol[:, n:n + 1], 1.0 / width).then_inc(dve_made, 1)
            ch.link(dve.memset(meancol[:, 4:6], 0.0))
            dve.memset(meancol[0:HD, 4:5], 1.0 / HD).then_inc(dve_made, 1)
            dve.memset(meancol[HD:P, 5:6], 1.0 / HD).then_inc(dve_made, 1)
            dve.wait_ge(gains_loaded, 16)
            for r in (1, 5, 7, 11):
                ch.link(dve.tensor_scalar(gains[:, r, :], gains[:, r, :], 0.5, None, ALU.mult))
            rows = {("ffn", 0): 0, ("even", 0): 2, ("ffn", 1): 4, ("ffn", 2): 6, ("odd", 0): 8, ("ffn", 3): 10,
                    ("mix2", 0): 12, ("ffn2", 0): 14, ("mix2", 1): 16, ("ffn2", 1): 18}
            for kind, i in PHASES:
                pre_dve(dve, ch, c, rows[kind, i])
                pre_end(c)
                if kind == "ffn":
                    ffn_dve(dve, ch, c, i)
                elif kind == "even":
                    even_dve(dve, ch, c)
                elif kind == "odd":
                    odd_dve(dve, ch, c)
                elif kind == "mix2":
                    mix2_dve(dve, ch, c)
                else:
                    ffn2_dve(dve, ch, c)
                end(kind, c)
                post_dve(dve, ch, c, rows[kind, i] + 1, {"odd": o_y, "ffn2": y_b}.get(kind, y))
                post_end(c)


def tiles_of(w):
    K, N = w.shape
    return np.ascontiguousarray(w.reshape(K // P, P, N // P, P).transpose(2, 1, 0, 3).reshape(N // P, P, K))


def columns(v):
    return v.reshape(-1, P).T


def even_table():
    f = np.float32
    inv = (f(1.0) / (f(10000.0) ** (np.arange(0, HD, 2, dtype=f) / f(HD)))).astype(f)
    ang = (inv[np.arange(P) % 32][:, None] * np.arange(S, dtype=f)[None]).astype(f)
    q, j = np.arange(P)[:, None], np.arange(P)[None]
    mask = np.concatenate([np.where(j >= q, 0, NEG), np.zeros((P, P)), np.where(j <= q, 0, NEG)], 1)
    s = np.arange(S)
    inv_count = np.stack([1.0 / (np.clip(s + w - w // 2, 0, S) - np.clip(s - w // 2, 0, S)) for w in (2, 4, 8, 16)])
    pool = np.concatenate([np.repeat(inv_count[0:2], HD, 0), np.repeat(inv_count[2:4], HD, 0)], 1)
    return np.concatenate([np.cos(ang), np.sin(ang), mask, pool, rotation(P, HD)], 1).astype(f)


def rotation(n, width, first=0):
    r = np.zeros((n, n), np.float32)
    for p in range(first, n):
        low = (p - first) % width < width // 2
        r[p + (width // 2 if low else -width // 2), p] = -1 if low else 1
    return r


def second_table():
    f = np.float32
    row, col = np.repeat(np.arange(S // 64), 64).astype(f), np.tile(np.arange(64), S // 64).astype(f)

    def angles(dim):
        half = dim // 2
        inv = (f(10000.0) ** (-np.arange(0, half, 2, dtype=f) / f(half))).astype(f)
        r, c = row[:, None] * inv, col[:, None] * inv
        return np.concatenate([r, r, c, c], 1).T.astype(f)
    a, b = np.tile(angles(HD), (2, 1)), angles(32)
    pad = np.zeros((QK - HD, S), f)
    cos_b = np.concatenate([np.ones((HD, S)), np.cos(b), pad])
    sin_b = np.concatenate([np.zeros((HD, S)), np.sin(b), pad])
    rot_b = np.zeros((P, P), f)
    rot_b[:QK, :QK] = rotation(QK, 16, HD)
    return np.concatenate([np.cos(a), np.sin(a), cos_b, sin_b, rotation(P, 32), rot_b], 1).astype(f)


def lay_out(a):
    r = {}
    r["x"] = np.ascontiguousarray(a["x"][0].T.reshape(KD, P, S).transpose(1, 0, 2))
    gate, up, down = a["ffn_w_gate"], a["ffn_w_up"], a["ffn_w_down"]
    r["ffn_up"] = np.stack([np.stack([tiles_of(gate[l, i]), tiles_of(up[l, i])], 1).reshape(2 * NF, P, D)
                            for l in range(2) for i in range(2)])
    r["ffn_down"] = np.stack([tiles_of(down[l, i]) for l in range(2) for i in range(2)])
    g = [a["norm_w"].reshape(12, D)] + [a[n][l:l + 1] for l in range(2)
                                        for n in ("pre_mix_g_2", "post_mix_g_2", "pre_ffn_g_2", "post_ffn_g_2")]
    r["gains"] = np.ascontiguousarray(np.concatenate(g).reshape(20, KD, P).transpose(2, 0, 1))

    w = a["ev_w_in"][0]
    qw, kw = Q_HEADS * HD, KV_HEADS * HD
    q0, k0, v0 = POOL_W, POOL_W + qw, POOL_W + qw + kw
    q_cols = np.concatenate([np.arange(HD) + HD * head for pair in EVEN_PAIRS for head in pair])
    r["ev_in"] = tiles_of(np.concatenate([w[:, :q0], w[:, k0:v0], w[:, q0 + q_cols], w[:, v0:]], 1))
    w = a["ev_w_out"][0]
    r["ev_out"] = tiles_of(np.concatenate([w[:POOL_W], w[POOL_W + q_cols]]))
    wg = np.zeros((P, 2, P), np.float32)
    for g in range(4):
        half = slice(g % 2 * HD, g % 2 * HD + HD)
        wg[half, g // 2, half] = a["ev_pool_w"][0, g]
    r["ev_wg"] = wg
    r["ev_small"] = np.ascontiguousarray(np.concatenate(
        [columns(a["ev_pool_scale"][0]), np.broadcast_to(a["ev_sink"][0], (P, Q_HEADS))], 1))
    r["tab_even"] = even_table()

    w = a["od_w_in"][0]
    cc = CONV_T * P
    pairs = np.concatenate([np.arange(P) + P * i + cc * j for i in range(CONV_T) for j in range(2)])
    z0, x0, d0 = 2 * cc, 2 * cc + D, 2 * cc + D + D + 2 * SG * SN
    r["od_in"] = tiles_of(np.concatenate([w[:, pairs], w[:, x0:d0], w[:, d0:], np.zeros((D, P - 2 * SH), np.float32),
                                          w[:, z0:x0]], 1))
    r["od_out"] = tiles_of(a["od_w_out"][0])
    steps = np.zeros((P, 2), np.float32)
    steps[:2 * SH, 0] = a["ssm_dt_bias"][0].reshape(-1)
    steps[:2 * SH, 1] = a["ssm_A_log"][0].reshape(-1)
    r["od_small"] = np.ascontiguousarray(np.concatenate([
        a["cv_dw_w"][0].reshape(CONV_K, CONV_T, P).transpose(2, 1, 0).reshape(P, -1), columns(a["cv_dw_b"][0]),
        columns(a["cv_ln_g"][0]), columns(a["cv_ln_b"][0]),
        a["ssm_conv_w"][0].reshape(SSM_K, 16, P).transpose(2, 1, 0).reshape(P, -1), columns(a["ssm_conv_b"][0]),
        columns(np.repeat(a["ssm_D"][0], HD)), columns(a["ssm_norm_w"][0]), steps], 1))
    s, l = np.arange(P)[:, None], np.arange(P)[None]
    back = (np.arange(P) >= SH)[:, None]
    r["tab_odd"] = np.concatenate([np.where(back, -1, 1), back, np.where(l >= s, 0, NEG), np.where(l <= s, 0, NEG)],
                                  1).astype(np.float32)

    a_cols = np.concatenate([np.arange(HD) + HD * head for j in range(4) for head in (j, j + 4)])
    ins, ups, kvs, gates, outs, smalls, fup, fdown = ([] for _ in range(8))
    for i in range(2):
        w = a["w_in_2"][i]
        kr = np.zeros((D, P), np.float32)
        kr[:, HD:QK] = w[:, 1408:1440]
        ins.append(tiles_of(np.concatenate([w[:, a_cols], w[:, 512:640], w[:, 768:1408], kr, w[:, 640:768]], 1)))
        ups.append(a["w_q_up_2"][i].reshape(QR, P, 8, QK).transpose(1, 2, 0, 3).reshape(P, -1))
        kv = a["w_kv_up_2"][i].reshape(KR * P, 8, 2, HD)
        kvs.append(np.stack([tiles_of(np.ascontiguousarray(kv[:, :, j]).reshape(KR * P, 8 * HD))
                             .transpose(1, 0, 2).reshape(P, -1) for j in range(2)]))
        ga, gb = tiles_of(w[:, 1440:1440 + D]), tiles_of(w[:, 1440 + D:])
        br = np.concatenate([tiles_of(a["w_branch_a_2"][i][a_cols]), tiles_of(a["w_branch_b_2"][i])], 2)
        gates.append(np.stack([ga, gb, br], 1).reshape(3 * KD, P, D))
        outs.append(tiles_of(a["w_o_2"][i]))
        smalls.append(np.concatenate([np.tile(a["q_norm_g_2"][i], 2)[:, None], np.tile(a["k_norm_g_2"][i], 2)[:, None],
                                      columns(a["q_a_norm_g_2"][i]), columns(a["kv_a_norm_g_2"][i]),
                                      np.zeros((P, 1), np.float32), columns(a["b_gate_2"][i])], 1))
        fup.append(tiles_of(a["w_ffn_up_2"][i]).reshape(2, NH, P, D))
        fdown.append(np.stack([tiles_of(part).reshape(KD, P, 2, D).transpose(0, 2, 1, 3).reshape(2 * KD, P, D)
                               for part in np.split(a["w_ffn_down_2"][i], 2)]))
    for name, parts in (("b_in", ins), ("b_up", ups), ("b_kv", kvs), ("b_gates", gates), ("b_out", outs),
                        ("b_small", smalls), ("b_ffn_up", fup), ("b_ffn_down", fdown)):
        r[name] = np.ascontiguousarray(np.stack(parts))
    r["tab_b"] = second_table()
    return {n: np.ascontiguousarray(v) for n, v in r.items()}


def kernel(**inputs):
    import concourse.bacc as bacc
    from concourse.bass_utils import run_bass_kernel_spmd

    nc = bacc.Bacc("TRN2", target_bir_lowering=False, num_devices=1)
    arrays = lay_out({k: np.asarray(v) for k, v in inputs.items()})
    t = {n: nc.dram_tensor(f"in_{n}", a.shape, F32, kind="ExternalInput").ap() for n, a in arrays.items()}
    t["out"] = nc.dram_tensor("out_x", (P, KD, S), F32, kind="ExternalOutput").ap()
    build(nc, t)
    got = run_bass_kernel_spmd(nc, [{f"in_{n}": a for n, a in arrays.items()}], core_ids=[0])
    return np.ascontiguousarray(got.results[0]["out_x"].transpose(1, 0, 2).reshape(D, S).T)[None]
```

```python
from contextlib import ExitStack

import concourse.bass as bass
import numpy as np
from concourse import mybir

P = 128
S = 512
D = 1024
KD = D // P
F = 2816
NF = F // P
EPS = 1e-6
RING = 4
AHEAD = 3
PIECES = 4
OPEN = 3
DOWN = (8, 8, 6)
ACCS = 4
STAT, SPREAD = 4, 5
SCORES, TURNED, HEADS = 4, 6, 7
F2 = 4096
NH = F2 // 2 // P
HD = 64
NEG = -1e30

POOL_W, Q_HEADS, KV_HEADS = 256, 12, 4
EVEN_PAIRS = [(0, 3), (1, 4), (2, 5), (6, 9), (7, 10), (8, 11)]
EVEN_ORDER = [("lin", 0), ("lin", 1), ("lin", 2), ("lin", 3), ("rot", 2)]
for _i in range(4, 10):
    EVEN_ORDER += [("lin", _i)] + ([("grp", _i - 5)] if _i in (5, 6) else []) + [("rot", _i - 1)]
EVEN_ORDER += [("val", 0), ("rot", 9), ("val", 1)]

CONV_K, CONV_T = 31, 4
SSM_K = 4
SH, SG, SN = 16, 4, 128
ODD_LINS = 2 * CONV_T + 16 + 1 + 8
LOG_TERMS = 7

QR, KR = 3, 2
RAWS = 5
QK = 96

ALU = mybir.AluOpType
ACT = mybir.ActivationFunctionType
F32 = mybir.dt.float32
F32R = mybir.dt.float32r


class Counts:

    def __init__(self):
        self.blocks = 0
        self.tiles = 0
        self.hidden = 0
        self.sums = 0
        self.squares = 0
        self.norms = 0
        self.xr = 0
        self.xn = 0
        self.units = 0
        self.heads = 0
        self.marks = {}

    def at(self, name):
        return self.marks.get(name, 0)

    def copy(self):
        k = Counts()
        k.blocks, k.tiles, k.hidden, k.sums, k.squares = self.blocks, self.tiles, self.hidden, self.sums, self.squares
        k.norms, k.xr, k.xn, k.units, k.heads = self.norms, self.xr, self.xn, self.units, self.heads
        k.marks = dict(self.marks)
        return k

    def add(self, name, n):
        self.marks[name] = self.at(name) + n


class Chain:

    def __init__(self, eng, sem):
        self.eng, self.sem, self.n = eng, sem, 0

    def step(self, ins):
        self.n += 1
        ins.then_inc(self.sem, 1)
        return self.n

    def link(self, ins):
        self.eng.wait_ge(self.sem, self.step(ins))


def build(nc, t, stop=99):
    with ExitStack() as ctx:
        def sb(name, shape, dt=F32):
            return ctx.enter_context(nc.sbuf_tensor(name, shape, dt))

        def sem(name):
            return ctx.enter_context(nc.semaphore(name))

        def over(under, *tensors):
            with ExitStack() as same:
                return [same.enter_context(nc.sbuf_tensor(name, shape, dt)) for name, shape, dt in tensors]

        x = sb("x", [P, KD, S])
        y, = over("xh", ("y", [P, KD, S], F32))
        o_xf, o_xb = over("xh, xl", ("o_xf", [P, 4, D], F32), ("o_xb", [P, 4, D], F32))
        xh = sb("xh", [P, KD, S], F32R)
        xl = sb("xl", [P, KD, S], F32R)
        w_raw = sb("w_raw", [P, RING, 1024])
        w_hi = sb("w_hi", [P, RING, 1024], F32R)
        w_lo = sb("w_lo", [P, RING, 1024], F32R)
        ident = sb("ident", [P, P])
        meancol = sb("meancol", [P, 6])
        gains = sb("gains", [P, 20, KD])
        stat = sb("stat", [P, 2, 48])
        red = sb("red", [P, 3, 8])
        sq = sb("sq", [P, 2, S])
        sqsum = sb("sqsum", [P, S])
        tmp = sb("tmp", [P, 2, S])
        work = sb("work", [P, 6, S])
        factor = sqsum[:]
        sig, h = work[:, 0:2, :], work[:, 2:4, :]
        pbuf, ptb, raw = work[:, 0:4, :], tmp, work[:, 4:6, :]
        o_e = work[:].rearrange("p a b -> p (a b)")[:, 0:1920].rearrange("p (a b) -> p a b", a=3)

        BF16 = mybir.dt.bfloat16
        e_tab, e_wg, e_small, e_nsink, e_pw, e_u, e_a, e_qk, e_v, m_hi, m_lo = over(
            "hh", ("e_tab", [P, 2560], F32), ("e_wg", [P, 2, P], F32), ("e_small", [P, 14], F32),
            ("e_nsink", [P, 12], F32), ("e_pw", [P, 2, S], F32), ("e_u", [P, 2, S + 16], F32),
            ("e_a", [P, 2, S + 16], F32), ("e_qk", [P, 8, S], F32), ("e_v", [P, 2, S], F32),
            ("m_hi", [P, KD, S], F32R), ("m_lo", [P, KD, S], F32R))
        odd_fixed = [("o_tab", [P, 2 + 2 * P], F32), ("o_small", [P, 234], F32), ("o_a", [32, 2], F32),
                     ("o_r", [32, S], F32), ("o_dt", [P, 4, 32], F32), ("o_nr", [P, 4, 32], F32),
                     ("o_mask", [P, 2, P], BF16), ("identb", [P, P], BF16), ("o_r3", [96, S], BF16), ("o_part", [32, S], BF16),
                     ("o_pick", [96, 32], BF16), ("o_x", [P, KD, S], F32), ("o_b", [P, SG, S], F32),
                     ("o_c", [P, SG, S], F32)]
        o_tab, o_small, o_a, o_r, o_dt, o_nr, o_mask, identb, o_r3, o_part, o_pick, o_x, o_b, o_c, g_hi, g_lo, o_z, o_g, o_cv = over(
            "hh", *odd_fixed, ("g_hi", [P, CONV_T, S], F32R), ("g_lo", [P, CONV_T, S], F32R),
            ("o_z", [P, KD, S], F32), ("o_g", [P, CONV_T, S], F32), ("o_cv", [P, CONV_T, S], F32))
        o_cb, o_y = over("hh", *[(n + "_", s, d) for n, s, d in odd_fixed], ("o_cb", [P, 2, 4, S], F32),
                         ("o_y", [P, KD, S], F32))[-2:]
        o_sum, o_product = work[:, 4, :], work[:, 4:6, :]
        tab2 = [("b_tab", [P, 4 * S + 2 * P], F32), ("b_small", [P, 24], F32)]
        head2 = [("c_hi", [P, QR + KR, S], F32R), ("c_lo", [P, QR + KR, S], F32R)]
        mid2 = [("b_qk", [P, RAWS, S], F32), ("b_va", [P, S], F32), ("krot", [P, S], F32), ("gap2", [P, S], F32)]
        b_tab, b_small, c_hi, c_lo, b_qk, b_va, krot, _, b_q, b_k, b_vb = over(
            "hh", *tab2, *head2, *mid2, ("b_q", [P, 8, S], F32), ("b_k", [P, 8, S], F32), ("b_vb", [P, 4, S], F32))
        (ya_hi, ya_lo, _, yb_hi, yb_lo, mm_hi, mm_lo) = over(
            "hh", *[(n + "_", s, d) for n, s, d in tab2], ("ya_hi", [P, 4, S], F32R), ("ya_lo", [P, 4, S], F32R),
            ("gap3", [P, 2, S], F32), ("yb_hi", [P, 4, S], F32R), ("yb_lo", [P, 4, S], F32R),
            ("mm_hi", [P, KD, S], F32R), ("mm_lo", [P, KD, S], F32R))[2:]
        c_raw = over("hh", *[(n + "__", s, d) for n, s, d in tab2 + head2 + mid2], ("c_raw", [P, QR + KR, S], F32))[-1]
        hh2, hl2, y_b = over("hh", ("hh2", [P, NH, S], F32R), ("hl2", [P, NH, S], F32R), ("y_b", [P, KD, S], F32))
        hh = sb("hh", [P, NF, S], F32R)
        hl = sb("hl", [P, NF, S], F32R)
        bank = [ctx.enter_context(nc.psum_tensor(f"bank{i}", [P, S], F32)) for i in range(8)]

        gains_loaded, x_loaded = sem("gains_loaded"), [sem(f"x_loaded{i}") for i in range(PIECES)]
        pool_made, dve_made = sem("pool_made"), sem("dve_made")
        w_loaded = [sem(f"w_loaded{i}") for i in range(RING)]
        w_rounded, w_rest = sem("w_rounded"), sem("w_rest")
        blocks_done, acc_drained = sem("blocks_done"), sem("acc_drained")
        silu_done, hh_done, hl_done = sem("silu_done"), sem("hh_done"), sem("hl_done")
        y_squared, sum_used = sem("y_squared"), sem("sum_used")
        dve_step = sem("dve_step")
        x_ready, x_squared = sem("x_ready"), sem("x_squared")
        squares_added = sem("squares_added")
        squares_summed, std_ready = sem("squares_summed"), sem("std_ready")
        h_ready = sem("h_ready")
        rstd_ready, spread_ready = sem("rstd_ready"), sem("spread_ready")
        xn_ready, xh_ready, xl_ready = sem("xn_ready"), sem("xh_ready"), sem("xl_ready")
        stored = sem("stored")
        side_done, raw_copied, rotated = sem("side_done"), sem("raw_copied"), sem("rotated")
        tables_loaded, odd_loaded = sem("tables_loaded"), sem("odd_loaded")
        pooled, pool_rounded, pool_split = sem("pooled"), sem("pool_rounded"), sem("pool_split")
        scores_ready, rowmax_ready, probs_ready = sem("scores_ready"), sem("rowmax_ready"), sem("probs_ready")
        probs_scaled, probs_turned, turned_copied = sem("probs_scaled"), sem("probs_turned"), sem("turned_copied")
        attended, head_rounded, head_split = sem("attended"), sem("head_rounded"), sem("head_split")
        a_ready, glu_done, xbc_done, z_done = sem("a_ready"), sem("glu_done"), sem("xbc_done"), sem("z_done")
        xbc_convolved, conv_tap, conv_added, conv_product = (
            sem(n) for n in ("xbc_convolved", "conv_tap", "conv_added", "conv_product"))
        dt_arg, dt_exp, steps_ready = sem("dt_arg"), sem("dt_exp"), sem("steps_ready")
        centered, normed, g_silu, g_rounded, g_split = (sem(n) for n in ("centered", "normed", "g_silu", "g_rounded", "g_split"))
        scaled_in, cb_summed, cb_copied = sem("scaled_in"), sem("cb_summed"), sem("cb_copied")
        decays_spread, exps_ready, weighted = sem("decays_spread"), sem("exps_ready"), sem("weighted")
        scanned, pair_read, gated = sem("scanned"), sem("pair_read"), sem("gated")
        up_done, kr_copied, rstd2_ready, cn_ready = sem("up_done"), sem("kr_copied"), sem("rstd2_ready"), sem("cn_ready")
        gate_ready, merged, merged_rounded, merged_split = (sem(n) for n in ("gate_ready", "merged", "merged_rounded", "merged_split"))
        block = ctx.enter_context(nc.Block())

        def raw_free(g):
            return g + 1

        def rest_done(g):
            return RING + g + 1

        def slot_free(g):
            return g + 1

        def block_done(g):
            return RING + g + 1

        def acc_free(n):
            return n + 1

        def drained(n):
            return ACCS + n + 1

        widths = []

        def load(sp, g, slot, src):
            sp.wait_ge(w_rest, raw_free(g))
            sp.dma_start(w_raw[:, slot, 0:src.shape[1]], src).then_inc(w_loaded[slot], 16)

        def round_block(act, g, slot, turn, width):
            act.wait_ge(w_loaded[slot], (turn + 1) * 16)
            act.wait_ge(blocks_done, slot_free(g))
            act.activation(w_hi[:, slot, 0:width], w_raw[:, slot, 0:width], ACT.Copy).then_inc(w_rounded, 1)

        def round_ahead(act, g):
            g += AHEAD
            if g < len(widths):
                round_block(act, g, g % RING, g // RING, widths[g])

        def rest_block(pool, g, slot, width):
            pool.wait_ge(w_rounded, g + 1)
            pool.tensor_tensor(w_lo[:, slot, 0:width], w_raw[:, slot, 0:width],
                               w_hi[:, slot, 0:width].bitcast(F32), ALU.subtract).then_inc(w_rest, 1)

        def products(pe, out, slot, hi, lo, first, last):
            for k in range(len(hi)):
                wh, wl = w_hi[:, slot, k * P:(k + 1) * P], w_lo[:, slot, k * P:(k + 1) * P]
                pe.matmul(out, wh, hi[k], start=first and k == 0, stop=False)
                pe.matmul(out, wh, lo[k], start=False, stop=False)
                mm = pe.matmul(out, wl, hi[k], start=False, stop=last and k == len(hi) - 1)
            mm.then_inc(blocks_done, 1)

        def sum_squares(pe, src, first, mean=0, to=STAT):
            for n in range(4):
                mm = pe.matmul(bank[to][:, n:n + 1], src[:, n * P:(n + 1) * P], meancol[:, mean:mean + 1],
                               start=first and n == 0, stop=True, skip_group_check=True)
            mm.then_inc(squares_summed, 1)

        def spread(pe, c, to=SPREAD):
            pe.wait_ge(rstd_ready, c.norms + 1)
            for n in range(4):
                mm = pe.matmul(bank[to][:, n * P:(n + 1) * P], stat[:, 1, n:n + 1].to_broadcast([P, P]),
                               ident[:], start=True, stop=True)
            mm.then_inc(spread_ready, 1)

        def std(act, c, n, source=STAT):
            act.wait_ge(squares_summed, c.squares + n)
            act.activation(stat[:, 0, 0:4], bank[source][:, 0:4], ACT.Sqrt, bias=EPS).then_inc(std_ready, 1)

        def rstd(dve, c):
            dve.wait_ge(std_ready, c.at("std") + 1)
            dve.reciprocal(stat[:, 1, 0:4], stat[:, 0, 0:4]).then_inc(rstd_ready, 1)
            dve.wait_ge(spread_ready, c.norms + 1)

        def post_pe(pe, c):
            pe.wait_ge(sum_used, 2 + c.sums)
            sum_squares(pe, sqsum, True)
            pe.wait_ge(y_squared, c.at("ysq"))
            sum_squares(pe, sq[:, 1, :], False)
            spread(pe, c)

        def post_act(act, c):
            std(act, c, 2)

        def post_dve(dve, c):
            rstd(dve, c)

        def post_end(c):
            c.norms += 1
            c.add("std", 1)
            c.squares += 2
            c.xr += KD

        def grow_dve(dve, ch, c, gain, y, low):
            at = {}

            def scaled(k):
                if k >= 2:
                    dve.wait_ge(x_ready, c.xr - KD + k - 1)
                at[k] = ch.step(dve.scalar_tensor_tensor(
                    out=tmp[:, k % 2, :], in0=y[:, k, :], scalar=gains[:, gain, k:k + 1],
                    in1=bank[SPREAD][:], op0=ALU.mult, op1=ALU.mult))
            scaled(0)
            for k in range(KD):
                dve.wait_ge(dve_step, at[k])
                dve.tensor_tensor(x[:, k, :], x[:, k, :], tmp[:, k % 2, :], ALU.add).then_inc(x_ready, 1)
                if k + 1 < KD:
                    scaled(k + 1)
                low(k)

        def pre_dve(dve, ch, c, gain, prev):
            def low(k):
                dve.wait_ge(xh_ready, c.xn + k + 1)
                dve.scalar_tensor_tensor(out=xl[:, k, :], in0=x[:, k, :], scalar=gains[:, gain, k:k + 1],
                                         in1=xh[:, k, :].bitcast(F32), op0=ALU.mult, op1=ALU.subtract)\
                   .then_inc(xl_ready, 1)
            if prev is None:
                for k in range(KD):
                    low(k)
            else:
                grow_dve(dve, ch, c, prev[0], prev[1], low)
            rstd(dve, c)
            ch.link(dve.tensor_copy(factor, bank[SPREAD][:]))

        def pre_act(act, c, gain):
            if c.xr == 0:
                act.wait_ge(gains_loaded, 16)
            else:
                act.wait_ge(sum_used, 2 + c.sums)
            for k in range(KD):
                if k == (0 if c.xr else 2):
                    round_ahead(act, c.blocks)
                if c.xr:
                    act.wait_ge(x_ready, c.xr - KD + k + 1)
                elif k % (KD // PIECES) == 0:
                    act.wait_ge(x_loaded[k // (KD // PIECES)], 16)
                act.activation(xh[:, k, :], x[:, k, :], ACT.Copy, scale=gains[:, gain, k:k + 1]).then_inc(xh_ready, 1)
                square(act, c, k, x)
            std(act, c, 1)

        def square(act, c, k, src):
            if k >= 2:
                act.wait_ge(squares_added, c.at("added") + max(1, k - 2))
            act.activation(sq[:, k % 2, :], src[:, k, :], ACT.Square).then_inc(x_squared, 1)

        def add_squares(pool, c, n=KD):
            for k in range(1, n):
                pool.wait_ge(x_squared, c.at("sq") + k + 1)
                if k >= 2:
                    pool.wait_ge(squares_added, c.at("added") + k - 1)
                pool.tensor_tensor(sqsum[:], sq[:, 0, :] if k == 1 else sqsum[:], sq[:, k % 2, :], ALU.add)\
                    .then_inc(squares_added, 1)

        def pre_pool(pool, c):
            for j in range(RING):
                rest_block(pool, c.blocks + j, (c.blocks + j) % RING, 1024)
            add_squares(pool, c)

        def part(pe, out, slot, k, hi, lo, first, last):
            wh, wl = w_hi[:, slot, k * P:(k + 1) * P], w_lo[:, slot, k * P:(k + 1) * P]
            pe.matmul(out, wh, hi, start=first, stop=False)
            pe.matmul(out, wh, lo, start=False, stop=False)
            return pe.matmul(out, wl, hi, start=False, stop=last)

        def pre_pe(pe, c):
            B, T = c.blocks, c.tiles
            for j in range(OPEN):
                pe.wait_ge(acc_drained, acc_free(T + j))
            pe.wait_ge(w_rest, rest_done(B + OPEN - 1))
            for k in range(KD):
                pe.wait_ge(xl_ready, c.xn + k + 1)
                for j in range(OPEN):
                    mm = part(pe, bank[(T + j) % ACCS][:], (B + j) % RING, k, xh[:, k, :], xl[:, k, :], k == 0, k == KD - 1)
                    if k == KD - 1:
                        mm.then_inc(blocks_done, 1)
            pe.wait_ge(squares_added, c.at("added") + KD - 1)
            sum_squares(pe, sqsum, True)
            pe.wait_ge(acc_drained, acc_free(T + OPEN))
            pe.wait_ge(w_rest, rest_done(B + OPEN))
            for k in range(KD):
                if k == KD // 2:
                    spread(pe, c)
                mm = part(pe, bank[(T + OPEN) % ACCS][:], (B + OPEN) % RING, k, xh[:, k, :], xl[:, k, :], k == 0, k == KD - 1)
            mm.then_inc(blocks_done, 1)

        def pre_end(c):
            c.norms += 1
            c.add("std", 1)
            c.add("sq", KD)
            c.add("added", KD - 1)
            c.squares += 1
            c.xn += KD

        def norm_dve(dve, c, src, gain):
            rstd(dve, c)

            def scaled(k):
                if k >= 2:
                    dve.wait_ge(xl_ready, c.xn + k - 1)
                dve.scalar_tensor_tensor(
                    out=tmp[:, k % 2, :], in0=src[:, k, :], scalar=gain(k),
                    in1=bank[SPREAD][:], op0=ALU.mult, op1=ALU.mult).then_inc(xn_ready, 1)
            scaled(0)
            for k in range(KD):
                if k + 1 < KD:
                    scaled(k + 1)
                dve.wait_ge(xh_ready, c.xn + k + 1)
                dve.tensor_tensor(xl[:, k, :], tmp[:, k % 2, :], xh[:, k, :].bitcast(F32), ALU.subtract)\
                   .then_inc(xl_ready, 1)
            dve.wait_ge(xl_ready, c.xn + KD)

        def norm_end(c):
            pre_end(c)
            c.add("xnr", KD)

        def y_act(act, c, m, y):
            act.wait_ge(sum_used, c.sums + m + 1)
            if m == KD - 1:
                load_sqrt(act)
            act.wait_ge(acc_drained, drained(c.tiles + m))
            act.activation(sq[:, m % 2, :], y[:, m, :], ACT.Square).then_inc(y_squared, 1)

        def load_sqrt(act):
            act.activation(red[:, 0, 7:8], meancol[:, 0:1], ACT.Sqrt)

        def y_dve(dve, c, m, blk):
            dve.wait_ge(blocks_done, block_done(blk))
            dve.tensor_copy(y[:, m, :], bank[(c.tiles + m) % ACCS][:]).then_inc(acc_drained, 1)

        def y_sum(dve, c, m):
            if m < KD - 1:
                dve.wait_ge(y_squared, c.at("ysq") + m + 1)
                dve.wait_ge(sum_used, 2 + c.sums + m)
                dve.tensor_tensor(sqsum[:], sqsum[:], sq[:, m % 2, :], ALU.add).then_inc(sum_used, 1)

        def ffn_sp(sp, c, i):
            B = c.blocks
            with sp.Fori(0, NF // 2) as it:
                for j in range(4):
                    load(sp, it * 4 + (B + j), (B + j) % RING, t["ffn_up"][i, it * 4 + j])
            B += 2 * NF
            with sp.Fori(0, 2) as it:
                for m in range(4):
                    for b, nk in enumerate(DOWN):
                        j = 3 * m + b
                        load(sp, it * 12 + (B + j), (B + j) % RING,
                             t["ffn_down"][i, it * 4 + m][:, b * 1024:b * 1024 + nk * P])

        def ffn_pool(pool, c, i):
            B = c.blocks
            with pool.Fori(1, NF // 2) as it:
                for j in range(4):
                    rest_block(pool, it * 4 + (B + j), (B + j) % RING, 1024)
            B += 2 * NF
            with pool.Fori(0, 2) as it:
                for j in range(12):
                    rest_block(pool, it * 12 + (B + j), (B + j) % RING, DOWN[j % 3] * P)

        def ffn_pe(pe, c, i):
            B, T = c.blocks, c.tiles
            with pe.Fori(1, NF // 2) as it:
                for j in range(4):
                    pe.wait_ge(acc_drained, it * 4 + acc_free(T + j))
                    pe.wait_ge(w_rest, it * 4 + rest_done(B + j))
                    products(pe, bank[(T + j) % ACCS][:], (B + j) % RING,
                             [xh[:, k, :] for k in range(KD)], [xl[:, k, :] for k in range(KD)], True, True)
            B += 2 * NF
            T += 2 * NF
            with pe.Fori(0, 2) as it:
                for m in range(4):
                    pe.wait_ge(acc_drained, it * 4 + acc_free(T + m))
                    for b, nk in enumerate(DOWN):
                        j = 3 * m + b
                        pe.wait_ge(w_rest, it * 12 + rest_done(B + j))
                        pe.wait_ge(hl_done, 2 + c.hidden + 8 * b + nk)
                        products(pe, bank[(T + m) % ACCS][:], (B + j) % RING,
                                 [hh[:, 8 * b + k, :] for k in range(nk)], [hl[:, 8 * b + k, :] for k in range(nk)],
                                 b == 0, b == 2)

        def ffn_act(act, c, i):
            B, T, H = c.blocks, c.tiles, c.hidden

            def two(it, first):
                for n in range(2):
                    for j in (2 * n, 2 * n + 1):
                        g = B + j + AHEAD
                        if j or not first:
                            round_block(act, it * 4 + g, g % RING, it + g // RING, 1024)
                    act.wait_ge(acc_drained, it * 4 + drained(T + 2 * n))
                    act.activation(sig[:, n, :], sig[:, n, :], ACT.Silu).then_inc(silu_done, 1)
                    act.wait_ge(h_ready, it * 2 + (c.at("h") + n + 1))
                    act.activation(hh[:, it * 2 + n, :], h[:, n, :], ACT.Copy).then_inc(hh_done, 1)
            two(0, True)
            with act.Fori(1, NF // 2) as it:
                two(it, False)
            c.tiles += 2 * NF
            for m in range(KD):
                for b in range(3):
                    round_ahead(act, B + 2 * NF + 3 * m + b)
                y_act(act, c, m, y)
            c.tiles -= 2 * NF

        def ffn_dve(dve, ch, c, i):
            B, T, H = c.blocks, c.tiles, c.hidden
            with dve.Fori(0, NF // 2) as it:
                for n in range(2):
                    dve.wait_ge(blocks_done, it * 4 + block_done(B + 2 * n))
                    dve.wait_ge(hl_done, it * 2 + (H + n + 1))
                    dve.tensor_tensor(sig[:, n, :], bank[(T + 2 * n) % ACCS][:], factor, ALU.mult)\
                       .then_inc(acc_drained, 1)
                    dve.wait_ge(blocks_done, it * 4 + block_done(B + 2 * n + 1))
                    dve.tensor_tensor(h[:, n, :], bank[(T + 2 * n + 1) % ACCS][:], factor, ALU.mult)\
                       .then_inc(acc_drained, 1)
                    dve.wait_ge(silu_done, it * 2 + (c.at("h") + n + 1))
                    dve.wait_ge(acc_drained, it * 4 + drained(T + 2 * n + 1))
                    dve.tensor_tensor(h[:, n, :], h[:, n, :], sig[:, n, :], ALU.mult).then_inc(h_ready, 1)
                    dve.wait_ge(hh_done, it * 2 + (H + n + 1))
                    dve.tensor_tensor(hl[:, it * 2 + n, :], h[:, n, :], hh[:, it * 2 + n, :].bitcast(F32),
                                      ALU.subtract).then_inc(hl_done, 1)
            c.tiles += 2 * NF
            y_begin(dve, ch)
            for m in range(KD):
                y_dve(dve, c, m, B + 2 * NF + 3 * m + 2)
                y_sum(dve, c, m)
            c.tiles -= 2 * NF

        def ffn_end(c):
            c.blocks += 2 * NF + 3 * KD
            c.tiles += 2 * NF + KD
            c.hidden += NF
            c.add("h", NF)
            c.sums += KD - 1
            c.add("ysq", KD)

        def stream_sp(sp, g, arr, n):
            if n >= RING:
                with sp.Fori(0, n // RING) as it:
                    for j in range(RING):
                        load(sp, it * RING + (g + j), (g + j) % RING, arr[it * RING + j])
            for j in range(n // RING * RING, n):
                load(sp, g + j, (g + j) % RING, arr[j])

        def stream_pool(pool, g, n):
            if n >= RING:
                with pool.Fori(0, n // RING) as it:
                    for j in range(RING):
                        rest_block(pool, it * RING + (g + j), (g + j) % RING, 1024)
            for j in range(n // RING * RING, n):
                rest_block(pool, g + j, (g + j) % RING, 1024)

        def xs_of(hi, lo, n, first=0):
            return [hi[:, first + k, :] for k in range(n)], [lo[:, first + k, :] for k in range(n)]

        def take_block(pe, c):
            g = c.blocks
            pe.wait_ge(w_rest, rest_done(g))
            c.blocks += 1
            return g % RING

        def project(pe, c, tile, parts):
            pe.wait_ge(acc_drained, acc_free(tile))
            for b, (hi, lo) in enumerate(parts):
                products(pe, bank[tile % ACCS][:], take_block(pe, c), hi, lo, b == 0, b == len(parts) - 1)

        def project_values(pe, c, tile):
            pe.wait_ge(acc_drained, acc_free(tile))
            slot = take_block(pe, c)
            for n in range(4):
                out, tok = bank[tile % ACCS][:, n * P:(n + 1) * P], slice(n * P, (n + 1) * P)
                for k in range(KD):
                    wh, wl = w_hi[:, slot, k * P:(k + 1) * P], w_lo[:, slot, k * P:(k + 1) * P]
                    pe.matmul(out, xh[:, k, tok], wh, start=k == 0, stop=False)
                    pe.matmul(out, xh[:, k, tok], wl, start=False, stop=False)
                    mm = pe.matmul(out, xl[:, k, tok], wh, start=False, stop=k == KD - 1)
            mm.then_inc(blocks_done, 1)

        def scale_values(dve, out, src):
            dve.tensor_tensor(out.rearrange("p (n v) -> p n v", v=P), src.rearrange("p (n v) -> p n v", v=P),
                              stat[:, 1, 0:4].unsqueeze(2).broadcast_to([P, 4, P]), ALU.mult).then_inc(acc_drained, 1)

        def y_begin(dve, ch):
            ch.link(dve.memset(sqsum[:], 0.0))

        def out_pe(pe, c, parts):
            for m in range(KD):
                project(pe, c, c.tiles + m, parts)

        def out_act(act, c, nblk, g0, y, done=0):
            for m in range(KD):
                for b in range(nblk):
                    if nblk * m + b >= done:
                        round_ahead(act, g0 + nblk * m + b)
                y_act(act, c, m, y)

        def out_dve(dve, ch, c, nblk, g0, y):
            y_begin(dve, ch)
            for m in range(KD):
                dve.wait_ge(blocks_done, block_done(g0 + nblk * m + nblk - 1))
                dve.tensor_copy(y[:, m, :], bank[(c.tiles + m) % ACCS][:]).then_inc(acc_drained, 1)
                y_sum(dve, c, m)

        def out_end(c):
            c.tiles += KD
            c.sums += KD - 1
            c.add("ysq", KD)

        def attend_pe(pe, c, units, fill):
            n = len(units)
            for s in range(n + 4):
                if s in fill:
                    fill[s]()
                if s < n:
                    u, g = units[s], c.units + s
                    if g >= 2:
                        pe.wait_ge(probs_ready, g - 1)
                    pe.matmul(bank[SCORES + g % 2][:, 0:u["keys"]], u["q"], u["k"], start=True, stop=True)\
                      .then_inc(scores_ready, 1)
                if 0 <= s - 3 < n:
                    u, g = units[s - 3], c.units + s - 3
                    pe.wait_ge(probs_scaled, g + 1)
                    if g:
                        pe.wait_ge(turned_copied, g)
                    for j in range(len(u["v"])):
                        mm = pe.transpose(bank[TURNED][:, j * P:(j + 1) * P], pbuf[:, g % 4, j * P:(j + 1) * P],
                                          ident[:])
                    mm.then_inc(probs_turned, 1)
                if 0 <= s - 4 < n:
                    u, g = units[s - 4], c.units + s - 4
                    pe.wait_ge(turned_copied, g + 1)
                    hd = c.heads + (s - 4) // 4
                    if (s - 4) % 4 == 0 and hd >= 2:
                        pe.wait_ge(head_split, hd - 1)
                    for j, v in enumerate(u["v"]):
                        mm = pe.matmul(bank[HEADS][u["half"], u["n"] * P:(u["n"] + 1) * P], v,
                                       ptb[:, g % 2, j * P:(j + 1) * P], start=j == 0, stop=j == len(u["v"]) - 1)
                    mm.then_inc(attended, 1)

        def attend_dve(dve, ch, c, units):
            n = len(units)
            at = {}
            for s in range(n + 7):
                if s < n:
                    u, g = units[s], c.units + s
                    r = red[:, g % 3, :]
                    dve.wait_ge(scores_ready, g + 1)
                    if g >= 4:
                        dve.wait_ge(probs_turned, g - 3)
                    if u["mask"] is not None:
                        ch.link(dve.tensor_tensor_reduce(pbuf[:, g % 4, 0:u["keys"]], bank[SCORES + g % 2][:, 0:u["keys"]],
                                                         u["mask"], 1.0, NEG, ALU.add, ALU.max, r[:, 0:1]))
                        dve.tensor_scalar(r[:, 1:2], r[:, 0:1], -u["scale"], u["nsink"], ALU.mult, ALU.min)\
                           .then_inc(rowmax_ready, 1)
                    else:
                        ch.link(dve.reduce_max(r[:, 0:1], bank[SCORES + g % 2][:, 0:u["keys"]], mybir.AxisListType.X))
                        dve.tensor_scalar(r[:, 1:2], r[:, 0:1], -u["scale"], None, ALU.mult).then_inc(rowmax_ready, 1)
                if 0 <= s - 1 < n:
                    u, g = units[s - 1], c.units + s - 1
                    r = red[:, g % 3, :]
                    dve.wait_ge(probs_ready, g + 1)
                    if u["mask"] is not None:
                        ch.link(dve.tensor_tensor(r[:, 4:5], r[:, 2:3], r[:, 3:4], ALU.add))
                        ch.link(dve.reciprocal(r[:, 5:6], r[:, 4:5]))
                    else:
                        ch.link(dve.reciprocal(r[:, 5:6], r[:, 2:3]))
                    dve.tensor_scalar(pbuf[:, g % 4, 0:u["keys"]], pbuf[:, g % 4, 0:u["keys"]], r[:, 5:6], None,
                                      ALU.mult).then_inc(probs_scaled, 1)
                if s - 6 >= 0 and (s - 6) % 4 == 3 and s - 6 < n:
                    u, hd = units[s - 6], (s - 6) // 4
                    dve.wait_ge(head_rounded, c.heads + hd + 1)
                    dve.tensor_tensor(u["lo"], bank[HEADS][u["half"], :], u["hi"].bitcast(F32), ALU.subtract)\
                       .then_inc(head_split, 1)

        def attend_act(act, c, units):
            n = len(units)
            for s in range(n + 6):
                if 0 <= s - 3 < n:
                    u, g = units[s - 3], c.units + s - 3
                    act.wait_ge(probs_turned, g + 1)
                    if g >= 2:
                        act.wait_ge(attended, g - 1)
                    act.activation(ptb[:, g % 2, 0:u["keys"]], bank[TURNED][:, 0:u["keys"]], ACT.Copy)\
                       .then_inc(turned_copied, 1)
                if s < n:
                    u, g = units[s], c.units + s
                    r = red[:, g % 3, :]
                    act.wait_ge(rowmax_ready, g + 1)
                    if u["mask"] is not None:
                        act.activation(pbuf[:, g % 4, 0:u["keys"]], pbuf[:, g % 4, 0:u["keys"]], ACT.Exp,
                                       bias=r[:, 1:2], scale=u["scale"], accum_out=r[:, 2:3])
                        act.activation(r[:, 3:4], u["sink"], ACT.Exp, bias=r[:, 1:2]).then_inc(probs_ready, 1)
                    else:
                        act.activation(pbuf[:, g % 4, 0:u["keys"]], bank[SCORES + g % 2][:, 0:u["keys"]], ACT.Exp,
                                       bias=r[:, 1:2], scale=u["scale"], accum_out=r[:, 2:3]).then_inc(probs_ready, 1)
                if s - 5 >= 0 and (s - 5) % 4 == 3 and s - 5 < n:
                    u, g = units[s - 5], c.units + s - 5
                    act.wait_ge(attended, g + 1)
                    act.activation(u["hi"], bank[HEADS][u["half"], :], ACT.Copy).then_inc(head_rounded, 1)

        def attend_end(c, units):
            c.units += len(units)
            c.heads += len(units) // 4

        NB = S // P

        def even_units():
            units = []
            for j, pair in enumerate(EVEN_PAIRS):
                for side, head in enumerate(pair):
                    half = slice(side * HD, (side + 1) * HD)
                    keys = head // 3 // 2
                    for n in range(NB):
                        lo, hi = max(n - 1, 0), min(n + 1, NB - 1)
                        width = (hi - lo + 1) * P
                        off = 0 if n else P
                        units.append(dict(
                            q=e_qk[half, 2 + j, n * P:(n + 1) * P], k=e_qk[half, keys, lo * P:(hi + 1) * P],
                            keys=width, scale=HD ** -0.5, mask=e_tab[:, 1024 + off:1024 + off + width], n=n, half=half,
                            sink=e_small[:, 2 + head:3 + head], nsink=e_nsink[:, head:head + 1],
                            v=[e_v[:, keys, m * P + half.start:m * P + half.stop] for m in range(lo, hi + 1)],
                            hi=m_hi[half, 2 + j, :], lo=m_lo[half, 2 + j, :]))
            return units

        def even_sp(sp, c):
            stream_sp(sp, c.blocks, t["ev_in"], 12)
            stream_sp(sp, c.blocks + 12, t["ev_out"], 8)

        def even_pool(pool, c):
            stream_pool(pool, c.blocks + RING, 12 - RING)
            stream_pool(pool, c.blocks + 12, 8)

        def even_end(c):
            c.blocks += 20
            c.tiles += len(EVEN_ORDER)
            c.add("side", 10)
            c.add("raw", 8)
            c.add("rotated", 8)
            attend_end(c, even_units())
            out_end(c)

        def even_pe(pe, c):
            k = Counts()
            k.blocks = c.blocks + OPEN + 1
            for n, (kind, i) in list(enumerate(EVEN_ORDER))[OPEN + 1:]:
                tile = c.tiles + n
                out = bank[tile % ACCS][:]
                if kind == "lin":
                    project(pe, k, tile, [xs_of(xh, xl, KD)])
                elif kind == "val":
                    project_values(pe, k, tile)
                elif kind == "rot":
                    pe.wait_ge(acc_drained, acc_free(tile))
                    pe.wait_ge(raw_copied, c.at("raw") + i - 2 + 1)
                    pe.wait_ge(tables_loaded, 48)
                    pe.matmul(out, e_tab[:, 2432:2560], raw[:, i % 2, :], start=True, stop=True).then_inc(side_done, 1)
                else:
                    pe.wait_ge(acc_drained, acc_free(tile))
                    pe.wait_ge(pooled, i + 1)
                    pe.wait_ge(tables_loaded, 48)
                    pe.matmul(out, e_wg[:, i, :], e_pw[:, i, :], start=True, stop=True).then_inc(side_done, 1)
            pe.wait_ge(acc_drained, drained(c.tiles + len(EVEN_ORDER) - 1))
            pe.wait_ge(rotated, 8)
            units = even_units()
            B, T = c.blocks + 12, c.tiles + len(EVEN_ORDER)

            def columns_of(ks):
                for q in ks:
                    for m in range(OPEN):
                        mm = part(pe, bank[(T + m) % ACCS][:], (B + m) % RING, q, m_hi[:, q, :], m_lo[:, q, :],
                                  q == 0, q == KD - 1)
                        if q == KD - 1:
                            mm.then_inc(blocks_done, 1)

            def pooled_part():
                pe.wait_ge(pool_split, 2)
                pe.wait_ge(w_rest, rest_done(B + OPEN - 1))
                columns_of((0,))
            attend_pe(pe, c, units, {len(units) + 2: pooled_part, len(units) + 3: lambda: columns_of((1,))})
            pe.wait_ge(head_split, c.heads + len(units) // 4 - 2)
            columns_of(range(2, KD - 1))
            pe.wait_ge(head_split, c.heads + len(units) // 4)
            columns_of((KD - 1,))
            k.blocks = B + OPEN
            for m in range(OPEN, KD):
                project(pe, k, T + m, [xs_of(m_hi, m_lo, KD)])

        def even_act(act, c):
            act.wait_ge(blocks_done, block_done(c.blocks - 1))
            act.dma_start(e_tab[:], t["tab_even"]).then_inc(tables_loaded, 16)
            act.dma_start(e_wg[:], t["ev_wg"]).then_inc(tables_loaded, 16)
            act.dma_start(e_small[:], t["ev_small"]).then_inc(tables_loaded, 16)
            g = c.blocks
            for n, (kind, i) in enumerate(EVEN_ORDER):
                if kind in ("lin", "val"):
                    if n:
                        round_ahead(act, g)
                    g += 1
                if kind == "lin" and i >= 2:
                    act.wait_ge(blocks_done, block_done(g - 1))
                    act.activation(raw[:, i % 2, :], bank[(c.tiles + n) % ACCS][:], ACT.Copy).then_inc(raw_copied, 1)
                if kind == "grp":
                    act.wait_ge(acc_drained, drained(c.tiles + n))
                    act.activation(m_hi[:, i, :], tmp[:, i, :], ACT.Copy).then_inc(pool_rounded, 1)
            attend_act(act, c, even_units())
            k = c.copy()
            k.tiles += len(EVEN_ORDER)
            out_act(act, k, 1, c.blocks + 12, y)

        def even_dve(dve, ch, c):
            dve.wait_ge(tables_loaded, 48)
            ch.link(dve.memset(e_u[:], 0.0))
            ch.link(dve.tensor_scalar(e_nsink[:], e_small[:, 2:14], -1.0, None, ALU.mult))
            for q in range(2):
                ch.link(dve.tensor_tensor(e_tab[:, q * S:(q + 1) * S], e_tab[:, q * S:(q + 1) * S], factor, ALU.mult))
            side = c.at("side")

            def pools(i):
                dve.wait_ge(acc_drained, drained(c.tiles + 1))
                u, a, b = e_u[:, i, :], e_a[:, 0, :], e_a[:, 1, :]
                W = S + 16
                ch.link(dve.tensor_tensor(a[:, 1:W], u[:, 0:W - 1], u[:, 1:W], ALU.add))
                rows = slice(HD, P) if i == 0 else slice(0, P)
                ch.link(dve.tensor_tensor(b[rows, 2:W - 1], a[rows, 1:W - 2], a[rows, 3:W], ALU.add))
                if i == 1:
                    ch.link(dve.tensor_tensor(a[:, 4:W - 3], b[:, 2:W - 5], b[:, 6:W - 1], ALU.add))
                    ch.link(dve.tensor_tensor(b[HD:P, 8:W - 8], a[HD:P, 4:W - 12], a[HD:P, 12:W - 4], ALU.add))
                ch.link(dve.tensor_tensor(e_pw[0:HD, i, :], a[0:HD, 8:8 + S], e_tab[0:HD, 1408 + i * S:1408 + (i + 1) * S], ALU.mult))
                ch.link(dve.tensor_tensor(e_pw[HD:P, i, :], b[HD:P, 8:8 + S], e_tab[HD:P, 1408 + i * S:1408 + (i + 1) * S], ALU.mult))
                dve.tensor_tensor(e_pw[:, i, :], e_pw[:, i, :], u[:, 8:8 + S], ALU.subtract).then_inc(pooled, 1)

            for n, (kind, i) in enumerate(EVEN_ORDER):
                src = bank[(c.tiles + n) % ACCS][:]
                if kind == "lin" and i < 2:
                    dve.wait_ge(blocks_done, block_done(c.blocks + i))
                    dve.tensor_tensor(e_u[:, i, 8:8 + S], src, factor, ALU.mult).then_inc(acc_drained, 1)
                elif kind == "lin":
                    dve.wait_ge(raw_copied, c.at("raw") + i - 1)
                    dve.tensor_tensor(e_qk[:, i - 2, :], src, e_tab[:, 0:S], ALU.mult).then_inc(acc_drained, 1)
                    if i in (3, 4):
                        pools(i - 3)
                elif kind == "rot":
                    side += 1
                    dve.wait_ge(side_done, side)
                    if i >= 4:
                        dve.wait_ge(rotated, i - 3)
                    dve.tensor_tensor(tmp[:, i % 2, :], src, e_tab[:, S:2 * S], ALU.mult).then_inc(acc_drained, 1)
                    dve.wait_ge(acc_drained, drained(c.tiles + n))
                    dve.tensor_tensor(e_qk[:, i - 2, :], e_qk[:, i - 2, :], tmp[:, i % 2, :], ALU.add)\
                       .then_inc(rotated, 1)
                elif kind == "grp":
                    side += 1
                    dve.wait_ge(side_done, side)
                    dve.tensor_scalar(tmp[:, i, :], src, e_small[:, i:i + 1], None, ALU.mult).then_inc(acc_drained, 1)
                    dve.wait_ge(pool_rounded, i + 1)
                    dve.tensor_tensor(m_lo[:, i, :], tmp[:, i, :], m_hi[:, i, :].bitcast(F32), ALU.subtract)\
                       .then_inc(pool_split, 1)
                    dve.wait_ge(pool_split, i + 1)
                else:
                    dve.wait_ge(blocks_done, block_done(c.blocks + 10 + i))
                    scale_values(dve, e_v[:, i, :], src)
            dve.wait_ge(acc_drained, drained(c.tiles + len(EVEN_ORDER) - 1))
            dve.wait_ge(rotated, 8)
            attend_dve(dve, ch, c, even_units())
            k = c.copy()
            k.tiles += len(EVEN_ORDER)
            out_dve(dve, ch, k, 1, c.blocks + 12, y)

        SIGN, BACK, MASK_F, MASK_B = 0, 1, 2, 2 + P
        CW, CB_, LG, LB, SW, SB, DS, NG, DTB, ALOG = 0, 124, 128, 132, 136, 200, 216, 224, 232, 233
        LAST = 2 * CONV_T + 25
        PRODUCTS_AT = 0
        LN_AT = 46

        def odd_sp(sp, c):
            stream_sp(sp, c.blocks, t["od_in"], ODD_LINS)
            g = c.blocks + ODD_LINS
            for m in range(KD):
                for b, nk in enumerate((8, 4)):
                    n = 2 * m + b
                    load(sp, g + n, (g + n) % RING, t["od_out"][m][:, b * 1024:b * 1024 + nk * P])

        def odd_pool(pool, c):
            stream_pool(pool, c.blocks + RING, ODD_LINS - RING)
            g = c.blocks + ODD_LINS
            pool.wait_ge(steps_ready, 1)
            ch = Chain(pool, conv_tap)
            ch.link(conv(pool, 3, TAPS[0]))
            for q, j in enumerate(TAPS[1:]):
                d = j - CONV_K // 2
                a, b = max(0, -d), min(S, S - d)
                pool.wait_ge(conv_product, q + 1)
                ch.link(pool.tensor_tensor(o_cv[:, 3, a:b], o_cv[:, 3, a:b], o_product[:, q % 2, a + d:b + d], ALU.add))
            pool.wait_ge(weighted, PRODUCTS_AT + CONV_K)
            for i in range(1, CONV_T):
                if i > 1:
                    pool.wait_ge(conv_added, i - 1)
                pool.tensor_tensor(o_sum, o_cv[:, 0, :] if i == 1 else o_sum, o_cv[:, i, :], ALU.add).then_inc(conv_added, 1)
            add_squares(pool, c, CONV_T)
            k = c.copy()
            k.add("sq", CONV_T)
            k.add("added", CONV_T - 1)
            for n in range(2 * KD):
                if n == RING:
                    add_squares(pool, k)
                rest_block(pool, g + n, (g + n) % RING, (1024, 512)[n % 2])

        TAPS = [CONV_K // 2] + [j for j in range(CONV_K) if j != CONV_K // 2]

        def tap_weight(i, j):
            return o_small[:, CW + i * CONV_K + j:CW + i * CONV_K + j + 1]

        def conv(eng, i, j):
            d = j - CONV_K // 2
            w = tap_weight(i, j)
            if d == 0:
                return eng.tensor_scalar(o_cv[:, i, :], o_g[:, i, :], w, o_small[:, CB_ + i:CB_ + i + 1], ALU.mult, ALU.add)
            a, b = max(0, -d), min(S, S - d)
            return eng.scalar_tensor_tensor(out=o_cv[:, i, a:b], in0=o_g[:, i, a + d:b + d], scalar=w,
                                            in1=o_cv[:, i, a:b], op0=ALU.mult, op1=ALU.add)

        def odd_end(c):
            c.blocks += ODD_LINS + 2 * KD
            c.tiles += LAST + 1 + 8
            c.add("side", 1 + 8)
            c.norms += 2
            c.add("std", 1)
            c.squares += 2
            c.add("sq", CONV_T)
            c.add("added", CONV_T - 1)
            norm_end(c)
            out_end(c)

        def ssm_units():
            return [(head, st) for head in range(SH) for st in range(4)]

        def odd_pe(pe, c):
            k = c.copy()
            k.blocks += OPEN + 1
            for n in range(OPEN + 1, LAST):
                project(pe, k, c.tiles + n, [xs_of(xh, xl, KD)])
            T = c.tiles + LAST
            pe.wait_ge(acc_drained, acc_free(T))
            pe.wait_ge(steps_ready, 1)
            for n in range(4):
                tok = slice(n * P, (n + 1) * P)
                pe.transpose(bank[T % ACCS][:, n * 32:(n + 1) * 32], work[0:32, 2, tok], ident[0:32, 0:32])
                mm = pe.transpose(bank[T % ACCS][:, P + n * 32:P + (n + 1) * 32], o_r[:, tok], ident[0:32, 0:32])
            mm.then_inc(side_done, 1)
            def turn(j):
                pe.wait_ge(acc_drained, acc_free(T + 1 + j))
                pe.wait_ge(xbc_done, 16)
                n, half = j // 2, j % 2
                for q in range(4):
                    mm = pe.transpose(bank[(T + 1 + j) % ACCS][:, q * P:(q + 1) * P],
                                      o_x[:, 4 * half + q, n * P:(n + 1) * P], ident[:])
                mm.then_inc(side_done, 1)
            for j in range(8):
                turn(j)
            pe.wait_ge(acc_drained, drained(T + 8))
            units = ssm_units()
            n = len(units)
            for s in range(n + 2):
                if s == 0 or (s % 16 == 12 and s < 60):
                    grp = 0 if s == 0 else s // 16 + 1
                    if grp < SG:
                        for st in range(4):
                            q = grp * 4 + st
                            if q >= 2:
                                pe.wait_ge(cb_copied, q - 1)
                            pe.matmul(bank[q % 2][:], o_b[:, grp, st * P:(st + 1) * P], o_c[:, grp, :],
                                      start=True, stop=True).then_inc(cb_summed, 1)
                if s == LN_AT:
                    pe.wait_ge(conv_added, CONV_T - 1)
                    pe.wait_ge(cb_copied, 16)
                    sum_squares(pe, o_sum, True, 1, 0)
                elif s == LN_AT + 2:
                    spread(pe, k, 1)
                    k.norms += 1
                elif s == LN_AT + 10:
                    pe.wait_ge(squares_added, c.at("added") + CONV_T - 1)
                    sum_squares(pe, sqsum, True, 1, 0)
                elif s == LN_AT + 13:
                    spread(pe, k, 1)
                    k.norms += 1
                if s < n:
                    head, st = units[s]
                    if s >= 2:
                        pe.wait_ge(exps_ready, s - 1)
                    for d, (lo, hi, mask) in enumerate(((st * P, S, o_mask[:, 0, :]), (0, (st + 1) * P, o_mask[:, 1, :]))):
                        row = d * SH + head
                        out = bank[4 + 2 * (s % 2) + d]
                        pe.matmul(out[:, lo:hi], o_pick[:, row:row + 1].to_broadcast([96, P]), o_r3[:, lo:hi],
                                  start=True, stop=True)
                        mm = pe.matmul(out[:, st * P:(st + 1) * P], identb[:], mask, start=False, stop=True,
                                       skip_group_check=True)
                    mm.then_inc(decays_spread, 1)
                if 0 <= s - 2 < n:
                    head, st = units[s - 2]
                    half, pair = slice(head % 2 * HD, (head % 2 + 1) * HD), head // 2
                    pe.wait_ge(weighted, s - 1)
                    if head % 2 == 0 and st == 0 and pair >= 2:
                        pe.wait_ge(pair_read, pair - 1)
                    out, cols = bank[2 + pair % 2], slice(head * HD, (head + 1) * HD)
                    wide = S - st * P
                    e = o_e[:, (s - 2) % 3, :]
                    pe.matmul(out[half, st * P:S], o_xf[:, st, cols], e[:, 0:wide], start=st == 0, stop=False,
                              skip_group_check=True)
                    pe.matmul(out[half, 0:(st + 1) * P], o_xb[:, st, cols], e[:, wide:640], start=False, stop=st == 3,
                              skip_group_check=True).then_inc(scanned, 1)
            k.add("added", CONV_T - 1)
            B, T = c.blocks + ODD_LINS, T + 9
            for m in range(2):
                pe.wait_ge(acc_drained, acc_free(T + m))
            pe.wait_ge(w_rest, rest_done(B + 3))
            for k4 in range(CONV_T):
                pe.wait_ge(g_split, k4 + 1)
                if k4 == 2:
                    pe.wait_ge(squares_added, k.at("added") + KD - 1)
                    sum_squares(pe, sqsum, True)
                for m in range(2):
                    part(pe, bank[(T + m) % ACCS][:], (B + 2 * m) % RING, k4, g_hi[:, k4, :], g_lo[:, k4, :], k4 == 0, False)
            spread(pe, k)
            for k8 in range(KD):
                pe.wait_ge(xl_ready, c.xn + k8 + 1)
                for m in range(2):
                    b, at = divmod(CONV_T + k8, 8)
                    mm = part(pe, bank[(T + m) % ACCS][:], (B + 2 * m + b) % RING, at, xh[:, k8, :], xl[:, k8, :],
                              False, k8 == KD - 1)
                    if k8 == KD - 1:
                        mm.then_inc(blocks_done, 2)
            k.blocks = B + 4
            (gh, gl), (yh, yl) = xs_of(g_hi, g_lo, CONV_T), xs_of(xh, xl, 4)
            for m in range(2, KD):
                project(pe, k, T + m, [(gh + yh, gl + yl), xs_of(xh, xl, 4, 4)])

        def odd_act(act, c):
            act.wait_ge(blocks_done, block_done(c.blocks - 1))
            act.dma_start(o_tab[:], t["tab_odd"]).then_inc(odd_loaded, 16)
            act.dma_start(o_small[:], t["od_small"]).then_inc(odd_loaded, 16)
            act.wait_ge(odd_loaded, 32)
            act.activation(o_a[:, 0:1], o_small[0:32, ALOG:ALOG + 1], ACT.Exp).then_inc(a_ready, 1)
            B, T = c.blocks, c.tiles
            for n in range(LAST):
                if n:
                    round_ahead(act, B + n)
                tile = bank[(T + n) % ACCS][:]
                if n < 2 * CONV_T and n % 2 == 1:
                    i = n // 2
                    act.wait_ge(acc_drained, drained(T + n))
                    act.activation(work[:, i % 2, :], work[:, i % 2, :], ACT.Sigmoid).then_inc(glu_done, 1)
                elif 2 * CONV_T <= n < 2 * CONV_T + 16:
                    i = n - 2 * CONV_T
                    dst = (o_x[:, i, :] if i < 8 else o_b[:, i - 8, :] if i < 12 else o_c[:, i - 12, :])
                    act.wait_ge(xbc_convolved, i + 1)
                    act.activation(dst, tmp[:, i % 2, :], ACT.Silu).then_inc(xbc_done, 1)
                elif n == 2 * CONV_T + 16:
                    act.wait_ge(dt_arg, 1)
                    act.activation(work[0:32, 3, :], work[0:32, 3, :], ACT.Exp).then_inc(dt_exp, 1)
                elif n > 2 * CONV_T + 16:
                    i = n - 2 * CONV_T - 17
                    act.wait_ge(acc_drained, drained(T + n))
                    act.activation(o_z[:, i, :], o_z[:, i, :], ACT.Silu).then_inc(z_done, 1)
            k, y_k = c.copy(), c.copy()
            k.squares += 2
            y_k.squares += 2
            y_k.add("sq", CONV_T)
            y_k.add("added", CONV_T - 1)
            y_k.add("std", 1)

            def square_y(j):
                act.wait_ge(gated, j + 1)
                square(act, y_k, j, o_x)
            round_ahead(act, B + LAST)
            for s, (head, st) in enumerate(ssm_units()):
                act.wait_ge(decays_spread, s + 1)
                if s >= 3:
                    act.wait_ge(scanned, s - 2)
                wide = S - st * P
                act.activation(o_e[:, s % 3, 0:wide], bank[4 + 2 * (s % 2)][:, st * P:S], ACT.Exp,
                               bias=o_nr[:, st, head:head + 1])
                act.activation(o_e[:, s % 3, wide:640], bank[5 + 2 * (s % 2)][:, 0:(st + 1) * P], ACT.Exp,
                               bias=o_nr[:, st, SH + head:SH + head + 1]).then_inc(exps_ready, 1)
                q = s - PRODUCTS_AT
                if 0 <= q < CONV_K - 1:
                    act.wait_ge(conv_tap, 1 + max(0, q - 1))
                    act.activation(o_product[:, q % 2, :], o_g[:, 3, :], ACT.Copy, scale=tap_weight(3, TAPS[q + 1]))\
                       .then_inc(conv_product, 1)
                if s == LN_AT + 6:
                    for i in range(CONV_T):
                        act.wait_ge(centered, i + 1)
                        square(act, c, i, o_cv)
                elif s == LN_AT + 11:
                    std(act, c, 2, 0)
                elif s > LN_AT + 11:
                    square_y(s - LN_AT - 12)
            for i in range(CONV_T):
                if i == 2:
                    for j in range(len(ssm_units()) - LN_AT - 12, KD):
                        square_y(j)
                act.wait_ge(normed, i + 1)
                if i >= 2:
                    act.wait_ge(g_split, i - 1)
                act.activation(tmp[:, i % 2, :], o_cv[:, i, :], ACT.Silu, bias=o_small[:, LB + i:LB + i + 1],
                               scale=o_small[:, LG + i:LG + i + 1]).then_inc(g_silu, 1)
                act.wait_ge(g_silu, i + 1)
                act.activation(g_hi[:, i, :], tmp[:, i % 2, :], ACT.Copy).then_inc(g_rounded, 1)
            std(act, y_k, 1)
            for j in range(KD):
                act.wait_ge(xn_ready, c.at("xnr") + j + 1)
                act.activation(xh[:, j, :], tmp[:, j % 2, :], ACT.Copy).then_inc(xh_ready, 1)
            k.tiles = T + LAST + 9
            out_act(act, k, 2, B + LAST, o_y, 1)

        def odd_dve(dve, ch, c):
            B, T = c.blocks, c.tiles
            dve.wait_ge(odd_loaded, 32)
            ch.link(dve.tensor_copy(o_mask[:, 0, :], o_tab[:, MASK_F:MASK_F + P]))
            ch.link(dve.tensor_copy(o_mask[:, 1, :], o_tab[:, MASK_B:MASK_B + P]))
            ch.link(dve.tensor_copy(identb[:], ident[:]))
            dve.wait_ge(a_ready, 1)
            ch.link(dve.tensor_scalar(o_a[:, 1:2], o_a[:, 0:1], -1.0, None, ALU.mult))

            for q in range(3):
                ch.link(dve.tensor_copy(o_pick[32 * q:32 * (q + 1), :], ident[0:32, 0:32]))

            taps = [(i, j) for j in TAPS for i in (0, 1)] + [(2, j) for j in TAPS]
            last = {}

            def tap():
                if not taps:
                    return
                i, j = taps.pop(0)
                if i in last:
                    dve.wait_ge(dve_step, last[i])
                last[i] = ch.step(conv(dve, i, j))

            A, Bq, C, Dq = (work[0:32, q, :] for q in (2, 3, 4, 5))
            for n in range(LAST):
                src = bank[(T + n) % ACCS]
                dve.wait_ge(blocks_done, block_done(B + n))
                if n < 2 * CONV_T:
                    i = n // 2
                    dst = work[:, i % 2, :] if n % 2 else o_g[:, i, :]
                    dve.tensor_tensor(dst, src[:], factor, ALU.mult).then_inc(acc_drained, 1)
                    if n % 2:
                        dve.wait_ge(glu_done, i + 1)
                        ch.link(dve.tensor_tensor(o_g[:, i, :], o_g[:, i, :], work[:, i % 2, :], ALU.mult))
                    for _ in range(3 if n >= 4 else 0):
                        tap()
                    continue
                if n < 2 * CONV_T + 16:
                    i = n - 2 * CONV_T
                    if i >= 2:
                        dve.wait_ge(xbc_done, i - 1)
                    o = tmp[:, i % 2, :]

                    def w(j):
                        return o_small[:, SW + i * SSM_K + j:SW + i * SSM_K + j + 1]
                    src = work[:, 2 + i % 2, :]
                    dve.tensor_tensor(src, bank[(T + n) % ACCS][:], factor, ALU.mult).then_inc(acc_drained, 1)
                    tap()
                    dve.wait_ge(acc_drained, drained(T + n))
                    at = ch.step(dve.tensor_scalar(o, src, w(2), o_small[:, SB + i:SB + i + 1], ALU.mult, ALU.add))
                    for j, (a, b, d) in ((0, (2, S, -2)), (1, (1, S, -1)), (3, (0, S - 1, 1))):
                        if j == 1:
                            tap()
                        dve.wait_ge(dve_step, at)
                        ins = dve.scalar_tensor_tensor(out=o[:, a:b], in0=src[:, a + d:b + d], scalar=w(j), in1=o[:, a:b],
                                                       op0=ALU.mult, op1=ALU.add)
                        if j < 3:
                            at = ch.step(ins)
                        else:
                            ins.then_inc(xbc_convolved, 1)
                elif n == 2 * CONV_T + 16:
                    dve.wait_ge(xbc_convolved, 16)
                    dve.tensor_tensor(A, src[0:32, :], factor[0:32, :], ALU.mult).then_inc(acc_drained, 1)
                    dve.wait_ge(acc_drained, drained(T + n))
                    ch.link(dve.tensor_scalar(A, A, o_small[0:32, DTB:DTB + 1], None, ALU.add))
                    dve.scalar_tensor_tensor(out=Bq, in0=A, scalar=-1.0, in1=A, op0=ALU.mult, op1=ALU.min)\
                       .then_inc(dt_arg, 1)
                else:
                    i = n - 2 * CONV_T - 17
                    dve.tensor_tensor(o_z[:, i, :], src[:], factor, ALU.mult).then_inc(acc_drained, 1)
                    for _ in range((6, 0, 0, 1, 1, 6, 6, 6)[i]):
                        tap()
                if n == 2 * CONV_T + 18:
                    dve.wait_ge(dt_exp, 1)
                    ch.link(dve.tensor_scalar(C, Bq, 2.0, None, ALU.add))
                    ch.link(dve.reciprocal(C, C))
                    ch.link(dve.tensor_tensor(Bq, Bq, C, ALU.mult))
                    ch.link(dve.tensor_tensor(C, Bq, Bq, ALU.mult))
                    ch.link(dve.tensor_scalar(Dq, C, 1.0 / (2 * LOG_TERMS + 1), None, ALU.mult))
                elif n == 2 * CONV_T + 19:
                    for q in range(LOG_TERMS - 1, 0, -1):
                        ch.link(dve.scalar_tensor_tensor(out=Dq, in0=Dq, scalar=1.0 / (2 * q + 1), in1=C, op0=ALU.add, op1=ALU.mult))
                    ch.link(dve.scalar_tensor_tensor(out=Dq, in0=Dq, scalar=1.0, in1=Bq, op0=ALU.add, op1=ALU.mult))
                elif n == 2 * CONV_T + 20:
                    ch.link(dve.tensor_scalar(A, A, 0.0, None, ALU.max))
                    ch.link(dve.scalar_tensor_tensor(out=A, in0=Dq, scalar=2.0, in1=A, op0=ALU.mult, op1=ALU.add))
                    ch.link(dve.tensor_scalar(Bq, A, o_a[:, 1:2], None, ALU.mult))
                    ch.link(dve.memset(Dq, 1.0))
                    ch.link(dve.tensor_tensor_scan(C, Dq, Bq, 0.0, ALU.mult, ALU.add))
                    ch.link(dve.tensor_scalar(Bq, Bq, o_tab[0:32, BACK:BACK + 1], None, ALU.mult))
                    dve.scalar_tensor_tensor(out=o_r[:], in0=C, scalar=o_tab[0:32, SIGN:SIGN + 1], in1=Bq,
                                             op0=ALU.mult, op1=ALU.add).then_inc(steps_ready, 1)
                elif n == 2 * CONV_T + 21:
                    dve.wait_ge(steps_ready, 1)
                    ch.link(dve.tensor_copy(o_r3[0:32, :], o_r[:]))
                    ch.link(dve.tensor_tensor(Bq, o_r[:], o_r3[0:32, :], ALU.subtract))
                    ch.link(dve.tensor_copy(o_part[:], Bq))
                    ch.link(dve.tensor_copy(o_r3[32:64, :], o_part[:]))
                    ch.link(dve.tensor_tensor(o_r3[64:96, :], Bq, o_part[:], ALU.subtract))
            dve.wait_ge(dve_step, ch.n)
            k = c.copy()
            T2, side = T + LAST, c.at("side")
            dve.wait_ge(side_done, side + 1)
            ch.link(dve.tensor_copy(o_dt[:], bank[T2 % ACCS][:, 0:P]))
            dve.tensor_scalar(o_nr[:], bank[T2 % ACCS][:, P:2 * P], -1.0, None, ALU.mult).then_inc(acc_drained, 1)
            dve.wait_ge(acc_drained, drained(T2))

            def scale_in(j):
                n, half = j // 2, j % 2
                src = bank[(T2 + 1 + j) % ACCS][:].rearrange("p (h d) -> p h d", d=HD)
                dve.wait_ge(side_done, side + 2 + j)
                for d, dst in enumerate((o_xf, o_xb)):
                    step = o_dt[:, n, d * SH + 8 * half:d * SH + 8 * half + 8].unsqueeze(2).broadcast_to([P, 8, HD])
                    ins = dve.tensor_tensor(dst[:, n, half * S:(half + 1) * S].rearrange("p (h d) -> p h d", d=HD),
                                            src, step, ALU.mult)
                    ins.then_inc(scaled_in if d == 0 else acc_drained, 1)
            for j in range(8):
                scale_in(j)
            dve.wait_ge(z_done, KD)
            units = ssm_units()
            n = len(units)
            for s in range(n + 3):
                tap()
                if s == LN_AT + 1:
                    dve.wait_ge(squares_summed, c.squares + 1)
                    dve.tensor_copy(stat[:, 1, 0:4], bank[0][:, 0:4]).then_inc(rstd_ready, 1)
                elif s in (LN_AT + 4, LN_AT + 5):
                    dve.wait_ge(spread_ready, c.norms + 1)
                    for i in (0, 1) if s == LN_AT + 4 else (2, 3):
                        dve.tensor_tensor(o_cv[:, i, :], o_cv[:, i, :], bank[1][:], ALU.subtract).then_inc(centered, 1)
                elif s == LN_AT + 12:
                    dve.wait_ge(std_ready, c.at("std") + 1)
                    dve.reciprocal(stat[:, 1, 0:4], stat[:, 0, 0:4]).then_inc(rstd_ready, 1)
                elif s in (LN_AT + 14, LN_AT + 15):
                    dve.wait_ge(spread_ready, c.norms + 2)
                    dve.wait_ge(centered, CONV_T)
                    for i in (0, 1) if s == LN_AT + 14 else (2, 3):
                        dve.tensor_tensor(o_cv[:, i, :], o_cv[:, i, :], bank[1][:], ALU.mult).then_inc(normed, 1)
                if s == 0 or (s % 16 == 12 and s < 60):
                    grp = 0 if s == 0 else s // 16 + 1
                    if grp < SG:
                        for st in range(4):
                            dve.wait_ge(cb_summed, grp * 4 + st + 1)
                            dve.tensor_copy(o_cb[:, grp % 2, st, :], bank[st % 2][:]).then_inc(cb_copied, 1)
                if s < n:
                    head, st = units[s]
                    grp, wide = head // 4, S - st * P
                    if head % 4 == 0 and st == 0:
                        dve.wait_ge(cb_copied, 4 * grp + 4)
                    dve.wait_ge(exps_ready, s + 1)
                    e, cb = o_e[:, s % 3, :], o_cb[:, grp % 2, st, :]
                    dve.tensor_tensor(e[:, 0:wide], e[:, 0:wide], cb[:, st * P:S], ALU.mult)
                    dve.tensor_tensor(e[:, wide:640], e[:, wide:640], cb[:, 0:(st + 1) * P], ALU.mult)\
                       .then_inc(weighted, 1)
                if s - 3 >= 0 and (s - 3) % 8 == 7:
                    j = (s - 3) // 8
                    dve.wait_ge(scanned, s - 2)
                    dve.scalar_tensor_tensor(out=o_x[:, j, :], in0=o_x[:, j, :], scalar=o_small[:, DS + j:DS + j + 1],
                                             in1=bank[2 + j % 2][:], op0=ALU.mult, op1=ALU.add).then_inc(pair_read, 1)
                    dve.wait_ge(pair_read, j + 1)
                    dve.tensor_tensor(o_x[:, j, :], o_x[:, j, :], o_z[:, j, :], ALU.mult).then_inc(gated, 1)
            for i in range(CONV_T):
                dve.wait_ge(g_rounded, i + 1)
                dve.tensor_tensor(g_lo[:, i, :], tmp[:, i % 2, :], g_hi[:, i, :].bitcast(F32), ALU.subtract)\
                   .then_inc(g_split, 1)
            dve.wait_ge(g_split, CONV_T)
            dve.wait_ge(gated, KD)
            k.norms += 2
            k.add("std", 1)
            norm_dve(dve, k, o_x, lambda j: o_small[:, NG + j:NG + j + 1])
            k.tiles = T2 + 9
            out_dve(dve, ch, k, 2, B + LAST, o_y)

        COS_A, SIN_A, COS_B, SIN_B, ROT_A, ROT_B = 0, S, 2 * S, 3 * S, 4 * S, 4 * S + P
        NORMS2 = [("qk", i) for i in range(RAWS)] + [("cq", i) for i in range(QR)] + [("kv", i) for i in range(KR)]
        LINS2 = NORMS2 + [("kr", 0), ("va", 0)]
        SIDES2 = [("spread", i) for i in (RAWS, RAWS + 1)] + [("spread", i) for i in range(RAWS)] + [("rotkr", 0)]
        UPS2 = []
        for _h in range(8):
            UPS2 += [("up", _h)] + ([("rotup", _h - 1)] if _h else []) + ([("rot", _h)] if _h < RAWS else [])
        UPS2 += [("kn", 0), ("rotup", 7), ("kn", 1), ("kn", 2), ("kn", 3)] + [("vb", i) for i in range(4)]
        ORDER2 = LINS2 + SIDES2 + UPS2
        UP_HEADS = (3, 3, 2)

        def mix2_blocks():
            return [1024] * len(LINS2) + [n * QR * QK for n in UP_HEADS] + [1024, 1024] + [1024] * (3 * KD) + [1024] * KD

        def grouped_units():
            return [dict(q=b_qk[half, j, n * P:(n + 1) * P], k=b_qk[half, 4, :], keys=S, scale=HD ** -0.5, mask=None, n=n, half=half,
                         v=[b_va[:, m * P + half.start:m * P + half.stop] for m in range(4)], hi=ya_hi[half, j, :], lo=ya_lo[half, j, :])
                    for j in range(4) for half in (slice(0, HD), slice(HD, P)) for n in range(4)]

        def latent_units():
            return [dict(q=b_q[0:QK, head, n * P:(n + 1) * P], k=b_k[0:QK, head, :], keys=S, scale=QK ** -0.5, mask=None, n=n, half=half,
                         v=[b_vb[:, head // 2, m * P + half.start:m * P + half.stop] for m in range(4)], hi=yb_hi[half, head // 2, :],
                         lo=yb_lo[half, head // 2, :])
                    for head in range(8) for half in (slice(head % 2 * HD, head % 2 * HD + HD),) for n in range(4)]

        def mix2_sp(sp, c, i):
            g = c.blocks
            stream_sp(sp, g, t["b_in"][i], len(LINS2))
            g += len(LINS2)
            for b, n in enumerate(UP_HEADS):
                w = QR * QK
                load(sp, g + b, (g + b) % RING, t["b_up"][i][:, 3 * b * w:(3 * b + n) * w])
            g += 3
            stream_sp(sp, g, t["b_kv"][i], 2)
            stream_sp(sp, g + 2, t["b_gates"][i], 3 * KD)
            stream_sp(sp, g + 2 + 3 * KD, t["b_out"][i], KD)

        def mix2_pool(pool, c):
            g = c.blocks
            stream_pool(pool, g + RING, len(LINS2) - RING)
            g += len(LINS2)
            for b, n in enumerate(UP_HEADS):
                rest_block(pool, g + b, (g + b) % RING, n * QR * QK)
            stream_pool(pool, g + 3, 2 + 4 * KD)

        def mix2_end(c):
            c.blocks += len(mix2_blocks())
            c.tiles += len(ORDER2)
            c.add("side", len(SIDES2) + RAWS + 8)
            c.add("raw", 1 + 8)
            c.add("rotated", RAWS + 1 + 8)
            c.add("sq", len(NORMS2))
            c.squares += len(NORMS2)
            c.add("std", 1)
            c.add("rstd2", 1)
            c.xn += QR + KR
            attend_end(c, grouped_units())
            attend_end(c, latent_units())
            c.tiles += 4 * KD
            c.add("tables", 1)
            out_end(c)

        def stat_cols(i):
            return slice(8 * i, 8 * i + 8) if i < RAWS else slice(8 * RAWS + 4 * (i - RAWS), 8 * RAWS + 4 * (i - RAWS) + 4)

        def norm_group(i):
            return i if i < RAWS else RAWS if i < RAWS + QR else RAWS + 1

        def mix2_pe(pe, c):
            k = c.copy()
            k.blocks += OPEN + 1
            kn_slot = vb_slot = None

            def sums(i):
                pe.wait_ge(x_squared, c.at("sq") + i + 1)
                col = stat_cols(norm_group(i))
                for n in range(4):
                    src = sq[:, i % 2, n * P:(n + 1) * P]
                    if i < RAWS:
                        mm = pe.matmul(bank[STAT][:, col.start + 2 * n:col.start + 2 * n + 2], src, meancol[:, 4:6],
                                       start=i == 0 and n == 0, stop=True, skip_group_check=True)
                    else:
                        m = 2 if i < RAWS + QR else 3
                        mm = pe.matmul(bank[STAT][:, col.start + n:col.start + n + 1], src, meancol[:, m:m + 1],
                                       start=False, stop=True, skip_group_check=True)
                mm.then_inc(squares_summed, 1)

            for n, (kind, i) in enumerate(ORDER2):
                tile = c.tiles + n
                out = bank[tile % ACCS][:]
                if kind in ("qk", "cq", "kv", "kr"):
                    if n > OPEN:
                        project(pe, k, tile, [xs_of(xh, xl, KD)])
                elif kind == "va":
                    project_values(pe, k, tile)
                elif kind == "spread":
                    pe.wait_ge(acc_drained, acc_free(tile))
                    pe.wait_ge(rstd2_ready, c.at("rstd2") + 1)
                    col = stat_cols(i).start
                    for m in range(4):
                        many = 2 if i < RAWS else 1
                        for half in range(many):
                            r = stat[:, 0, col + many * m + half:col + many * m + half + 1].to_broadcast([P, P // many])
                            rows = slice(half * HD, (half + 1) * HD) if many == 2 else slice(0, P)
                            mm = pe.matmul(out[rows, m * P:(m + 1) * P], r, ident[:], start=True, stop=True)
                    mm.then_inc(side_done, 1)
                elif kind == "rotkr":
                    pe.wait_ge(acc_drained, acc_free(tile))
                    pe.wait_ge(raw_copied, c.at("raw") + 1)
                    pe.wait_ge(tables_loaded, 48 + 32 * (c.at("tables") + 1))
                    pe.matmul(out[0:QK, :], b_tab[0:QK, ROT_B:ROT_B + QK], raw[0:QK, 0, :], start=True, stop=True)\
                      .then_inc(side_done, 1)
                elif kind == "rot":
                    pe.wait_ge(acc_drained, acc_free(tile))
                    pe.wait_ge(acc_drained, drained(c.tiles + ORDER2.index(("spread", i))))
                    pe.matmul(out, b_tab[:, ROT_A:ROT_A + P], b_qk[:, i, :], start=True, stop=True)\
                      .then_inc(side_done, 1)
                elif kind == "rotup":
                    pe.wait_ge(acc_drained, acc_free(tile))
                    pe.wait_ge(raw_copied, c.at("raw") + 1 + i + 1)
                    pe.matmul(out[0:QK, :], b_tab[0:QK, ROT_B:ROT_B + QK], raw[0:QK, (1 + i) % 2, :], start=True, stop=True)\
                      .then_inc(side_done, 1)
                elif kind == "up":
                    pe.wait_ge(acc_drained, acc_free(tile))
                    if i == 0:
                        pe.wait_ge(xl_ready, c.xn + QR + KR)
                    if i % 3 == 0:
                        up_slot = take_block(pe, k)
                    for q in range(QR):
                        at = (i % 3 * QR + q) * QK
                        wh, wl = w_hi[:, up_slot, at:at + QK], w_lo[:, up_slot, at:at + QK]
                        pe.matmul(out[0:QK, :], wh, c_hi[:, q, :], start=q == 0, stop=False)
                        pe.matmul(out[0:QK, :], wh, c_lo[:, q, :], start=False, stop=False)
                        mm = pe.matmul(out[0:QK, :], wl, c_hi[:, q, :], start=False, stop=q == QR - 1)
                    mm.then_inc(blocks_done if i % 3 == 2 or i == 7 else up_done, 1)
                elif kind == "kn":
                    pe.wait_ge(acc_drained, acc_free(tile))
                    if i == 0:
                        kn_slot = take_block(pe, k)
                    for q in range(KR):
                        at = (i * KR + q) * P
                        wh, wl = w_hi[:, kn_slot, at:at + P], w_lo[:, kn_slot, at:at + P]
                        pe.matmul(out, wh, c_hi[:, QR + q, :], start=q == 0, stop=False)
                        pe.matmul(out, wh, c_lo[:, QR + q, :], start=False, stop=False)
                        mm = pe.matmul(out, wl, c_hi[:, QR + q, :], start=False, stop=q == KR - 1)
                    mm.then_inc(blocks_done if i == 3 else up_done, 1)
                else:
                    pe.wait_ge(acc_drained, acc_free(tile))
                    if i == 0:
                        vb_slot = take_block(pe, k)
                    for m in range(4):
                        tok = slice(m * P, (m + 1) * P)
                        for q in range(KR):
                            at = (i * KR + q) * P
                            wh, wl = w_hi[:, vb_slot, at:at + P], w_lo[:, vb_slot, at:at + P]
                            pe.matmul(out[:, tok], c_hi[:, QR + q, tok], wh, start=q == 0, stop=False)
                            pe.matmul(out[:, tok], c_hi[:, QR + q, tok], wl, start=False, stop=False)
                            mm = pe.matmul(out[:, tok], c_lo[:, QR + q, tok], wh, start=False, stop=q == KR - 1)
                    mm.then_inc(blocks_done if i == 3 else up_done, 1)
                if 1 <= n <= len(NORMS2):
                    sums(n - 1)
            pe.wait_ge(acc_drained, drained(c.tiles + len(ORDER2) - 1))
            pe.wait_ge(rotated, c.at("rotated") + RAWS + 1 + 8)
            pe.wait_ge(kr_copied, c.at("tables") + 1)
            k.tiles = c.tiles + len(ORDER2)
            units = grouped_units() + latent_units()

            def gate():
                project(pe, k, k.tiles, [xs_of(xh, xl, KD)])
                k.tiles += 1
            attend_pe(pe, k, units, {len(units) + 2: gate, len(units) + 3: gate})
            for m in range(KD):
                if m:
                    gate()
                    gate()
                else:
                    pe.wait_ge(head_split, c.heads + len(units) // 4)
                slot = take_block(pe, k)
                for q, (hi, lo) in enumerate(((ya_hi, ya_lo), (yb_hi, yb_lo))):
                    pe.wait_ge(acc_drained, acc_free(k.tiles))
                    out = bank[k.tiles % ACCS][:]
                    for j in range(4):
                        at = (4 * q + j) * P
                        wh, wl = w_hi[:, slot, at:at + P], w_lo[:, slot, at:at + P]
                        pe.matmul(out, wh, hi[:, j, :], start=j == 0, stop=False)
                        pe.matmul(out, wh, lo[:, j, :], start=False, stop=False)
                        mm = pe.matmul(out, wl, hi[:, j, :], start=False, stop=j == 3)
                    if q:
                        mm.then_inc(blocks_done, 1)
                    k.tiles += 1
            pe.wait_ge(merged_split, KD * (c.at("tables") + 1))
            out_pe(pe, k, [xs_of(mm_hi, mm_lo, KD)])

        def mix2_act(act, c, layer):
            act.wait_ge(blocks_done, block_done(c.blocks - 1))
            act.dma_start(b_tab[:], t["tab_b"]).then_inc(tables_loaded, 16)
            act.dma_start(b_small[:], t["b_small"][layer]).then_inc(tables_loaded, 16)
            g = c.blocks
            T = c.tiles
            for n, (kind, i) in enumerate(ORDER2):
                src = bank[(T + n) % ACCS]
                if kind in ("qk", "cq", "kv", "kr", "va") or (kind == "up" and i % 3 == 0) or (kind in ("kn", "vb") and i == 0):
                    if n:
                        round_ahead(act, g)
                    g += 1
                if kind in ("qk", "cq", "kv"):
                    act.wait_ge(acc_drained, drained(T + n))
                    if n >= 2:
                        act.wait_ge(squares_summed, c.squares + n - 1)
                    dst = b_qk[:, i, :] if kind == "qk" else c_raw[:, i if kind == "cq" else QR + i, :]
                    act.activation(sq[:, n % 2, :], dst, ACT.Square).then_inc(x_squared, 1)
                elif kind == "kr":
                    act.wait_ge(blocks_done, block_done(g - 1))
                    act.activation(raw[0:QK, 0, :], src[0:QK, :], ACT.Copy).then_inc(raw_copied, 1)
                elif kind == "va":
                    act.wait_ge(squares_summed, c.squares + len(NORMS2))
                    act.activation(stat[:, 0, :], bank[STAT][:, 0:48], ACT.Sqrt, bias=EPS).then_inc(std_ready, 1)
                elif kind == "spread" and i >= RAWS:
                    for q in range(QR if i == RAWS else KR):
                        j = q if i == RAWS else QR + q
                        if q == (QR if i == RAWS else KR) - 1:
                            act.wait_ge(acc_drained, drained(T + n))
                        else:
                            act.wait_ge(cn_ready, (QR + KR - 2) * c.at("tables") + (q if i == RAWS else QR - 1 + q) + 1)
                        act.activation(c_hi[:, j, :], tmp[:, j % 2, :], ACT.Copy).then_inc(xh_ready, 1)
                elif kind == "up":
                    act.wait_ge(blocks_done if i % 3 == 2 or i == 7 else up_done, block_done(g - 1) if i % 3 == 2 or i == 7
                                else ups(c, i))
                    act.activation(raw[0:QK, (1 + i) % 2, :], src[0:QK, :], ACT.Copy).then_inc(raw_copied, 1)
                elif kind == "rotkr":
                    act.wait_ge(rotated, c.at("rotated") + 1)
                    act.activation(b_k[HD:QK, :, :], krot[HD:QK, :].unsqueeze(1).broadcast_to([QK - HD, 8, S]), ACT.Copy)\
                       .then_inc(kr_copied, 1)
            k = c.copy()
            attend_act(act, k, grouped_units() + latent_units())
            T += len(ORDER2)
            G = KD * c.at("tables")
            for m in range(KD):
                for q in range(2):
                    round_ahead(act, g)
                    g += 1
                    act.wait_ge(acc_drained, drained(T + 4 * m + q))
                    act.activation(work[:, q, :], work[:, q, :], ACT.Sigmoid,
                                   bias=b_small[:, 8 + KD * q + m:9 + KD * q + m]).then_inc(gate_ready, 1)
                round_ahead(act, g)
                g += 1
                act.wait_ge(merged, G + m + 1)
                act.activation(mm_hi[:, m, :], work[:, 2, :], ACT.Copy).then_inc(merged_rounded, 1)
            k.tiles = T + 4 * KD
            out_act(act, k, 1, g, y)

        def ups(c, i):
            return 11 * c.at("tables") + i + 1 - i // 3

        def mix2_dve(dve, ch, c):
            T, B, L = c.tiles, c.blocks, c.at("tables")
            side, rots = c.at("side"), c.at("rotated")
            dve.wait_ge(tables_loaded, 48 + 32 * (L + 1))
            xn = c.xn
            for n, (kind, i) in enumerate(ORDER2):
                src = bank[(T + n) % ACCS]
                if kind == "va":
                    dve.wait_ge(std_ready, c.at("std") + 1)
                    dve.reciprocal(stat[:, 0, :], stat[:, 0, :]).then_inc(rstd2_ready, 1)
                if n < len(LINS2):
                    dve.wait_ge(blocks_done, block_done(B + n))
                if kind == "qk":
                    dve.tensor_tensor(b_qk[:, i, :], src[:], factor, ALU.mult).then_inc(acc_drained, 1)
                elif kind in ("cq", "kv"):
                    dve.tensor_tensor(c_raw[:, i if kind == "cq" else QR + i, :], src[:], factor, ALU.mult)\
                       .then_inc(acc_drained, 1)
                elif kind == "kr":
                    dve.wait_ge(raw_copied, c.at("raw") + 1)
                    dve.tensor_tensor(krot[0:QK, :], src[0:QK, :], b_tab[0:QK, COS_B:COS_B + S], ALU.mult).then_inc(acc_drained, 1)
                elif kind == "va":
                    scale_values(dve, b_va[:], src[:])
                    dve.wait_ge(acc_drained, drained(T + n))
                elif kind == "spread" and i < RAWS:
                    side += 1
                    dve.wait_ge(side_done, side)
                    gain = b_small[:, 0:1] if i < 4 else b_small[:, 1:2]
                    dve.scalar_tensor_tensor(out=b_qk[:, i, :], in0=b_qk[:, i, :], scalar=gain, in1=src[:],
                                             op0=ALU.mult, op1=ALU.mult).then_inc(acc_drained, 1)
                elif kind == "spread":
                    side += 1
                    dve.wait_ge(side_done, side)
                    many = QR if i == RAWS else KR
                    for q in range(many):
                        j = q if i == RAWS else QR + q
                        if j >= 2:
                            dve.wait_ge(xl_ready, xn + j - 1)
                        dve.scalar_tensor_tensor(out=tmp[:, j % 2, :], in0=c_raw[:, j, :], scalar=b_small[:, 2 + j:3 + j],
                                                 in1=src[:], op0=ALU.mult, op1=ALU.mult)\
                           .then_inc(acc_drained if q == many - 1 else cn_ready, 1)
                        dve.wait_ge(xh_ready, xn + j + 1)
                        dve.tensor_tensor(c_lo[:, j, :], tmp[:, j % 2, :], c_hi[:, j, :].bitcast(F32), ALU.subtract)\
                           .then_inc(xl_ready, 1)
                    dve.wait_ge(xl_ready, xn + j + 1)
                elif kind == "rotkr":
                    side, rots = side + 1, rots + 1
                    dve.wait_ge(side_done, side)
                    dve.tensor_tensor(work[0:QK, 0, :], src[0:QK, :], b_tab[0:QK, SIN_B:SIN_B + S], ALU.mult).then_inc(acc_drained, 1)
                    dve.wait_ge(acc_drained, drained(T + n))
                    ch.link(dve.tensor_tensor(krot[0:QK, :], krot[0:QK, :], work[0:QK, 0, :], ALU.add))
                    dve.tensor_tensor(krot[0:QK, :], krot[0:QK, :], factor[0:QK, :], ALU.mult).then_inc(rotated, 1)
                elif kind == "rot":
                    side, rots = side + 1, rots + 1
                    dve.wait_ge(side_done, side)
                    dve.wait_ge(rotated, rots - 1)
                    dve.tensor_tensor(work[:, 0, :], src[:], b_tab[:, SIN_A:SIN_A + S], ALU.mult).then_inc(acc_drained, 1)
                    ch.link(dve.tensor_tensor(b_qk[:, i, :], b_qk[:, i, :], b_tab[:, COS_A:COS_A + S], ALU.mult))
                    dve.tensor_tensor(b_qk[:, i, :], b_qk[:, i, :], work[:, 0, :], ALU.add).then_inc(rotated, 1)
                elif kind == "up":
                    dve.wait_ge(raw_copied, c.at("raw") + 1 + i + 1)
                    dve.tensor_tensor(b_q[0:QK, i, :], src[0:QK, :], b_tab[0:QK, COS_B:COS_B + S], ALU.mult).then_inc(acc_drained, 1)
                elif kind == "rotup":
                    side, rots = side + 1, rots + 1
                    dve.wait_ge(side_done, side)
                    dve.wait_ge(rotated, rots - 1)
                    dve.tensor_tensor(work[0:QK, 0, :], src[0:QK, :], b_tab[0:QK, SIN_B:SIN_B + S], ALU.mult).then_inc(acc_drained, 1)
                    dve.wait_ge(acc_drained, drained(T + n))
                    dve.tensor_tensor(b_q[0:QK, i, :], b_q[0:QK, i, :], work[0:QK, 0, :], ALU.add).then_inc(rotated, 1)
                elif kind == "kn":
                    if i == 3:
                        dve.wait_ge(blocks_done, block_done(B + len(LINS2) + 3))
                    else:
                        dve.wait_ge(up_done, 11 * L + 5 + i + 1)
                    ch.link(dve.tensor_copy(b_k[0:HD, 2 * i, :], src[0:HD, :]))
                    dve.tensor_copy(b_k[0:HD, 2 * i + 1, :], src[HD:P, :]).then_inc(acc_drained, 1)
                elif kind == "vb":
                    if i == 3:
                        dve.wait_ge(blocks_done, block_done(B + len(LINS2) + 4))
                    else:
                        dve.wait_ge(up_done, 11 * L + 8 + i + 1)
                    dve.tensor_copy(b_vb[:, i, :], src[:]).then_inc(acc_drained, 1)
            k = c.copy()
            attend_dve(dve, ch, k, grouped_units() + latent_units())
            T += len(ORDER2)
            G, g = KD * L, B + len(LINS2) + 5
            for m in range(KD):
                for q in range(2):
                    dve.wait_ge(blocks_done, block_done(g + 3 * m + q))
                    dve.tensor_tensor(work[:, q, :], bank[(T + 4 * m + q) % ACCS][:], factor, ALU.mult).then_inc(acc_drained, 1)
                dve.wait_ge(gate_ready, 2 * (G + m) + 2)
                dve.wait_ge(blocks_done, block_done(g + 3 * m + 2))
                if G + m:
                    dve.wait_ge(merged_split, G + m)
                dve.tensor_tensor(work[:, 2, :], work[:, 0, :], bank[(T + 4 * m + 2) % ACCS][:], ALU.mult).then_inc(acc_drained, 1)
                dve.tensor_tensor(work[:, 3, :], work[:, 1, :], bank[(T + 4 * m + 3) % ACCS][:], ALU.mult).then_inc(acc_drained, 1)
                dve.wait_ge(acc_drained, drained(T + 4 * m + 3))
                dve.tensor_tensor(work[:, 2, :], work[:, 2, :], work[:, 3, :], ALU.add).then_inc(merged, 1)
                dve.wait_ge(merged_rounded, G + m + 1)
                dve.tensor_tensor(mm_lo[:, m, :], work[:, 2, :], mm_hi[:, m, :].bitcast(F32), ALU.subtract)\
                   .then_inc(merged_split, 1)
            k.tiles = T + 4 * KD
            out_dve(dve, ch, k, 1, g + 3 * KD, y)

        def ffn2_end(c):
            c.blocks += 2 * (NH + 2 * KD)
            c.tiles += 2 * (NH + KD)
            c.hidden += 2 * NH
            c.sums += KD - 1
            c.add("ysq", KD)

        def ffn2_sp(sp, c, i):
            g = c.blocks
            for part in range(2):
                stream_sp(sp, g, t["b_ffn_up"][i, part], NH)
                stream_sp(sp, g + NH, t["b_ffn_down"][i, part], 2 * KD)
                g += NH + 2 * KD

        def ffn2_pool(pool, c):
            stream_pool(pool, c.blocks + RING, 2 * (NH + 2 * KD) - RING)

        def ffn2_pe(pe, c):
            B, T = c.blocks, c.tiles
            for part in range(2):
                with pe.Fori(1 - part, NH // 4) as it:
                    for j in range(4):
                        pe.wait_ge(acc_drained, it * 4 + acc_free(T + j))
                        pe.wait_ge(w_rest, it * 4 + rest_done(B + j))
                        products(pe, bank[(T + j) % ACCS][:], (B + j) % RING, *xs_of(xh, xl, KD), True, True)
                B += NH
                T += NH
                with pe.Fori(0, 2) as it:
                    for m in range(4):
                        pe.wait_ge(acc_drained, it * 4 + acc_free(T + m))
                        for b in range(2):
                            pe.wait_ge(w_rest, it * 8 + rest_done(B + 2 * m + b))
                            pe.wait_ge(hl_done, 2 + c.hidden + NH * part + 8 * (b + 1))
                            products(pe, bank[(T + m) % ACCS][:], (B + 2 * m + b) % RING,
                                     *xs_of(hh2, hl2, 8, 8 * b), b == 0, b == 1)
                B += 2 * KD
                T += KD

        def ffn2_act(act, c):
            B, T, H = c.blocks, c.tiles, c.hidden

            def four(it, j):
                g = B + j + AHEAD
                round_block(act, it * 4 + g, g % RING, it + g // RING, 1024)
                square_relu(it, j)

            def square_relu(it, j):
                act.wait_ge(acc_drained, it * 4 + drained(T + j))
                act.wait_ge(hl_done, it * 4 + (H + j + 1))
                act.activation(h[:, j % 2, :], sig[:, j % 2, :], ACT.Square)
                act.activation(hh2[:, it * 4 + j, :], sig[:, j % 2, :], ACT.Square).then_inc(hh_done, 1)

            for part in range(2):
                if part == 0:
                    square_relu(0, 0)
                    for j in range(1, 4):
                        four(0, j)
                with act.Fori(1 - part, NH // 4) as it:
                    for j in range(4):
                        four(it, j)
                B += NH
                T += NH
                H += NH
                k = c.copy()
                k.tiles = T
                for m in range(KD):
                    for b in range(2):
                        round_ahead(act, B + 2 * m + b)
                    if part:
                        if m == KD - 1:
                            load_sqrt(act)
                        act.wait_ge(acc_drained, drained(T + m))
                        act.wait_ge(sum_used, c.sums + m + 1)
                        act.activation(sq[:, m % 2, :], y_b[:, m, :], ACT.Square).then_inc(y_squared, 1)
                B += 2 * KD
                T += KD

        def ffn2_dve(dve, ch, c):
            B, T, H = c.blocks, c.tiles, c.hidden
            for part in range(2):
                with dve.Fori(0, NH // 4) as it:
                    for j in range(4):
                        dve.wait_ge(blocks_done, it * 4 + block_done(B + j))
                        dve.scalar_tensor_tensor(out=sig[:, j % 2, :], in0=bank[(T + j) % ACCS][:], scalar=0.0,
                                                 in1=factor, op0=ALU.max, op1=ALU.mult).then_inc(acc_drained, 1)
                        dve.wait_ge(hh_done, it * 4 + (H + j + 1))
                        dve.tensor_tensor(hl2[:, it * 4 + j, :], h[:, j % 2, :], hh2[:, it * 4 + j, :].bitcast(F32),
                                          ALU.subtract).then_inc(hl_done, 1)
                B += NH
                T += NH
                H += NH
                if part:
                    y_begin(dve, ch)
                for m in range(KD):
                    dve.wait_ge(blocks_done, block_done(B + 2 * m + 1))
                    if part == 0:
                        dve.tensor_copy(y_b[:, m, :], bank[(T + m) % ACCS][:]).then_inc(acc_drained, 1)
                    else:
                        dve.wait_ge(acc_drained, drained(T + m - 1))
                        dve.tensor_tensor(y_b[:, m, :], y_b[:, m, :], bank[(T + m) % ACCS][:], ALU.add)\
                           .then_inc(acc_drained, 1)
                        y_sum(dve, c, m)
                B += 2 * KD
                T += KD

        PHASES = [("ffn", 0), ("even", 0), ("ffn", 1), ("ffn", 2), ("odd", 0), ("ffn", 3),
                  ("mix2", 0), ("ffn2", 0), ("mix2", 1), ("ffn2", 1)][:stop]
        for kind, _ in PHASES:
            widths.extend({"ffn": [1024] * (2 * NF) + [n * P for n in DOWN] * KD,
                           "even": [1024] * 20,
                           "odd": [1024] * ODD_LINS + [1024, 512] * KD,
                           "mix2": mix2_blocks(),
                           "ffn2": [1024] * (2 * (NH + 2 * KD))}[kind])
        ROWS = {("ffn", 0): 0, ("even", 0): 2, ("ffn", 1): 4, ("ffn", 2): 6, ("odd", 0): 8, ("ffn", 3): 10,
                ("mix2", 0): 12, ("ffn2", 0): 14, ("mix2", 1): 16, ("ffn2", 1): 18}
        END = {"ffn": ffn_end, "even": even_end, "odd": odd_end, "mix2": mix2_end, "ffn2": ffn2_end}

        @block.sync
        def _(sp):
            c = Counts()
            sp.dma_start(gains[:], t["gains"]).then_inc(gains_loaded, 16)
            for kind, i in PHASES:
                if kind == "ffn":
                    ffn_sp(sp, c, i)
                elif kind == "even":
                    even_sp(sp, c)
                elif kind == "odd":
                    odd_sp(sp, c)
                elif kind == "mix2":
                    mix2_sp(sp, c, i)
                else:
                    ffn2_sp(sp, c, i)
                END[kind](c)
                post_end(c)
            for k in range(KD):
                sp.wait_ge(x_ready, c.xr - KD + k + 1)
                sp.dma_start(t["out"][:, k, :], x[:, k, :]).then_inc(stored, 16)
            sp.wait_ge(stored, 16 * KD)

        @block.gpsimd
        def _(pool):
            c = Counts()
            pool.sem_inc(w_rest, RING)
            pool.memset(ident[:], 0.0).then_inc(pool_made, 1)
            pool.wait_ge(pool_made, 1)
            pool.affine_select(out=ident[:], in_=ident[:], compare_op=ALU.not_equal, fill=1.0, base=0,
                               pattern=[[-1, P]], channel_multiplier=1).then_inc(pool_made, 1)
            for kind, i in PHASES:
                pre_pool(pool, c)
                pre_end(c)
                if kind == "ffn":
                    ffn_pool(pool, c, i)
                elif kind == "even":
                    even_pool(pool, c)
                elif kind == "odd":
                    odd_pool(pool, c)
                elif kind == "mix2":
                    mix2_pool(pool, c)
                else:
                    ffn2_pool(pool, c)
                END[kind](c)
                post_end(c)

        @block.tensor
        def _(pe):
            c = Counts()
            pe.sem_inc(blocks_done, RING)
            pe.wait_ge(pool_made, 2)
            pe.wait_ge(dve_made, 6)
            for kind, i in PHASES:
                pre_pe(pe, c)
                pre_end(c)
                if kind == "ffn":
                    ffn_pe(pe, c, i)
                elif kind == "even":
                    even_pe(pe, c)
                elif kind == "odd":
                    odd_pe(pe, c)
                elif kind == "mix2":
                    mix2_pe(pe, c)
                else:
                    ffn2_pe(pe, c)
                END[kind](c)
                post_pe(pe, c)
                post_end(c)

        @block.scalar
        def _(act):
            c = Counts()
            for i in range(PIECES):
                piece = slice(i * KD // PIECES, (i + 1) * KD // PIECES)
                act.dma_start(x[:, piece, :], t["x"][:, piece, :]).then_inc(x_loaded[i], 16)
            for g in range(AHEAD):
                round_block(act, g, g, 0, widths[g])
            for kind, i in PHASES:
                pre_act(act, c, ROWS[kind, i])
                pre_end(c)
                if kind == "ffn":
                    ffn_act(act, c, i)
                elif kind == "even":
                    even_act(act, c)
                elif kind == "odd":
                    odd_act(act, c)
                elif kind == "mix2":
                    mix2_act(act, c, i)
                else:
                    ffn2_act(act, c)
                END[kind](c)
                post_act(act, c)
                post_end(c)

        @block.vector
        def _(dve):
            c = Counts()
            ch = Chain(dve, dve_step)
            dve.sem_inc(acc_drained, ACCS)
            dve.sem_inc(hl_done, 2)
            dve.sem_inc(sum_used, 2)
            for n, width in enumerate((D, CONV_T * P, QR * P, KR * P)):
                dve.memset(meancol[:, n:n + 1], 1.0 / width).then_inc(dve_made, 1)
            ch.link(dve.memset(meancol[:, 4:6], 0.0))
            dve.memset(meancol[0:HD, 4:5], 1.0 / HD).then_inc(dve_made, 1)
            dve.memset(meancol[HD:P, 5:6], 1.0 / HD).then_inc(dve_made, 1)
            dve.wait_ge(gains_loaded, 16)
            for r in (1, 5, 7, 11):
                ch.link(dve.tensor_scalar(gains[:, r, :], gains[:, r, :], 0.5, None, ALU.mult))
            prev = None
            for kind, i in PHASES:
                pre_dve(dve, ch, c, ROWS[kind, i], prev)
                pre_end(c)
                if kind == "ffn":
                    ffn_dve(dve, ch, c, i)
                elif kind == "even":
                    even_dve(dve, ch, c)
                elif kind == "odd":
                    odd_dve(dve, ch, c)
                elif kind == "mix2":
                    mix2_dve(dve, ch, c)
                else:
                    ffn2_dve(dve, ch, c)
                END[kind](c)
                post_dve(dve, c)
                post_end(c)
                prev = ROWS[kind, i] + 1, {"odd": o_y, "ffn2": y_b}.get(kind, y)
            grow_dve(dve, ch, c, prev[0], prev[1], lambda k: None)


def tiles_of(w):
    K, N = w.shape
    return np.ascontiguousarray(w.reshape(K // P, P, N // P, P).transpose(2, 1, 0, 3).reshape(N // P, P, K))


def columns(v):
    return v.reshape(-1, P).T


def even_table():
    f = np.float32
    inv = (f(1.0) / (f(10000.0) ** (np.arange(0, HD, 2, dtype=f) / f(HD)))).astype(f)
    ang = (inv[np.arange(P) % 32][:, None] * np.arange(S, dtype=f)[None]).astype(f)
    q, j = np.arange(P)[:, None], np.arange(P)[None]
    mask = np.concatenate([np.where(j >= q, 0, NEG), np.zeros((P, P)), np.where(j <= q, 0, NEG)], 1)
    s = np.arange(S)
    inv_count = np.stack([1.0 / (np.clip(s + w - w // 2, 0, S) - np.clip(s - w // 2, 0, S)) for w in (2, 4, 8, 16)])
    pool = np.concatenate([np.repeat(inv_count[0:2], HD, 0), np.repeat(inv_count[2:4], HD, 0)], 1)
    return np.concatenate([np.cos(ang), np.sin(ang), mask, pool, rotation(P, HD)], 1).astype(f)


def rotation(n, width, first=0):
    r = np.zeros((n, n), np.float32)
    for p in range(first, n):
        low = (p - first) % width < width // 2
        r[p + (width // 2 if low else -width // 2), p] = -1 if low else 1
    return r


def second_table():
    f = np.float32
    row, col = np.repeat(np.arange(S // 64), 64).astype(f), np.tile(np.arange(64), S // 64).astype(f)

    def angles(dim):
        half = dim // 2
        inv = (f(10000.0) ** (-np.arange(0, half, 2, dtype=f) / f(half))).astype(f)
        r, c = row[:, None] * inv, col[:, None] * inv
        return np.concatenate([r, r, c, c], 1).T.astype(f)
    a, b = np.tile(angles(HD), (2, 1)), angles(32)
    pad = np.zeros((QK - HD, S), f)
    cos_b = np.concatenate([np.ones((HD, S)), np.cos(b), pad])
    sin_b = np.concatenate([np.zeros((HD, S)), np.sin(b), pad])
    rot_b = np.zeros((P, P), f)
    rot_b[:QK, :QK] = rotation(QK, 16, HD)
    return np.concatenate([np.cos(a), np.sin(a), cos_b, sin_b, rotation(P, 32), rot_b], 1).astype(f)


def lay_out(a):
    r = {}
    r["x"] = np.ascontiguousarray(a["x"][0].T.reshape(KD, P, S).transpose(1, 0, 2))
    gate, up, down = a["ffn_w_gate"], a["ffn_w_up"], a["ffn_w_down"]
    r["ffn_up"] = np.stack([np.stack([tiles_of(gate[l, i]), tiles_of(up[l, i])], 1).reshape(2 * NF, P, D)
                            for l in range(2) for i in range(2)])
    r["ffn_down"] = np.stack([tiles_of(down[l, i]) for l in range(2) for i in range(2)])
    g = [a["norm_w"].reshape(12, D)] + [a[n][l:l + 1] for l in range(2)
                                        for n in ("pre_mix_g_2", "post_mix_g_2", "pre_ffn_g_2", "post_ffn_g_2")]
    r["gains"] = np.ascontiguousarray(np.concatenate(g).reshape(20, KD, P).transpose(2, 0, 1))

    w = a["ev_w_in"][0]
    qw, kw = Q_HEADS * HD, KV_HEADS * HD
    q0, k0, v0 = POOL_W, POOL_W + qw, POOL_W + qw + kw
    q_cols = np.concatenate([np.arange(HD) + HD * head for pair in EVEN_PAIRS for head in pair])
    r["ev_in"] = tiles_of(np.concatenate([w[:, :q0], w[:, k0:v0], w[:, q0 + q_cols], w[:, v0:]], 1))
    w = a["ev_w_out"][0]
    r["ev_out"] = tiles_of(np.concatenate([w[:POOL_W], w[POOL_W + q_cols]]))
    wg = np.zeros((P, 2, P), np.float32)
    for g in range(4):
        half = slice(g % 2 * HD, g % 2 * HD + HD)
        wg[half, g // 2, half] = a["ev_pool_w"][0, g]
    r["ev_wg"] = wg
    r["ev_small"] = np.ascontiguousarray(np.concatenate(
        [columns(a["ev_pool_scale"][0]), np.broadcast_to(a["ev_sink"][0], (P, Q_HEADS))], 1))
    r["tab_even"] = even_table()

    w = a["od_w_in"][0]
    cc = CONV_T * P
    pairs = np.concatenate([np.arange(P) + P * i + cc * j for i in range(CONV_T) for j in range(2)])
    z0, x0, d0 = 2 * cc, 2 * cc + D, 2 * cc + D + D + 2 * SG * SN
    r["od_in"] = tiles_of(np.concatenate([w[:, pairs], w[:, x0:d0], w[:, d0:], np.zeros((D, P - 2 * SH), np.float32),
                                          w[:, z0:x0]], 1))
    r["od_out"] = tiles_of(a["od_w_out"][0])
    steps = np.zeros((P, 2), np.float32)
    steps[:2 * SH, 0] = a["ssm_dt_bias"][0].reshape(-1)
    steps[:2 * SH, 1] = a["ssm_A_log"][0].reshape(-1)
    r["od_small"] = np.ascontiguousarray(np.concatenate([
        a["cv_dw_w"][0].reshape(CONV_K, CONV_T, P).transpose(2, 1, 0).reshape(P, -1), columns(a["cv_dw_b"][0]),
        columns(a["cv_ln_g"][0]), columns(a["cv_ln_b"][0]),
        a["ssm_conv_w"][0].reshape(SSM_K, 16, P).transpose(2, 1, 0).reshape(P, -1), columns(a["ssm_conv_b"][0]),
        columns(np.repeat(a["ssm_D"][0], HD)), columns(a["ssm_norm_w"][0]), steps], 1))
    s, l = np.arange(P)[:, None], np.arange(P)[None]
    back = (np.arange(P) >= SH)[:, None]
    r["tab_odd"] = np.concatenate([np.where(back, -1, 1), back, np.where(l >= s, 0, NEG), np.where(l <= s, 0, NEG)],
                                  1).astype(np.float32)

    a_cols = np.concatenate([np.arange(HD) + HD * head for j in range(4) for head in (j, j + 4)])
    ins, ups, kvs, gates, outs, smalls, fup, fdown = ([] for _ in range(8))
    for i in range(2):
        w = a["w_in_2"][i]
        kr = np.zeros((D, P), np.float32)
        kr[:, HD:QK] = w[:, 1408:1440]
        ins.append(tiles_of(np.concatenate([w[:, a_cols], w[:, 512:640], w[:, 768:1408], kr, w[:, 640:768]], 1)))
        ups.append(a["w_q_up_2"][i].reshape(QR, P, 8, QK).transpose(1, 2, 0, 3).reshape(P, -1))
        kv = a["w_kv_up_2"][i].reshape(KR * P, 8, 2, HD)
        kvs.append(np.stack([tiles_of(np.ascontiguousarray(kv[:, :, j]).reshape(KR * P, 8 * HD))
                             .transpose(1, 0, 2).reshape(P, -1) for j in range(2)]))
        ga, gb = tiles_of(w[:, 1440:1440 + D]), tiles_of(w[:, 1440 + D:])
        br = np.concatenate([tiles_of(a["w_branch_a_2"][i][a_cols]), tiles_of(a["w_branch_b_2"][i])], 2)
        gates.append(np.stack([ga, gb, br], 1).reshape(3 * KD, P, D))
        outs.append(tiles_of(a["w_o_2"][i]))
        smalls.append(np.concatenate([np.tile(a["q_norm_g_2"][i], 2)[:, None], np.tile(a["k_norm_g_2"][i], 2)[:, None],
                                      columns(a["q_a_norm_g_2"][i]), columns(a["kv_a_norm_g_2"][i]),
                                      np.zeros((P, 1), np.float32), columns(a["b_gate_2"][i])], 1))
        fup.append(tiles_of(a["w_ffn_up_2"][i]).reshape(2, NH, P, D))
        fdown.append(np.stack([tiles_of(part).reshape(KD, P, 2, D).transpose(0, 2, 1, 3).reshape(2 * KD, P, D)
                               for part in np.split(a["w_ffn_down_2"][i], 2)]))
    for name, parts in (("b_in", ins), ("b_up", ups), ("b_kv", kvs), ("b_gates", gates), ("b_out", outs),
                        ("b_small", smalls), ("b_ffn_up", fup), ("b_ffn_down", fdown)):
        r[name] = np.ascontiguousarray(np.stack(parts))
    r["tab_b"] = second_table()
    return {n: np.ascontiguousarray(v) for n, v in r.items()}


def kernel(**inputs):
    import concourse.bacc as bacc
    from concourse.bass_utils import run_bass_kernel_spmd

    nc = bacc.Bacc("TRN2", target_bir_lowering=False, num_devices=1)
    arrays = lay_out({k: np.asarray(v) for k, v in inputs.items()})
    t = {n: nc.dram_tensor(f"in_{n}", a.shape, F32, kind="ExternalInput").ap() for n, a in arrays.items()}
    t["out"] = nc.dram_tensor("out_x", (P, KD, S), F32, kind="ExternalOutput").ap()
    build(nc, t)
    got = run_bass_kernel_spmd(nc, [{f"in_{n}": a for n, a in arrays.items()}], core_ids=[0])
    return np.ascontiguousarray(got.results[0]["out_x"].transpose(1, 0, 2).reshape(D, S).T)[None]
```
